# Optimizing a Trainium2 kernel written in Bass

```python
import math
import jax, jax.numpy as jnp
from jax import lax
import numpy as np

D_MODEL = 1024
BATCH = 1
SEQ = 1024
DEPTH = 1

D_MIX = D_MODEL
A_HEADS = 8
A_HEAD_DIM = 64
D_A = A_HEADS * A_HEAD_DIM
B_GROUPS = 8
B_GROUP_DIM = 64
D_B = B_GROUPS * B_GROUP_DIM
D_IN = 2 * D_A + D_B
CHUNK = 128

N_EXPERTS = 64
TOP_K = 8
N_EXPERT_GROUPS = 8
TOPK_GROUPS = 4
D_EXPERT = 256
D_SHARED = 256
ROUTED_SCALE = 2.5
EXPERT_BLOCK = 128
EPS = 1e-6

kernel_name = "hybrid_sgu_fnet_moe_encoder"

def rms_norm(x, g):
    xf = x.astype(jnp.float32)
    y = xf * lax.rsqrt(jnp.mean(xf * xf, axis=-1, keepdims=True) + EPS)
    return (y * g.astype(jnp.float32)).astype(x.dtype)

def layer_norm(x, g, b):
    xf = x.astype(jnp.float32)
    mu = jnp.mean(xf, axis=-1, keepdims=True)
    xc = xf - mu
    y = xc * lax.rsqrt(jnp.mean(xc * xc, axis=-1, keepdims=True) + EPS)
    return (y * g.astype(jnp.float32) + b.astype(jnp.float32)).astype(x.dtype)

def spatial_gating(z, ln_g, ln_b, w_s, b_s):
    u, v = jnp.split(z, 2, axis=-1)
    v = layer_norm(v, ln_g, ln_b)
    bsz, s, _ = v.shape
    v = v.reshape(bsz, s // CHUNK, CHUNK, A_HEADS, A_HEAD_DIM)
    mixed = jnp.einsum('hpq,bcqhd->bcphd', w_s, v) + b_s.T[None, None, :, :, None]
    return u * mixed.reshape(bsz, s, D_A)

def fourier_mix(z):
    bsz, s, _ = z.shape
    zf = z.astype(jnp.float32).reshape(bsz, s, B_GROUPS, B_GROUP_DIM)
    f = jnp.fft.fft2(zf, axes=(1, 3), norm='ortho')
    return jnp.real(f).reshape(bsz, s, D_B).astype(z.dtype)

def route(xf, w_router, router_bias):
    t = xf.shape[0]
    scores = jax.nn.sigmoid(xf.astype(jnp.float32) @ w_router.astype(jnp.float32))
    biased = scores + router_bias.astype(jnp.float32)
    grp = biased.reshape(t, N_EXPERT_GROUPS, N_EXPERTS // N_EXPERT_GROUPS)
    group_score = jnp.sum(lax.top_k(grp, 2)[0], axis=-1)
    _, gidx = lax.top_k(group_score, TOPK_GROUPS)
    gmask = jnp.sum(jax.nn.one_hot(gidx, N_EXPERT_GROUPS, dtype=jnp.float32), axis=1) > 0
    emask = jnp.repeat(gmask, N_EXPERTS // N_EXPERT_GROUPS, axis=1)
    masked = jnp.where(emask, biased, -jnp.inf)
    _, eidx = lax.top_k(masked, TOP_K)
    w = jnp.take_along_axis(scores, eidx, axis=1)
    w = w / jnp.sum(w, axis=-1, keepdims=True) * ROUTED_SCALE
    return eidx, w

def routed_experts(xf, eidx, gates, w_gate, w_up, w_down):
    t, d = xf.shape
    n_assign = t * TOP_K
    e_flat = eidx.reshape(n_assign)
    tok_flat = jnp.repeat(jnp.arange(t, dtype=jnp.int32), TOP_K)
    g_flat = gates.reshape(n_assign).astype(xf.dtype)
    order = jnp.argsort(e_flat)
    e_s = e_flat[order]
    tok_s = tok_flat[order]
    g_s = g_flat[order]
    counts = jnp.bincount(e_flat, length=N_EXPERTS)
    starts = jnp.cumsum(counts) - counts
    padded = (counts + EXPERT_BLOCK - 1) // EXPERT_BLOCK * EXPERT_BLOCK
    pad_ends = jnp.cumsum(padded)
    pad_starts = pad_ends - padded
    dest = pad_starts[e_s] + (jnp.arange(n_assign, dtype=jnp.int32) - starts[e_s])
    total = n_assign + N_EXPERTS * EXPERT_BLOCK
    n_blocks = total // EXPERT_BLOCK
    buf_tok = jnp.full((total,), t, jnp.int32).at[dest].set(tok_s)
    buf_gate = jnp.zeros((total,), xf.dtype).at[dest].set(g_s)
    block_e = jnp.minimum(
        jnp.searchsorted(pad_ends, jnp.arange(n_blocks, dtype=jnp.int32) * EXPERT_BLOCK, side='right'),
        N_EXPERTS - 1)
    x_pad = jnp.concatenate([xf, jnp.zeros((1, d), xf.dtype)], axis=0)

    def step(y, blk):
        tok, gate, e = blk
        xb = x_pad[tok]
        h = jax.nn.silu(xb @ w_gate[e]) * (xb @ w_up[e])
        out = (h @ w_down[e]) * gate[:, None]
        return y.at[tok].add(out), None

    y0 = jnp.zeros((t + 1, d), xf.dtype)
    y, _ = lax.scan(step, y0, (buf_tok.reshape(n_blocks, EXPERT_BLOCK),
                               buf_gate.reshape(n_blocks, EXPERT_BLOCK), block_e))
    return y[:t]

def setup_inputs(seed: int = 0) -> dict:
    key = jax.random.key(seed)
    ks = jax.random.split(key, 22)
    f32 = jnp.float32
    L = DEPTH

    def nrm(k, shape, scale):
        return jax.random.normal(k, shape, f32) * scale

    return {
        "x": jax.random.normal(ks[0], (BATCH, SEQ, D_MODEL), f32),
        "norm1_g": 1.0 + nrm(ks[1], (L, D_MODEL), 0.01),
        "w_in": nrm(ks[2], (L, D_MODEL, D_IN), D_MODEL ** -0.5),
        "sgu_ln_g": 1.0 + nrm(ks[3], (L, D_A), 0.01),
        "sgu_ln_b": nrm(ks[4], (L, D_A), 0.02),
        "w_spatial": nrm(ks[5], (L, A_HEADS, CHUNK, CHUNK), CHUNK ** -0.5),
        "b_spatial": 1.0 + nrm(ks[6], (L, A_HEADS, CHUNK), 0.01),
        "out_norm_a_g": 1.0 + nrm(ks[7], (L, D_A), 0.01),
        "out_norm_b_g": 1.0 + nrm(ks[8], (L, D_B), 0.01),
        "w_out": nrm(ks[9], (L, D_MIX, D_MODEL), D_MIX ** -0.5),
        "norm2_g": 1.0 + nrm(ks[10], (L, D_MODEL), 0.01),
        "w_router": nrm(ks[11], (L, D_MODEL, N_EXPERTS), D_MODEL ** -0.5),
        "router_bias": nrm(ks[12], (L, N_EXPERTS), 0.01),
        "w_gate": nrm(ks[13], (L, N_EXPERTS, D_MODEL, D_EXPERT), D_MODEL ** -0.5),
        "w_up": nrm(ks[14], (L, N_EXPERTS, D_MODEL, D_EXPERT), D_MODEL ** -0.5),
        "w_down": nrm(ks[15], (L, N_EXPERTS, D_EXPERT, D_MODEL), D_EXPERT ** -0.5),
        "ws_gate": nrm(ks[16], (L, D_MODEL, D_SHARED), D_MODEL ** -0.5),
        "ws_up": nrm(ks[17], (L, D_MODEL, D_SHARED), D_MODEL ** -0.5),
        "ws_down": nrm(ks[18], (L, D_SHARED, D_MODEL), D_SHARED ** -0.5),
        "final_norm_g": 1.0 + nrm(ks[19], (D_MODEL,), 0.01),
    }

def reference(x, norm1_g, w_in, sgu_ln_g, sgu_ln_b, w_spatial, b_spatial,
              out_norm_a_g, out_norm_b_g, w_out, norm2_g, w_router, router_bias,
              w_gate, w_up, w_down, ws_gate, ws_up, ws_down, final_norm_g):
    bsz, s, d = x.shape
    h = x
    for l in range(DEPTH):
        xn = rms_norm(h, norm1_g[l])
        z = jnp.einsum('bsd,de->bse', xn, w_in[l])
        z_a = jax.nn.gelu(z[..., :2 * D_A], approximate=False)
        z_b = z[..., 2 * D_A:]
        y_a = spatial_gating(z_a, sgu_ln_g[l], sgu_ln_b[l], w_spatial[l], b_spatial[l])
        y_b = fourier_mix(z_b)
        mix = jnp.concatenate([rms_norm(y_a, out_norm_a_g[l]),
                               rms_norm(y_b, out_norm_b_g[l])], axis=-1)
        h = h + jnp.einsum('bse,ed->bsd', mix, w_out[l])
        hn = rms_norm(h, norm2_g[l]).reshape(bsz * s, d)
        eidx, gates = route(hn, w_router[l], router_bias[l])
        routed = routed_experts(hn, eidx, gates, w_gate[l], w_up[l], w_down[l])
        shared = (jax.nn.silu(hn @ ws_gate[l]) * (hn @ ws_up[l])) @ ws_down[l]
        h = h + (routed + shared).reshape(bsz, s, d)
    return rms_norm(h, final_norm_g)


_drawn_inputs = setup_inputs


def setup_inputs(seed=0):
    import zlib

    import numpy as np

    out = dict(_drawn_inputs(seed))
    spreads = {}
    factors = {}
    for name, (base, spread) in spreads.items():
        noise = np.random.default_rng([zlib.crc32(name.encode()), seed]).standard_normal(out[name].shape)
        drawn = base * np.exp(spread * noise) if base else spread * noise
        out[name] = __import__('jax').numpy.asarray(drawn.astype(out[name].dtype))
    for name, factor in factors.items():
        out[name] = (out[name] * factor).astype(out[name].dtype)
    return out
```

```python
from contextlib import ExitStack

import concourse.bass as bass
from concourse import mybir

P = 128
D = 1024
S = 1024
NC = S // P
KD = D // P
DA = 512
NH = 8
HD = DA // NH
NE = 64
TOPK = 8
NG = 8
GE = NE // NG
TOPG = 4
F = 256
KF = F // P
RSCALE = 2.5
EPS = 1e-6
MAXCH = S // P
NITEM = (S * TOPK) // P + NE
TAB = NITEM + 4
EMPTY = 4096.0
BIG = 3.0e38
RING = 3

ALU = mybir.AluOpType
ACT = mybir.ActivationFunctionType
AX = mybir.AxisListType
F32 = mybir.dt.float32
BF16 = mybir.dt.bfloat16
I32 = mybir.dt.int32
U32 = mybir.dt.uint32
R8 = 0.5 ** 0.5


def build(nc, x, g1, w_in, ln_g, ln_b, wsT, bsT, ga, gb, w_out, g2, w_router, rbias, wg, wu, wd,
          sg, su, sd, dft_pos, dft_ch, gf, out, hn_d, y_d):
    ctx = ExitStack()
    with ctx:
        top = [nc.sbuf_base]

        def place(name, shape, dt, at=None):
            size = 2 if dt == BF16 else 4
            n = size
            for s in shape[1:]:
                n *= s
            n = (n + 31) // 32 * 32
            if at is None:
                at = top[0]
                top[0] += n
            return nc.alloc_sbuf_tensor_at(name, shape, dt, offset=at)

        base0 = top[0] = (top[0] + 63) // 64 * 64
        KB = 1024
        X_AT = base0
        T_AT = X_AT + 32 * KB
        W_AT = T_AT + 32 * KB
        U_AT = W_AT + 48 * KB
        V_AT = U_AT + 16 * KB
        Z_AT = V_AT + 16 * KB
        S_AT = Z_AT + 16 * KB
        D_AT = S_AT + 8 * KB
        R_AT = D_AT + 8 * KB
        top[0] = R_AT + 12 * KB

        xh = place("xh", [P, NC, D], F32, X_AT)
        T = place("T", [P, KD, S], F32, T_AT)
        ab = place("ab", [P, 2, 4, 512], F32, T_AT + 16 * KB)
        w_in_sb = place("w_in_sb", [P, KD, 3 * DA], F32, W_AT)
        w_out_sb = place("w_out_sb", [P, KD, D], F32, W_AT)
        U = place("U", [P, 8, 4, P], F32, W_AT + 32 * KB)
        sgu_w = place("sgu_w", [P, 2, KD, F], F32, W_AT + 32 * KB)
        u_sb = place("u_sb", [P, NC, DA], F32, U_AT)
        v_sb = place("v_sb", [P, NC, DA], F32, V_AT)
        yb = place("yb", [P, NC, DA], F32, V_AT)
        zT = place("zT", [P, 4, S], F32, Z_AT)
        rows = place("rows", [P, 2, D], F32, S_AT)
        V = place("V", [P, 2, 4, 2, P], F32, S_AT)
        hsT = place("hsT", [P, KF, S], F32, S_AT)
        dpos = place("dpos", [P, 2, 8, P], F32, D_AT)
        sd_w = place("sd_w", [P, KF, D], F32, D_AT)
        g1_row = place("g1_row", [P, D], F32, R_AT)
        lng_row = place("lng_row", [P, DA], F32, R_AT + 4 * KB)
        lnb_row = place("lnb_row", [P, DA], F32, R_AT + 6 * KB)
        ga_row = place("ga_row", [P, DA], F32, R_AT + 8 * KB)
        gb_row = place("gb_row", [P, DA], F32, R_AT + 10 * KB)
        pos = place("pos", [P, NC, NE], F32, R_AT)
        info = place("info", [P, NC, NE, 5], BF16, R_AT + 2 * KB)
        slots = place("slots", [P, 1024 + P], F32, R_AT + 7 * KB)
        wgu = place("wgu", [P, RING, 2, KD, F], F32, U_AT)
        wdn = place("wdn", [P, RING, KF, D], F32, W_AT)
        s_tmp = place("s_tmp", [P, 2, 512], F32, W_AT + 24 * KB)
        rt_a = place("rt_a", [P, NC, NE], F32, W_AT + 28 * KB)
        rt_b = place("rt_b", [P, NC, NE], F32, W_AT + 30 * KB)
        Xg = place("Xg", [P, 2, D], F32, T_AT)
        xT = place("xT", [P, KD, P], F32, T_AT + 8 * KB)
        ob = place("ob", [P, 2, D], F32, T_AT + 12 * KB)
        onehot = place("onehot", [P, 2, NC, P], BF16, T_AT + 20 * KB)
        hs = place("hs", [P, 2, F], F32, T_AT + 24 * KB)
        hh = place("hh", [P, 2, F], F32, T_AT + 26 * KB)
        hT = place("hT", [P, KF, P], F32, T_AT + 28 * KB)
        g2_row = place("g2_row", [P, D], F32)
        idx_all = place("idx_all", [P, TAB], I32, top[0] - 4 * KB)
        gate_all = place("gate_all", [P, TAB], F32, top[0] - 3 * KB)
        le = place("le", [P, 3, NE], F32, top[0] - 2 * KB)
        dch = place("dch", [P, 3, 2, P], F32)
        C_AT = top[0] - 3 * KB
        scores = place("scores", [P, NC, NE], F32, C_AT)
        mask = place("mask", [P, NC, NE], BF16, C_AT + 2 * KB)
        wsp = place("wsp", [P, NH, P], F32)
        M_AT = top[0] - 4 * KB
        m8 = place("m8", [P, NC, NG, 8], F32, M_AT)
        geq = place("geq", [P, NC, NG, TOPG], F32, M_AT + 2 * KB)
        gs = place("gs", [P, NC, NG], F32, M_AT + 3 * KB)
        gtop = place("gtop", [P, NC, 8], F32, M_AT + 3 * KB + 256)
        gidx = place("gidx", [P, NC, 8], U32, M_AT + 3 * KB + 512)
        etop = place("etop", [P, NC, 8], F32, M_AT + 3 * KB + 768)
        junk = place("junk", [P, D], BF16)
        bsp = place("bsp", [P, NH], F32)
        ident = place("ident", [P, P], F32)
        wr_sb = place("wr_sb", [P, KD, NE], F32)
        rb_row = place("rb_row", [P, NE], F32)
        tri = place("tri", [P, P], BF16)
        triI = place("triI", [NE, NE], BF16)
        ones = place("ones", [P, P], BF16)
        ms = place("ms", [P, 5, NC], F32)
        rs = place("rs", [P, 5, NC], F32)
        bst = place("bst", [P, NC, 6], F32)
        bag = place("bag", [P, NC, 2], F32)
        vr = place("vr", [P, NC], F32)
        gidxf = place("gidxf", [P, NC, TOPG], F32)
        gi = place("gi", [P, NG], F32)
        gm = place("gm", [P, NC, NG], F32)
        gsum = place("gsum", [P, NC], F32)
        grec = place("grec", [P, NC], F32)
        pidx = place("pidx", [P, 1], F32)
        dump = place("dump", [P, 1], F32)
        nch = place("nch", [NE, 1 + MAXCH], F32)
        nchb = place("nchb", [NE, P], BF16)
        cols = place("cols", [P, 8], F32)
        tab = place("tab", [4, TAB], I32)
        ends = place("ends", [1, NE + 4], I32)
        mhalf = place("mhalf", [P, 1], F32)
        thirds = place("thirds", [P, 1], I32)
        sumf = place("sumf", [P, 8], F32)
        idxf = place("idxf", [P, 1], F32)
        idxg = place("idxg", [P, 2], I32)
        idxs = place("idxs", [P, 2], I32)
        assert top[0] <= nc.sbuf_usable_end, (top[0], nc.sbuf_usable_end)
        gf_row = place("gf_row", [P, D], F32, W_AT + 24 * KB)

        ps = [ctx.enter_context(nc.psum_tensor(f"ps{i}", [P, 512], F32)) for i in range(8)]

        def sem(name):
            return ctx.enter_context(nc.semaphore(name))

        s_x = [sem(f"x_in{c}") for c in range(NC)]
        s_g1, s_wi, s_small, s_dft = sem("g1_in"), sem("w_in_in"), sem("small_in"), sem("dft_in")
        s_wo_in, s_sh_in, s_sd_in, s_gf = sem("w_out_in"), sem("shared_in"), sem("shared_down_in"), sem("gf_in")
        s_lr, s_eps = sem("v_rstd"), sem("eps_added")
        s_cst, s_mk, s_info = sem("consts_ready"), sem("const_made"), sem("token_info")
        s_sq, s_r1, s_xs, s_t1, s_t1a, s_t1d = (sem(n) for n in (
            "sq1", "rstd1", "xn_rows", "xn_tr", "xn_evac_act", "xn_evac_dve"))
        s_za, s_ge, s_ln, s_vp, s_zb, s_ze = (sem(n) for n in (
            "za_done", "gelu_done", "ln_step", "v_ready", "zb_done", "zT_ready"))
        s_sg, s_ya, s_sqa, s_ra, s_yn, s_ta, s_tae = (sem(n) for n in (
            "sgu_done", "ya_ready", "sqa", "rstda", "ya_normed", "ya_tr", "ya_evac"))
        s_bf, s_v, s_va, s_vd, s_y, s_sqb, s_rb, s_yb, s_tb, s_tbe = (sem(n) for n in (
            "butterfly", "V_done", "V_evac_act", "V_evac_dve", "Y_done", "sqb", "rstdb", "yb_ready", "yb_tr",
            "yb_evac"))
        s_wo, s_hx, s_sq2, s_r2, s_hn, s_t3, s_t3a, s_t3d, s_rt, s_sc = (sem(n) for n in (
            "w_out_done", "h_ready", "sq2", "rstd2", "hn_rows", "hn_tr", "hn_evac_act", "hn_evac_dve", "router_done",
            "scores_ready"))
        s_hst = [sem(f"hn_stored{i}") for i in range(2)]
        s_q, s_ssi, s_hm, s_sdn, s_y0, s_yst = (sem(n) for n in (
            "shared_gu", "shared_silu", "shared_h", "shared_down", "y0_ready", "y0_stored"))
        s_mask, s_chunks, s_cols = sem("mask_ready"), sem("chunks_ready"), sem("item_cols_ready")
        s_rv, s_pm, s_tab = sem("routing_step"), sem("routing_matmul"), sem("tables_ready")
        s_cp = sem("sums_copied")
        s_oh, s_ix, s_it, s_id, s_ia, s_gt = (sem(n) for n in (
            "onehot_ready", "slots_summed", "idx_tmp", "gather_idx", "idx_kept", "gate_kept"))
        s_ga = [sem(f"rows_gathered{u}") for u in range(2)]
        s_tr, s_xa, s_xd, s_gu, s_si, s_h, s_ht, s_he = (sem(n) for n in (
            "x_tr", "xT_act", "xT_dve", "gate_up", "silu", "h_rows", "h_tr", "hT_ready"))
        s_dn, s_oa, s_od, s_is, s_add, s_turn = (sem(n) for n in (
            "down_done", "out_act", "out_dve", "scatter_idx", "rows_added", "pool_turn"))
        s_wl = [sem(f"weights_in{i}") for i in range(RING)]
        s_w, s_turn_sp = sem("weights_landed"), sem("sp_turn")
        s_yl = [sem(f"y_in{c}") for c in range(NC)]
        s_sqf, s_rf, s_of, s_ost = sem("sqf"), sem("rstdf"), sem("out_rows"), sem("out_stored")

        x_v = x.rearrange("(c p) d -> c p d", p=P)
        out_v = out.rearrange("(c p) d -> c p d", p=P)
        hn_v = hn_d.rearrange("(c p) d -> c p d", p=P)
        yv = y_d.rearrange("(c p) d -> c p d", p=P)
        spread = lambda ap, n: ap.rearrange("(a n) -> a n", a=1).to_broadcast([P, n])

        def expert_load(eng, e, slot):
            eng.dma_start(wgu[:, slot, 0, :, :], wg[e].rearrange("(p k) f -> p k f", k=KD)).then_inc(s_wl[slot], 16)
            eng.dma_start(wgu[:, slot, 1, :, :], wu[e].rearrange("(p k) f -> p k f", k=KD)).then_inc(s_wl[slot], 16)
            eng.dma_start(wdn[:, slot, :, :], wd[e].rearrange("(k p) d -> p k d", p=P)).then_inc(s_wl[slot], 16)

        def item_count(eng, less=0):
            return eng.value_load(ends[0:1, NE + less:NE + less + 1], min_val=NE - less, max_val=NITEM - less)

        def look(eng, row, i, top_val):
            return eng.value_load(tab[row:row + 1, bass.ds(i, 1)], min_val=0, max_val=top_val)

        block = ctx.enter_context(nc.Block())

        @block.sync
        def _(sp):
            sp.dma_start(xh[:, 0, :], x_v[0]).then_inc(s_x[0], 16)
            sp.dma_start(g1_row[:, :], spread(g1, D)).then_inc(s_g1, 16)
            sp.dma_start(xh[:, 1, :], x_v[1]).then_inc(s_x[1], 16)
            for k in range(KD):
                sp.dma_start(w_in_sb[:, k, :], w_in.rearrange("(p k) e -> k p e", k=KD)[k]).then_inc(s_wi, 16)
            for c in range(2, NC):
                sp.dma_start(xh[:, c, :], x_v[c]).then_inc(s_x[c], 16)
            for dst, src in ((lng_row[:, :], spread(ln_g, DA)), (lnb_row[:, :], spread(ln_b, DA)),
                             (ga_row[:, :], spread(ga, DA)), (gb_row[:, :], spread(gb, DA)),
                             (g2_row[:, :], spread(g2, D)), (rb_row[:, :], spread(rbias, NE)),
                             (wsp[:, :, :], wsT.rearrange("h q p -> q h p")), (bsp[:, :], bsT),
                             (wr_sb[:, :, :], w_router.rearrange("(p k) e -> p k e", k=KD))):
                sp.dma_start(dst, src).then_inc(s_small, 16)
            sp.dma_start(dpos[:, :, :, :], dft_pos).then_inc(s_dft, 16)
            sp.dma_start(dch[:, :, :, :], dft_ch).then_inc(s_dft, 16)
            sp.wait_ge(s_zb, 8)
            sp.dma_start(w_out_sb[:, :, :], w_out.rearrange("(k p) d -> p k d", p=P)).then_inc(s_wo_in, 16)
            sp.wait_ge(s_v, 8)
            sp.dma_start(sgu_w[:, 0, :, :], sg.rearrange("(p k) f -> p k f", k=KD)).then_inc(s_sh_in, 16)
            sp.dma_start(sgu_w[:, 1, :, :], su.rearrange("(p k) f -> p k f", k=KD)).then_inc(s_sh_in, 16)
            sp.wait_ge(s_y, 8)
            sp.dma_start(sd_w[:, :, :], sd.rearrange("(k p) d -> p k d", p=P)).then_inc(s_sd_in, 16)
            sp.wait_ge(s_ta, 8)
            sp.wait_ge(s_tb, 8)
            for e in range(RING):
                for j, w in enumerate((wg, wu)):
                    sp.dma_start(wgu[:, e, j, :, :], w[e].rearrange("(p k) f -> p k f", k=KD)).then_inc(s_wl[e], 16)
            for c in range(NC):
                sp.wait_ge(s_hn, c + 1)
                sp.dma_start(hn_v[c], rows[:, c % 2, :]).then_inc(s_hst[c % 2], 16)
            sp.wait_ge(s_wo, NC)
            for e in range(RING):
                sp.dma_start(wdn[:, e, :, :], wd[e].rearrange("(k p) d -> p k d", p=P)).then_inc(s_wl[e], 16)
            for c in range(NC):
                sp.wait_ge(s_y0, c + 1)
                sp.dma_start(yv[c], xh[:, c, :]).then_inc(s_yst, 16)
            sp.dma_start(yv[NC], xh[:, 0, :]).then_inc(s_yst, 16)
            sp.wait_ge(s_tab, 1)
            for e in range(RING - 1):
                sp.wait_ge(s_wl[e], 48)
                sp.sem_inc(s_w, 1)

            def next_expert(e, slot):
                end = sp.value_load(ends[0:1, bass.ds(e - RING, 1)], min_val=1, max_val=NITEM)
                sp.wait_ge(s_dn, end)
                sp.sem_inc(s_turn_sp, 1)
                expert_load(sp, e, slot)

            def landed(slot, count):
                sp.wait_ge(s_wl[slot], count)
                sp.sem_inc(s_w, 1)

            LAST = NE - 1
            assert LAST % RING == 0
            with sp.Fori(1, LAST // RING) as t:
                for slot in range(RING):
                    next_expert(t * RING + slot, slot)
                    landed((slot - 1) % RING, t * 48 + (48 if slot else 0))
            next_expert(LAST, 0)
            landed(RING - 1, 48 * (LAST // RING))
            landed(0, 48 * (LAST // RING + 1))
            sp.dma_start(gf_row[:, :], spread(gf, D)).then_inc(s_gf, 16)
            n = item_count(sp)
            sp.wait_ge(s_add, n * 16)
            sp.sem_inc(s_turn_sp, 1)
            for c in range(NC):
                sp.dma_start(xh[:, c, :], yv[c]).then_inc(s_yl[c], 16)
            for c in range(NC):
                sp.wait_ge(s_of, c + 1)
                sp.dma_start(out_v[c], xh[:, c, :]).then_inc(s_ost, 16)
            sp.wait_ge(s_ost, 16 * NC)

        @block.tensor
        def _(pe):
            def turn_rows(src, banks, count=KD):
                for k in range(count):
                    last = pe.transpose(ps[banks[k // 4]][:, (k % 4) * P:(k % 4 + 1) * P], src[:, k:D:KD], ident[:, :])
                return last

            def turn_x(c):
                pe.wait_ge(s_xs, c + 1)
                if c >= 2:
                    pe.wait_ge(s_t1a, c - 1)
                    pe.wait_ge(s_t1d, c - 1)
                turn_rows(rows[:, c % 2, :], (0, 1) if c % 2 == 0 else (6, 7)).then_inc(s_t1, 1)

            def z_a(c):
                pe.wait_ge(s_t1a, c + 1)
                pe.wait_ge(s_t1d, c + 1)
                if c == 0:
                    pe.wait_ge(s_wi, 16 * KD)
                for half in range(2):
                    if c >= 2:
                        pe.wait_ge(s_ge, 2 * (c - 2) + half + 1)
                    for k in range(KD):
                        mm = pe.matmul(ps[2 + 2 * (c % 2) + half][:, :], T[:, k, c * P:(c + 1) * P],
                                       w_in_sb[:, k, half * DA:(half + 1) * DA], start=(k == 0), stop=(k == KD - 1))
                    mm.then_inc(s_za, 1)

            def z_b(g):
                th, et = g // 4, g % 4
                if g < 4:
                    pe.wait_ge(s_ge, 2 * (NC - 2) + g + 1)
                else:
                    pe.wait_ge(s_ze, g - 3)
                for k in range(KD):
                    mm = pe.matmul(ps[2 + g % 4][:, :], w_in_sb[:, k, 2 * DA + et * P:2 * DA + (et + 1) * P],
                                   T[:, k, th * 512:(th + 1) * 512], start=(k == 0), stop=(k == KD - 1))
                mm.then_inc(s_zb, 1)

            pe.wait_ge(s_cst, 1)
            turn_x(0)
            for c in range(NC):
                if c + 1 < NC:
                    turn_x(c + 1)
                z_a(c)
            for g in range(4):
                z_b(g)

            free4 = (0, 1, 6, 7)
            pe.wait_ge(s_vp, 2 * NC)
            pe.wait_ge(s_small, 16 * 9)
            for h in range(NH):
                if h >= 4:
                    pe.wait_ge(s_ya, h - 3)
                pe.matmul(ps[free4[h % 4]][:, :], wsp[:, h, :], v_sb[:, :, h * HD:(h + 1) * HD],
                          start=True, stop=True).then_inc(s_sg, 1)
            for g in range(4, 8):
                z_b(g)
            pe.wait_ge(s_ya, NH)
            for c in range(NC):
                pe.wait_ge(s_yn, c + 1)
                if c >= 4:
                    pe.wait_ge(s_tae, c - 3)
                for k in range(4):
                    tr = pe.transpose(ps[free4[c % 4]][:, k * P:(k + 1) * P], u_sb[:, c, k * P:(k + 1) * P], ident[:, :])
                tr.then_inc(s_ta, 1)

            terms = {0: [(0, 0)], 4: [(1, 0)], 1: [(2, 0), (3, 2)], 7: [(2, 0), (3, 1)], 2: [(4, 0), (5, 2)],
                     6: [(4, 0), (5, 1)], 3: [(6, 0), (7, 1)], 5: [(6, 0), (7, 2)]}

            def chan(s0):
                if s0 < 2:
                    pe.wait_ge(s_ze, 8)
                    pe.wait_ge(s_bf, BUTTERFLY)
                    pe.wait_ge(s_dft, 32)
                else:
                    pe.wait_ge(s_va, s0 - 1)
                    pe.wait_ge(s_vd, s0 - 1)
                for pair in range(4):
                    bank = ps[2 + 2 * (s0 % 2) + pair // 2]
                    for n, (a, m) in enumerate(terms[s0]):
                        mm = pe.matmul(bank[:, (pair % 2) * 256:(pair % 2 + 1) * 256], U[:, a, pair, :],
                                       dch[:, m, :, :], start=(n == 0), stop=(n == len(terms[s0]) - 1))
                mm.then_inc(s_v, 1)

            def posn(s0):
                pe.wait_ge(s_va, s0 + 1)
                pe.wait_ge(s_vd, s0 + 1)
                if s0 < 2:
                    pe.wait_ge(s_tae, NC)
                else:
                    pe.wait_ge(s_yb, s0 - 1)
                for ri in range(2):
                    mm = pe.matmul(ps[s0 % 2][:, :], dpos[:, ri, s0, :], V[:, s0 % 2, :, ri, :],
                                   start=(ri == 0), stop=(ri == 1))
                mm.then_inc(s_y, 1)

            def turn_b(s0):
                pe.wait_ge(s_yb, s0 + 1)
                if s0 >= 2:
                    pe.wait_ge(s_tbe, s0 - 1)
                for k in range(4):
                    tr = pe.transpose(ps[6 + s0 % 2][:, k * P:(k + 1) * P], yb[:, s0, k * P:(k + 1) * P], ident[:, :])
                tr.then_inc(s_tb, 1)

            for s0 in range(NC + 2):
                if s0 < NC:
                    chan(s0)
                if 1 <= s0 <= NC:
                    posn(s0 - 1)
                if s0 >= 2:
                    turn_b(s0 - 2)

            def w_o(c):
                if c == 0:
                    pe.wait_ge(s_wo_in, 16)
                    pe.wait_ge(s_tbe, NC)
                    pe.wait_ge(s_yb, NC)
                if c >= 2:
                    pe.wait_ge(s_hx, 2 * (c - 1))
                for half in range(2):
                    for k in range(KD):
                        mm = pe.matmul(ps[2 * (c % 2) + half][:, :], T[:, k, c * P:(c + 1) * P],
                                       w_out_sb[:, k, half * 512:(half + 1) * 512], start=(k == 0), stop=(k == KD - 1))
                mm.then_inc(s_wo, 1)

            def turn_hn(c):
                pe.wait_ge(s_hn, c + 1)
                if c >= 1:
                    pe.wait_ge(s_t3a, c)
                    pe.wait_ge(s_t3d, c)
                turn_rows(rows[:, c % 2, :], (4, 5)).then_inc(s_t3, 1)

            def router(c):
                pe.wait_ge(s_t3a, c + 1)
                pe.wait_ge(s_t3d, c + 1)
                if c >= 2:
                    pe.wait_ge(s_sc, c - 1)
                for k in range(KD):
                    mm = pe.matmul(ps[6 + c % 2][:, 0:NE], T[:, k, c * P:(c + 1) * P], wr_sb[:, k, :],
                                   start=(k == 0), stop=(k == KD - 1))
                mm.then_inc(s_rt, 1)

            for c in range(NC + 2):
                if c < NC:
                    w_o(c)
                if 1 <= c <= NC:
                    turn_hn(c - 1)
                if c >= 2:
                    router(c - 2)

            pe.wait_ge(s_sh_in, 32)
            pe.wait_ge(s_hx, 2 * NC)
            for q in range(4):
                th, ft = q // 2, q % 2
                if q >= 2:
                    pe.wait_ge(s_hm, q - 1)
                for j in range(2):
                    for k in range(KD):
                        mm = pe.matmul(ps[2 * (q % 2) + j][:, :], sgu_w[:, j, k, ft * P:(ft + 1) * P],
                                       T[:, k, th * 512:(th + 1) * 512], start=(k == 0), stop=(k == KD - 1))
                mm.then_inc(s_q, 1)
            pe.wait_ge(s_hm, 4)
            pe.wait_ge(s_mask, 1)
            flat = mask[:, :, :].rearrange("p c e -> p (c e)")
            pe.matmul(ps[0][:, :], tri[:, :], flat, start=True, stop=True)
            for d in range(1, NC):
                mm = pe.matmul(ps[0][:, d * NE:], ones[:, :], flat[:, 0:(NC - d) * NE], start=False, stop=True,
                               skip_group_check=True)
            for c in range(NC):
                mm = pe.matmul(ps[1][0:NE, 0:1], mask[:, c, :], ones[:, 0:1], start=(c == 0), stop=(c == NC - 1))
            mm.then_inc(s_pm, 1)

            def s_down(c):
                if c >= 2:
                    pe.wait_ge(s_y0, c - 1)
                if c == 0:
                    pe.wait_ge(s_sd_in, 16)
                    pe.wait_ge(s_sc, NC)
                    pe.wait_ge(s_t3a, NC)
                    pe.wait_ge(s_t3d, NC)
                for half in range(2):
                    for k in range(KF):
                        mm = pe.matmul(ps[4 + 2 * (c % 2) + half][:, :], hsT[:, k, c * P:(c + 1) * P],
                                       sd_w[:, k, half * 512:(half + 1) * 512], start=(k == 0), stop=(k == KF - 1))
                mm.then_inc(s_sdn, 1)

            for c in range(4):
                s_down(c)
            pe.wait_ge(s_chunks, 1)
            pe.matmul(ps[2][:, 0:NE], nchb[:, :], triI[:, :], start=True, stop=True).then_inc(s_pm, 1)
            for c in range(4, NC):
                s_down(c)
            pe.wait_ge(s_cols, 1)
            pe.matmul(ps[3][0:3, 0:P], cols[:, 0:3], ident[:, :], start=True, stop=True).then_inc(s_pm, 1)

            def slot_sums(i, u):
                e = look(pe, 0, i, NE - 1)
                pe.wait_ge(s_oh, i + 1)
                after(pe, s_cp, i)
                for c in range(NC):
                    mm = pe.matmul(ps[0][:, u * 8:u * 8 + 5], onehot[:, u, c, :], info[:, c, bass.ds(e, 1), :],
                                   start=(c == 0), stop=(c == NC - 1))
                mm.then_inc(s_ix, 1)

            def turn_item(i, u):
                pe.wait_ge(s_ga[u], 8 * i + (16 - 8 * u))
                turn_rows(Xg[:, u, :], (1, 2)).then_inc(s_tr, 1)

            def gate_up(i, u):
                e = look(pe, 0, i, NE - 1)
                slot = look(pe, 2, i, RING - 1)
                pe.wait_ge(s_w, e + 1)
                pe.wait_ge(s_xa, i + 1)
                pe.wait_ge(s_xd, i + 1)
                for k in range(KD):
                    mm = pe.matmul(ps[3 + u][:, :], xT[:, k, :], wgu[:, bass.ds(slot, 1), :, k, :],
                                   start=(k == 0), stop=(k == KD - 1))
                mm.then_inc(s_gu, 1)

            def down(i, first=False):
                slot = look(pe, 2, i, RING - 1)
                pe.wait_ge(s_he, i + 1)
                if not first:
                    pe.wait_ge(s_oa, i)
                    pe.wait_ge(s_od, i)
                for half in range(2):
                    for k in range(KF):
                        mm = pe.matmul(ps[6 + half][:, :], hT[:, k, :],
                                       wdn[:, bass.ds(slot, 1), k, half * 512:(half + 1) * 512],
                                       start=(k == 0), stop=(k == KF - 1))
                mm.then_inc(s_dn, 1)

            def turn_h(i, u):
                pe.wait_ge(s_h, i + 1)
                for k in range(KF):
                    tr = pe.transpose(ps[5][:, k * P:(k + 1) * P], hh[:, u, k * P:(k + 1) * P], ident[:, :])
                tr.then_inc(s_ht, 1)

            def item(i, u, first=0):
                gate_up(i, u)
                turn_item(i + 1, 1 - u)
                if first != 1:
                    down(i - 1, first == 2)
                turn_h(i, u)
                slot_sums(i + 2, u)

            pe.wait_ge(s_tab, 1)
            pe.wait_ge(s_y0, NC)
            slot_sums(0, 0)
            slot_sums(1, 1)
            turn_item(0, 0)
            item(0, 0, 1)
            item(1, 1, 2)
            n = item_count(pe)
            with pe.Fori(2, n, 2) as i0:
                item(i0, 0)
                item(i0 + 1, 1)
            down(item_count(pe, 1))

        @block.scalar
        def _(act):
            def square(src, scale, norm, c, done):
                act.activation(junk[:, 0:src.shape[-1]], src, ACT.Square, scale=scale,
                               accum_out=ms[:, norm, c:c + 1]).then_inc(done, 1)

            def sq1(c):
                act.wait_ge(s_x[c], 16)
                if c:
                    act.wait_ge(s_sq, c)
                square(xh[:, c, :], D ** -0.5, 0, c, s_sq)

            def evac_x(c):
                act.wait_ge(s_t1, c + 1)
                act.activation(T[:, 0:4, c * P:(c + 1) * P], ps[0 if c % 2 == 0 else 6][:, :].rearrange(
                    "p (k t) -> p k t", k=4), ACT.Copy).then_inc(s_t1a, 1)

            def gelu(c):
                for half, dst in enumerate((u_sb, v_sb)):
                    act.wait_ge(s_za, 2 * c + half + 1)
                    act.activation(dst[:, c, :], ps[2 + 2 * (c % 2) + half][:, :], ACT.Gelu).then_inc(s_ge, 1)

            sq1(0)
            sq1(1)
            for c in range(NC):
                evac_x(c)
                if c + 2 < NC:
                    sq1(c + 2)
                if c >= 1:
                    gelu(c - 1)
            gelu(NC - 1)

            def evac_z(g):
                act.wait_ge(s_zb, g + 1)
                act.activation(zT[:, g % 4, (g // 4) * 512:(g // 4 + 1) * 512], ps[2 + g % 4][:, :],
                               ACT.Copy).then_inc(s_ze, 1)

            for g in range(4):
                evac_z(g)
            act.wait_ge(s_sq, NC)
            act.wait_ge(s_ya, NH)
            for c in range(NC):
                if c:
                    act.wait_ge(s_sqa, c)
                square(u_sb[:, c, :], DA ** -0.5, 1, c, s_sqa)
            for g in range(4, 8):
                evac_z(g)
            for c in range(NC):
                act.wait_ge(s_ta, c + 1)
                act.activation(T[:, 0:4, c * P:(c + 1) * P], ps[(0, 1, 6, 7)[c % 4]][:, :].rearrange(
                    "p (k t) -> p k t", k=4), ACT.Copy).then_inc(s_tae, 1)
            for s0 in range(NC + 2):
                if s0 < NC:
                    act.wait_ge(s_v, s0 + 1)
                    if s0 >= 2:
                        act.wait_ge(s_y, s0 - 1)
                    act.activation(V[:, s0 % 2, 0:2, :, :], ps[2 + 2 * (s0 % 2)][:, :].rearrange(
                        "p (r i q) -> p r i q", r=2, i=2), ACT.Copy).then_inc(s_va, 1)
                if 1 <= s0 <= NC:
                    act.wait_ge(s_y, s0)
                    if s0 == 1:
                        act.wait_ge(s_sqa, NC)
                    else:
                        act.wait_ge(s_sqb, s0 - 1)
                    square(ps[(s0 - 1) % 2][:, :], DA ** -0.5, 2, s0 - 1, s_sqb)
                if s0 >= 2:
                    act.wait_ge(s_tb, s0 - 1)
                    act.activation(T[:, 4:8, s0 - 2:S:NC], ps[6 + s0 % 2][:, :].rearrange(
                        "p (k t) -> p k t", k=4), ACT.Copy).then_inc(s_tbe, 1)

            for c in range(NC + 2):
                if c < NC:
                    act.wait_ge(s_hx, 2 * c + 2)
                    if c == 0:
                        act.wait_ge(s_sqb, NC)
                    else:
                        act.wait_ge(s_sq2, c)
                    square(xh[:, c, :], D ** -0.5, 3, c, s_sq2)
                if 1 <= c <= NC:
                    act.wait_ge(s_t3, c)
                    act.activation(T[:, 0:4, (c - 1) * P:c * P], ps[4][:, :].rearrange(
                        "p (k t) -> p k t", k=4), ACT.Copy).then_inc(s_t3a, 1)
                if c >= 2:
                    act.wait_ge(s_rt, c - 1)
                    act.activation(scores[:, c - 2, :], ps[6 + c % 2][:, 0:NE], ACT.Sigmoid).then_inc(s_sc, 1)

            for q in range(4):
                act.wait_ge(s_q, q + 1)
                if q >= 2:
                    act.wait_ge(s_hm, q - 1)
                act.activation(s_tmp[:, q % 2, :], ps[2 * (q % 2)][:, :], ACT.Silu).then_inc(s_ssi, 1)

            def silu(i, u):
                act.wait_ge(s_gu, i + 1)
                after(act, s_h, i - 1)
                act.activation(hs[:, u, :], ps[3 + u][:, 0:F], ACT.Silu).then_inc(s_si, 1)

            def evac_xT(i):
                act.wait_ge(s_tr, i + 1)
                act.activation(xT[:, 0:4, :], ps[1][:, :].rearrange("p (k t) -> p k t", k=4),
                               ACT.Copy).then_inc(s_xa, 1)

            def evac_out(i, u, before=None):
                act.wait_ge(s_dn, i + 1)
                after(act, s_add, 16 * (i - 1 if before is None else before))
                act.activation(ob[:, u, 0:512], ps[6][:, :], ACT.Copy).then_inc(s_oa, 1)

            def evac_h(i):
                act.wait_ge(s_ht, i + 1)
                act.activation(hT[:, :, :], ps[5][:, 0:KF * P].rearrange("p (k t) -> p k t", k=KF),
                               ACT.Copy).then_inc(s_he, 1)

            def item(i, u, first=False):
                silu(i, u)
                evac_xT(i + 1)
                if not first:
                    evac_out(i - 1, 1 - u)
                evac_h(i)

            act.wait_ge(s_tab, 1)
            evac_xT(0)
            item(0, 0, True)
            item(1, 1)
            n = item_count(act)
            with act.Fori(2, n, 2) as i0:
                item(i0, 0)
                item(i0 + 1, 1)
            evac_out(item_count(act, 1), 1, item_count(act, 2))

            for c in range(NC):
                act.wait_ge(s_yl[c], 16)
                act.wait_ge(s_sq2, NC) if c == 0 else act.wait_ge(s_sqf, c)
                square(xh[:, c, :], D ** -0.5, 4, c, s_sqf)

        @block.vector
        def _(dv):
            def norm_x(c):
                dv.wait_ge(s_r1, c + 1)
                if c >= 2:
                    dv.wait_ge(s_t1, c - 1)
                if c == 0:
                    dv.wait_ge(s_g1, 16)
                dv.scalar_tensor_tensor(out=rows[:, c % 2, :], in0=xh[:, c, :], scalar=rs[:, 0, c:c + 1],
                                        in1=g1_row[:, :], op0=ALU.mult, op1=ALU.mult).then_inc(s_xs, 1)

            def evac_x(c):
                dv.wait_ge(s_t1, c + 1)
                dv.tensor_copy(T[:, 4:8, c * P:(c + 1) * P], ps[1 if c % 2 == 0 else 7][:, :].rearrange(
                    "p (k t) -> p k t", k=4)).then_inc(s_t1d, 1)

            def norm_v(c):
                dv.wait_ge(s_ge, 2 * c + 2)
                dv.bn_stats(bst[:, c, :], v_sb[:, c, :]).then_inc(s_ln, 1)
                dv.wait_ge(s_ln, 3 * c + 1)
                dv.bn_aggr(bag[:, c, :], bst[:, c, :]).then_inc(s_ln, 1)
                dv.wait_ge(s_lr, c + 1)
                dv.tensor_scalar(v_sb[:, c, :], v_sb[:, c, :], bag[:, c, 0:1], vr[:, c:c + 1], ALU.subtract,
                                 ALU.mult).then_inc(s_ln, 1)

            norm_x(0)
            norm_x(1)
            for c in range(NC):
                evac_x(c)
                if c + 2 < NC:
                    norm_x(c + 2)
                if c >= 1:
                    norm_v(c - 1)
            norm_v(NC - 1)

            dv.wait_ge(s_small, 16 * 9)
            for h in range(NH):
                dv.wait_ge(s_sg, h + 1)
                heads = u_sb[:, :, h * HD:(h + 1) * HD]
                dv.scalar_tensor_tensor(out=heads, in0=ps[(0, 1, 6, 7)[h % 4]][:, :].rearrange(
                    "p (c d) -> p c d", c=NC), scalar=bsp[:, h:h + 1], in1=heads, op0=ALU.add,
                    op1=ALU.mult).then_inc(s_ya, 1)
            for c in range(NC):
                dv.wait_ge(s_ra, c + 1)
                dv.scalar_tensor_tensor(out=u_sb[:, c, :], in0=u_sb[:, c, :], scalar=rs[:, 1, c:c + 1],
                                        in1=ga_row[:, :], op0=ALU.mult, op1=ALU.mult).then_inc(s_yn, 1)

            dv.wait_ge(s_ze, 8)
            steps = [0]

            def fly(ins):
                steps[0] += 1
                ins.then_inc(s_bf, 1)
                dv.wait_ge(s_bf, steps[0])

            a, b = ab[:, 0, :, :], ab[:, 1, :, :]
            pair4 = lambda t: t.rearrange("p r (a q) -> p a r q", q=P)
            fly(dv.tensor_tensor(a, zT[:, :, 0:512], zT[:, :, 512:1024], ALU.add))
            fly(dv.tensor_tensor(b, zT[:, :, 0:512], zT[:, :, 512:1024], ALU.subtract))
            fly(dv.tensor_tensor(U[:, 4:6, :, :], pair4(a[:, :, 0:256]), pair4(a[:, :, 256:512]), ALU.subtract))
            fly(dv.tensor_tensor(U[:, 6:8, :, :], pair4(a[:, :, 0:256]), pair4(a[:, :, 256:512]), ALU.add))
            fly(dv.tensor_tensor(U[:, 0, :, :], U[:, 6, :, :], U[:, 7, :, :], ALU.add))
            fly(dv.tensor_tensor(U[:, 1, :, :], U[:, 6, :, :], U[:, 7, :, :], ALU.subtract))
            dif, tot = a[:, :, 0:128], a[:, :, 128:256]
            fly(dv.tensor_tensor(dif, b[:, :, 128:256], b[:, :, 384:512], ALU.subtract))
            fly(dv.tensor_tensor(tot, b[:, :, 128:256], b[:, :, 384:512], ALU.add))
            for j, r in ((2, R8), (6, -R8)):
                fly(dv.scalar_tensor_tensor(out=U[:, j, :, :], in0=dif, scalar=r, in1=b[:, :, 0:128], op0=ALU.mult,
                                            op1=ALU.add))
                fly(dv.scalar_tensor_tensor(out=U[:, j + 1, :, :], in0=tot, scalar=r, in1=b[:, :, 256:384],
                                            op0=ALU.mult, op1=ALU.add))
            assert steps[0] == BUTTERFLY

            for s0 in range(NC + 1):
                if s0 < NC:
                    dv.wait_ge(s_v, s0 + 1)
                    if s0 >= 2:
                        dv.wait_ge(s_y, s0 - 1)
                    dv.tensor_copy(V[:, s0 % 2, 2:4, :, :], ps[3 + 2 * (s0 % 2)][:, :].rearrange(
                        "p (r i q) -> p r i q", r=2, i=2)).then_inc(s_vd, 1)
                if s0 >= 1:
                    dv.wait_ge(s_rb, s0)
                    dv.scalar_tensor_tensor(out=yb[:, s0 - 1, :], in0=ps[(s0 - 1) % 2][:, :],
                                            scalar=rs[:, 2, s0 - 1:s0], in1=gb_row[:, :], op0=ALU.mult,
                                            op1=ALU.mult).then_inc(s_yb, 1)

            for c in range(NC + 1):
                if c < NC:
                    dv.wait_ge(s_wo, c + 1)
                    for half in range(2):
                        piece = xh[:, c, half * 512:(half + 1) * 512]
                        dv.tensor_tensor(piece, ps[2 * (c % 2) + half][:, :], piece, ALU.add).then_inc(s_hx, 1)
                if c >= 1:
                    dv.wait_ge(s_t3, c)
                    dv.tensor_copy(T[:, 4:8, (c - 1) * P:c * P], ps[5][:, :].rearrange(
                        "p (k t) -> p k t", k=4)).then_inc(s_t3d, 1)
                if c < NC:
                    dv.wait_ge(s_r2, c + 1)
                    if c >= 2:
                        dv.wait_ge(s_t3, c - 1)
                        dv.wait_ge(s_hst[c % 2], 16 * (c // 2))
                    dv.scalar_tensor_tensor(out=rows[:, c % 2, :], in0=xh[:, c, :], scalar=rs[:, 3, c:c + 1],
                                            in1=g2_row[:, :], op0=ALU.mult, op1=ALU.mult).then_inc(s_hn, 1)

            count = [0]

            def step(ins):
                count[0] += 1
                ins.then_inc(s_rv, 1)
                dv.wait_ge(s_rv, count[0])

            def many(instructions):
                for ins in instructions:
                    count[0] += 1
                    ins.then_inc(s_rv, 1)
                dv.wait_ge(s_rv, count[0])

            def shared_h(q):
                dv.wait_ge(s_ssi, q + 1)
                dv.tensor_tensor(hsT[:, q % 2, (q // 2) * 512:(q // 2 + 1) * 512], s_tmp[:, q % 2, :],
                                 ps[2 * (q % 2) + 1][:, :], ALU.mult).then_inc(s_hm, 1)

            dv.wait_ge(s_cst, 1)
            dv.wait_ge(s_sc, NC)
            wide = [P, NC, NE]
            step(dv.tensor_tensor(rt_a[:, :, :], scores[:, :, :], rb_row[:, None, :].to_broadcast(wide), ALU.add))
            many(dv.max(m8[:, c, g, :], rt_a[:, c, g * GE:(g + 1) * GE]) for c in range(NC) for g in range(NG))
            step(dv.tensor_tensor(gs[:, :, :], m8[:, :, :, 0], m8[:, :, :, 1], ALU.add))
            many(dv.max(gtop[:, c, :], gs[:, c, :]) for c in range(NC))
            many(dv.max_index(gidx[:, c, :], gtop[:, c, :], gs[:, c, :]) for c in range(NC))
            step(dv.tensor_copy(gidxf[:, :, :], gidx[:, :, 0:TOPG]))
            step(dv.tensor_tensor(geq[:, :, :, :], gidxf[:, :, None, :].to_broadcast([P, NC, NG, TOPG]),
                                  gi[:, None, :, None].to_broadcast([P, NC, NG, TOPG]), ALU.is_equal))
            step(dv.tensor_reduce(gm[:, :, :], geq[:, :, :, :], AX.X, ALU.max))
            step(dv.tensor_scalar(gs[:, :, :], gm[:, :, :], 1.0, BIG, ALU.subtract, ALU.mult))
            by_group = lambda t: t[:, :, :].rearrange("p c (g e) -> p c g e", g=NG)
            step(dv.tensor_tensor(by_group(rt_b), by_group(rt_a), gs[:, :, :, None].to_broadcast([P, NC, NG, GE]),
                                  ALU.add))
            many(dv.max(etop[:, c, :], rt_b[:, c, :]) for c in range(NC))
            many(dv.match_replace(rt_a[:, c, :], etop[:, c, :], rt_b[:, c, :], -3.3e38) for c in range(NC))
            dv.wait_ge(s_hst[0], 16 * 4)
            dv.wait_ge(s_hst[1], 16 * 4)
            dv.wait_ge(s_t3, NC)
            shared_h(0)
            step(dv.tensor_tensor(mask[:, :, :], rt_a[:, :, :], rt_b[:, :, :], ALU.not_equal))
            dv.sem_inc(s_mask, 1)
            step(dv.tensor_tensor(rt_a[:, :, :], scores[:, :, :], mask[:, :, :], ALU.mult))
            step(dv.tensor_reduce(gsum[:, :], rt_a[:, :, :], AX.X, ALU.add))
            step(dv.reciprocal(grec[:, :], gsum[:, :]))
            step(dv.tensor_scalar(grec[:, :], grec[:, :], RSCALE, None, ALU.mult))
            step(dv.tensor_tensor(rt_a[:, :, :], rt_a[:, :, :], grec[:, :, None].to_broadcast(wide), ALU.mult))
            shared_h(1)
            dv.wait_ge(s_info, 3)
            step(dv.tensor_copy(info[:, :, :, 2], rt_a[:, :, :]))
            step(dv.tensor_tensor(rt_b[:, :, :], rt_a[:, :, :], info[:, :, :, 2], ALU.subtract))
            step(dv.tensor_copy(info[:, :, :, 3], rt_b[:, :, :]))
            step(dv.tensor_tensor(rt_a[:, :, :], rt_b[:, :, :], info[:, :, :, 3], ALU.subtract))
            step(dv.tensor_copy(info[:, :, :, 4], rt_a[:, :, :]))
            shared_h(2)
            shared_h(3)
            dv.wait_ge(s_pm, 1)
            step(dv.scalar_tensor_tensor(out=rt_b[:, :, :], in0=ps[0][:, :].rearrange("p (c e) -> p c e", c=NC),
                                         scalar=1.0, in1=mask[:, :, :], op0=ALU.add, op1=ALU.mult))
            step(dv.tensor_scalar(pos[:, :, :], rt_b[:, :, :], -1.0, None, ALU.add))
            for j in range(1, MAXCH):
                step(dv.scalar_tensor_tensor(out=nch[:, j:j + 1], in0=ps[1][0:NE, 0:1], scalar=float(P * j),
                                             in1=nch[:, j - 1:j], op0=ALU.is_gt, op1=ALU.add))
            step(dv.tensor_copy(nchb[:, :], nch[:, MAXCH - 1:MAXCH].to_broadcast([NE, P])))
            dv.sem_inc(s_chunks, 1)

            def y0(c):
                dv.wait_ge(s_sdn, c + 1)
                for half in range(2):
                    piece = xh[:, c, half * 512:(half + 1) * 512]
                    ins = dv.tensor_tensor(piece, ps[4 + 2 * (c % 2) + half][:, :], piece, ALU.add)
                ins.then_inc(s_y0, 1)

            for c in range(4):
                y0(c)
            dv.wait_ge(s_pm, 2)
            step(dv.tensor_copy(le[:, 2, :], ps[2][:, 0:NE]))
            step(dv.tensor_scalar(le[:, 0, :], le[:, 2, :], pidx[:, 0:1], None, ALU.is_le))
            step(dv.tensor_tensor(le[:, 1, :], le[:, 0, :], le[:, 2, :], ALU.mult))
            step(dv.tensor_reduce(cols[:, 3:4], le[:, 0, :], AX.X, ALU.add))
            step(dv.tensor_reduce(cols[:, 4:5], le[:, 1, :], AX.X, ALU.max))
            step(dv.tensor_scalar(cols[:, 0:1], cols[:, 3:4], float(NE - 1), None, ALU.min))
            step(dv.tensor_scalar(thirds[:, :], cols[:, 0:1], -1.0, 1.0 / RING, ALU.add, ALU.mult))
            step(dv.scalar_tensor_tensor(out=cols[:, 2:3], in0=thirds[:, :], scalar=-float(RING), in1=cols[:, 0:1],
                                         op0=ALU.mult, op1=ALU.add))
            step(dv.tensor_scalar(cols[:, 5:6], cols[:, 4:5], pidx[:, 0:1], float(P), ALU.subtract, ALU.mult))
            step(dv.tensor_scalar(cols[:, 6:7], cols[:, 3:4], float(NE), -float(S), ALU.is_ge, ALU.mult))
            step(dv.tensor_tensor(cols[:, 7:8], cols[:, 5:6], cols[:, 6:7], ALU.add))
            step(dv.tensor_scalar(cols[:, 1:2], cols[:, 7:8], float(S), 0.0, ALU.add, ALU.max))
            dv.sem_inc(s_cols, 1)
            for c in range(4, NC):
                y0(c)
            step(dv.tensor_copy(ends[0:1, 0:NE], ps[2][0:1, 0:NE]))
            step(dv.tensor_scalar(ends[0:1, NE + 3:NE + 4], ps[2][0:1, NE - 1:NE], 0.5, 0.5, ALU.add, ALU.mult))
            for less in (2, 1, 0):
                step(dv.tensor_scalar(ends[0:1, NE + less:NE + less + 1], ends[0:1, NE + 3:NE + 4], 2.0, float(less),
                                      ALU.mult, ALU.subtract))
            dv.wait_ge(s_pm, 3)
            dv.tensor_copy(tab[0:3, 0:P], ps[3][0:3, 0:P]).then_inc(s_tab, 1)

            def one_hot(i, u):
                e = look(dv, 0, i, NE - 1)
                back = look(dv, 1, i, S)
                shape = [P, NC, P]
                dv.tensor_tensor(onehot[:, u, :, :], pos[:, :, bass.ds(e, 1)].to_broadcast(shape),
                                 slots[:, None, bass.ds(S - back, P)].to_broadcast(shape),
                                 ALU.is_equal).then_inc(s_oh, 1)

            def indices(i, u):
                sums = ps[0][:, u * 8:u * 8 + 5]
                dv.wait_ge(s_ix, i + 1)
                after(dv, s_ia, i)
                after(dv, s_gt, i)
                dv.tensor_copy(sumf[:, 0:5], sums).then_inc(s_cp, 1)
                sums = sumf
                dv.wait_ge(s_cp, i + 1)
                dv.scalar_tensor_tensor(out=idxf[:, :], in0=sums[:, 0:1], scalar=EMPTY, in1=sums[:, 1:2],
                                        op0=ALU.add, op1=ALU.add).then_inc(s_it, 1)
                dv.scalar_tensor_tensor(out=gate_all[:, bass.ds(i, 1)], in0=sums[:, 2:3], scalar=sums[:, 3:4],
                                        in1=sums[:, 4:5], op0=ALU.add, op1=ALU.add).then_inc(s_gt, 1)
                dv.wait_ge(s_it, i + 1)
                dv.tensor_scalar(idxg[:, u:u + 1], idxf[:, :], dump[:, 0:1], None, ALU.min).then_inc(s_id, 1)
                dv.tensor_scalar(idx_all[:, bass.ds(i, 1)], idxf[:, :], dump[:, 0:1], None, ALU.min).then_inc(s_ia, 1)

            def gated_h(i, u):
                dv.wait_ge(s_si, i + 1)
                dv.wait_ge(s_gt, i + 1)
                after(dv, s_ht, i - 1)
                dv.scalar_tensor_tensor(out=hh[:, u, :], in0=hs[:, u, :], scalar=gate_all[:, bass.ds(i, 1)],
                                        in1=ps[3 + u][:, F:2 * F], op0=ALU.mult, op1=ALU.mult).then_inc(s_h, 1)

            def evac_xT(i):
                dv.wait_ge(s_tr, i + 1)
                dv.tensor_copy(xT[:, 4:8, :], ps[2][:, :].rearrange("p (k t) -> p k t", k=4)).then_inc(s_xd, 1)

            def evac_out(i, u, before=None):
                dv.wait_ge(s_dn, i + 1)
                dv.wait_ge(s_ia, i + 1)
                after(dv, s_add, 16 * (i - 1 if before is None else before))
                dv.tensor_scalar(idxs[:, u:u + 1], idx_all[:, bass.ds(i, 1)], 0.0, None, ALU.add).then_inc(s_is, 1)
                dv.tensor_copy(ob[:, u, 512:1024], ps[7][:, :]).then_inc(s_od, 1)

            def item(i, u, first=False):
                one_hot(i + 2, u)
                gated_h(i, u)
                evac_xT(i + 1)
                if not first:
                    evac_out(i - 1, 1 - u)
                indices(i + 2, u)

            dv.wait_ge(s_tab, 1)
            one_hot(0, 0)
            one_hot(1, 1)
            indices(0, 0)
            indices(1, 1)
            evac_xT(0)
            item(0, 0, True)
            item(1, 1)
            n = item_count(dv)
            with dv.Fori(2, n, 2) as i0:
                item(i0, 0)
                item(i0 + 1, 1)
            evac_out(item_count(dv, 1), 1, item_count(dv, 2))

            dv.wait_ge(s_gf, 16)
            for c in range(NC):
                dv.wait_ge(s_rf, c + 1)
                dv.scalar_tensor_tensor(out=xh[:, c, :], in0=xh[:, c, :], scalar=rs[:, 4, c:c + 1],
                                        in1=gf_row[:, :], op0=ALU.mult, op1=ALU.mult).then_inc(s_of, 1)

        @block.gpsimd
        def _(gp):
            made = [0]

            def make(ins):
                made[0] += 1
                ins.then_inc(s_mk, 1)

            make(gp.memset(ident[:, :], 0.0))
            make(gp.memset(tri[:, :], 1.0))
            make(gp.memset(triI[:, :], 1.0))
            make(gp.memset(ones[:, :], 1.0))
            make(gp.memset(nch[:, 0:1], 1.0))
            make(gp.memset(tab[:, :], 0))
            make(gp.memset(mhalf[:, :], -0.5))
            make(gp.iota(gi[:, :], pattern=[[1, NG]], base=0, channel_multiplier=0, allow_small_or_imprecise_dtypes=True))
            make(gp.iota(pidx[:, :], pattern=[[1, 1]], base=0, channel_multiplier=1, allow_small_or_imprecise_dtypes=True))
            make(gp.iota(dump[:, :], pattern=[[1, 1]], base=S, channel_multiplier=1, allow_small_or_imprecise_dtypes=True))
            gp.wait_ge(s_mk, made[0])
            make(gp.affine_select(out=ident[:, :], in_=ident[:, :], compare_op=ALU.not_equal, fill=1.0, base=0,
                                  pattern=[[-1, P]], channel_multiplier=1))
            make(gp.affine_select(out=tri[:, :], in_=tri[:, :], compare_op=ALU.is_gt, fill=0.0, base=0,
                                  pattern=[[1, P]], channel_multiplier=-1))
            make(gp.affine_select(out=triI[:, :], in_=triI[:, :], compare_op=ALU.is_ge, fill=0.0, base=0,
                                  pattern=[[1, NE]], channel_multiplier=-1))
            gp.wait_ge(s_mk, made[0])
            gp.sem_inc(s_cst, 1)

            roots = [0]

            def inverse_root(dst, src, done):
                roots[0] += 1
                gp.tensor_scalar(dst, src, EPS, None, ALU.add).then_inc(s_eps, 1)
                gp.wait_ge(s_eps, roots[0])
                gp.tensor_tensor(dst, dst, mhalf[:, :], ALU.pow).then_inc(done, 1)

            def rstd(norm, c, squares, done):
                gp.wait_ge(squares, c + 1)
                inverse_root(rs[:, norm, c:c + 1], ms[:, norm, c:c + 1], done)

            rstd(0, 0, s_sq, s_r1)
            rstd(0, 1, s_sq, s_r1)
            gp.wait_ge(s_small, 16 * 9)
            for step_ in range(NC + 1):
                if step_ + 2 < NC:
                    rstd(0, step_ + 2, s_sq, s_r1)
                if step_ == 0:
                    continue
                c = step_ - 1
                gp.wait_ge(s_ln, 3 * c + 2)
                inverse_root(vr[:, c:c + 1], bag[:, c, 1:2], s_lr)
                gp.wait_ge(s_ln, 3 * (c + 1))
                gp.tensor_tensor(v_sb[:, c, :], v_sb[:, c, :], lng_row[:, :], ALU.mult).then_inc(s_vp, 1)
                gp.wait_ge(s_vp, 2 * c + 1)
                gp.tensor_tensor(v_sb[:, c, :], v_sb[:, c, :], lnb_row[:, :], ALU.add).then_inc(s_vp, 1)
            for c in range(NC):
                rstd(1, c, s_sqa, s_ra)
            for c in range(NC):
                rstd(2, c, s_sqb, s_rb)

            gp.wait_ge(s_yb, NC)
            gp.iota(info[:, :, :, 0], pattern=[[P, NC], [0, NE]], base=-int(EMPTY), channel_multiplier=0,
                    allow_small_or_imprecise_dtypes=True).then_inc(s_info, 1)
            gp.iota(info[:, :, :, 1], pattern=[[0, NC], [0, NE]], base=0, channel_multiplier=1,
                    allow_small_or_imprecise_dtypes=True).then_inc(s_info, 1)
            gp.iota(slots[:, :], pattern=[[1, S + P]], base=0, channel_multiplier=0,
                    allow_small_or_imprecise_dtypes=True).then_inc(s_info, 1)

            for c in range(NC):
                rstd(3, c, s_sq2, s_r2)

            top_row = gp.to_reg(S - 1)
            top_dump = gp.to_reg(S + P - 1)

            def gather(i, u):
                gp.wait_ge(s_id, i + 1)
                after(gp, s_tr, i - 1)
                gp.sem_inc(s_turn, 1)
                gp.indirect_dma_start(out=Xg[:, u, :], out_offset=None, in_=hn_d[:, :],
                                      in_offset=bass.IndirectOffsetOnAxis(ap=idxg[:, u:u + 1], axis=0),
                                      bounds_check=top_row, oob_is_err=False).then_inc(s_ga[u], 16)

            def add_rows(i, u):
                gp.wait_ge(s_oa, i + 1)
                gp.wait_ge(s_od, i + 1)
                gp.wait_ge(s_is, i + 1)
                after(gp, s_add, 16 * i)
                gp.sem_inc(s_turn, 1)
                gp.indirect_dma_start(out=y_d[:, :], out_offset=bass.IndirectOffsetOnAxis(ap=idxs[:, u:u + 1], axis=0),
                                      in_=ob[:, u, :], in_offset=None, compute_op=ALU.add,
                                      bounds_check=top_dump).then_inc(s_add, 16)

            gp.wait_ge(s_hst[0], 16 * 4)
            gp.wait_ge(s_hst[1], 16 * 4)
            gp.wait_ge(s_yst, 16 * (NC + 1))
            gp.wait_ge(s_tab, 1)
            gather(0, 0)
            gather(1, 1)
            gather(2, 0)
            add_rows(0, 0)
            gather(3, 1)
            n = item_count(gp)
            with gp.Fori(2, n, 2) as i0:
                add_rows(i0 - 1, 1)
                gather(i0 + 2, 0)
                add_rows(i0, 0)
                gather(i0 + 3, 1)
            add_rows(item_count(gp, 1), 1)
            for c in range(NC):
                rstd(4, c, s_sqf, s_rf)


BUTTERFLY = 12


def after(eng, semaphore, value):
    if not isinstance(value, int) or value > 0:
        eng.wait_ge(semaphore, value)


_INS = ["x", "norm1_g", "w_in", "sgu_ln_g", "sgu_ln_b", "w_spatial", "b_spatial", "out_norm_a_g", "out_norm_b_g",
        "w_out", "norm2_g", "w_router", "router_bias", "w_gate", "w_up", "w_down", "ws_gate", "ws_up", "ws_down"]


def dft_tables():
    import numpy as np
    q = np.arange(P)[:, None, None]
    s = NC * np.arange(P)[None, None, :] + np.arange(NC)[None, :, None]
    th = 2 * np.pi * ((q * s) % S) / S
    pos = np.stack([np.cos(th), np.sin(th)], axis=1) / 256.0
    k = np.arange(64)
    th = 2 * np.pi * (np.outer(k, k) % 64) / 64
    C = np.kron(np.eye(2), np.cos(th))
    Sn = np.kron(np.eye(2), np.sin(th))
    ch = np.stack([np.stack([C, -Sn], 1), np.stack([Sn, C], 1), np.stack([-Sn, -C], 1)], 1)
    return pos.astype(np.float32), ch.astype(np.float32)


def kernel(**inputs):
    import numpy as np
    import concourse.bacc as bacc
    from concourse.bass_utils import run_bass_kernel_spmd as run

    nc = bacc.Bacc("TRN2", target_bir_lowering=False, num_devices=1)
    a = {k: np.asarray(inputs[k])[0] for k in _INS}
    a["final_norm_g"] = np.asarray(inputs["final_norm_g"])
    a["w_spatial"] = np.ascontiguousarray(a["w_spatial"].transpose(0, 2, 1))
    a["b_spatial"] = np.ascontiguousarray(a["b_spatial"].T)
    a["dft_pos"], a["dft_ch"] = dft_tables()
    order = _INS + ["dft_pos", "dft_ch"]
    order.insert(len(_INS), "final_norm_g")
    h = {k: nc.dram_tensor("in_" + k, a[k].shape, F32, kind="ExternalInput").ap() for k in order}
    out = nc.dram_tensor("result", (S, D), F32, kind="ExternalOutput").ap()
    hn_d = nc.dram_tensor("hn_rows_dram", (S, D), F32, kind="Internal").ap()
    y_d = nc.dram_tensor("y_rows_dram", (S + P, D), F32, kind="Internal").ap()
    build(nc, h["x"], h["norm1_g"], h["w_in"], h["sgu_ln_g"], h["sgu_ln_b"], h["w_spatial"], h["b_spatial"],
          h["out_norm_a_g"], h["out_norm_b_g"], h["w_out"], h["norm2_g"], h["w_router"], h["router_bias"],
          h["w_gate"], h["w_up"], h["w_down"], h["ws_gate"], h["ws_up"], h["ws_down"], h["dft_pos"], h["dft_ch"],
          h["final_norm_g"], out, hn_d, y_d)
    r = run(nc, [{"in_" + k: np.ascontiguousarray(a[k]) for k in order}], core_ids=[0])
    return r.results[0]["result"].reshape(1, S, D)
```

```python
from contextlib import ExitStack

import concourse.bass as bass
from concourse import mybir

P = 128
D = 1024
S = 1024
NC = S // P
KD = D // P
DA = 512
NH = 8
HD = DA // NH
NE = 64
TOPK = 8
NG = 8
GE = NE // NG
TOPG = 4
F = 256
KF = F // P
RSCALE = 2.5
EPS = 1e-6
MAXCH = S // P
NITEM = (S * TOPK) // P + NE
TAB = NITEM + 8
EMPTY = 4096.0
BIG = 3.0e38
TURN = 3
GU_PARTS = 4

ALU = mybir.AluOpType
ACT = mybir.ActivationFunctionType
AX = mybir.AxisListType
F32 = mybir.dt.float32
BF16 = mybir.dt.bfloat16
F32R = mybir.dt.float32r
I32 = mybir.dt.int32
U32 = mybir.dt.uint32
R8 = 0.5 ** 0.5


def build(nc, x, g1, w_in, ln_g, ln_b, wsT, bsT, ga, gb, w_out, g2, w_router, rbias, wg, wu, wd,
          sg, su, sd, dft_pos, dft_ch, gf, out, hn_d, y_d):
    ctx = ExitStack()
    with ctx:
        top = [nc.sbuf_base]

        def place(name, shape, dt, at=None):
            size = 2 if dt == BF16 else 4
            n = size
            for s in shape[1:]:
                n *= s
            n = (n + 31) // 32 * 32
            if at is None:
                at = top[0]
                top[0] += n
            return nc.alloc_sbuf_tensor_at(name, shape, dt, offset=at)

        base0 = top[0] = (top[0] + 63) // 64 * 64
        KB = 1024
        X_AT = base0
        T_AT = X_AT + 32 * KB
        W_AT = T_AT + 32 * KB
        U_AT = W_AT + 48 * KB
        V_AT = U_AT + 16 * KB
        Z_AT = V_AT + 16 * KB
        S_AT = Z_AT + 16 * KB
        D_AT = S_AT + 8 * KB
        R_AT = D_AT + 8 * KB
        top[0] = R_AT + 12 * KB

        xh = place("xh", [P, NC, D], F32, X_AT)
        T = place("T", [P, KD, S], F32, T_AT)
        ab = place("ab", [P, 2, 4, 512], F32, T_AT + 16 * KB)
        w_in_sb = place("w_in_sb", [P, KD, 3 * DA], F32, W_AT)
        w_out_sb = place("w_out_sb", [P, KD, D], F32, W_AT)
        U = place("U", [P, 8, 4, P], F32, W_AT + 32 * KB)
        sgu_w = place("sgu_w", [P, 2, KD, F], F32, W_AT + 32 * KB)
        u_sb = place("u_sb", [P, NC, DA], F32, U_AT)
        v_sb = place("v_sb", [P, NC, DA], F32, V_AT)
        yb = place("yb", [P, NC, DA], F32, V_AT)
        zT = place("zT", [P, 4, S], F32, Z_AT)
        rows = place("rows", [P, 2, D], F32, S_AT)
        V = place("V", [P, 2, 4, 2, P], F32, S_AT)
        hsT = place("hsT", [P, KF, S], F32, S_AT)
        dpos = place("dpos", [P, 2, 8, P], F32, D_AT)
        sd_w = place("sd_w", [P, KF, D], F32, D_AT)
        g1_row = place("g1_row", [P, D], F32, R_AT)
        lng_row = place("lng_row", [P, DA], F32, R_AT + 4 * KB)
        lnb_row = place("lnb_row", [P, DA], F32, R_AT + 6 * KB)
        ga_row = place("ga_row", [P, DA], F32, R_AT + 8 * KB)
        gb_row = place("gb_row", [P, DA], F32, R_AT + 10 * KB)
        pos = place("pos", [P, NC, NE], F32, R_AT)
        info = place("info", [P, NC, NE, 5], BF16, R_AT + 2 * KB)
        slots = place("slots", [P, 1024 + P], F32, R_AT + 7 * KB)
        raw_gu = place("raw_gu", [P, 2, 2, KD, F], F32, U_AT)
        raw_dn = place("raw_dn", [P, 2, KF, D], F32, Z_AT)
        w_gu = place("w_gu", [P, 2, 2, 2, KD, F], F32R, X_AT)
        w_dn = place("w_dn", [P, 2, 2, KF, D], F32R, W_AT)
        s_tmp = place("s_tmp", [P, 2, 512], F32, W_AT + 24 * KB)
        rt_a = place("rt_a", [P, NC, NE], F32, W_AT + 28 * KB)
        rt_b = place("rt_b", [P, NC, NE], F32, W_AT + 30 * KB)
        Xg = place("Xg", [P, TURN, D], F32, W_AT + 32 * KB)
        xTh = place("xTh", [P, KD, P], F32R, W_AT + 44 * KB)
        ob = place("ob", [P, TURN, D], F32, S_AT)
        xTl = place("xTl", [P, KD, P], F32R, S_AT + 12 * KB)
        g2_row = place("g2_row", [P, D], F32)
        idx_all = place("idx_all", [P, TAB], I32, top[0] - 4 * KB)
        gate_all = place("gate_all", [P, TAB], F32, top[0] - 3 * KB)
        le = place("le", [P, 3, NE], F32, top[0] - 2 * KB)
        dch = place("dch", [P, 3, 2, P], F32)
        C_AT = top[0] - 3 * KB
        scores = place("scores", [P, NC, NE], F32, C_AT)
        mask = place("mask", [P, NC, NE], BF16, C_AT + 2 * KB)
        hs = place("hs", [P, F], F32, C_AT)
        hh = place("hh", [P, F], F32, C_AT + KB)
        hTh = place("hTh", [P, KF, P], F32R, C_AT + 2 * KB)
        wsp = place("wsp", [P, NH, P], F32)
        M_AT = top[0] - 4 * KB
        onehot = place("onehot", [P, NC, P], BF16, M_AT)
        m8 = place("m8", [P, NC, NG, 8], F32, M_AT)
        geq = place("geq", [P, NC, NG, TOPG], F32, M_AT + 2 * KB)
        gs = place("gs", [P, NC, NG], F32, M_AT + 3 * KB)
        gtop = place("gtop", [P, NC, 8], F32, M_AT + 3 * KB + 256)
        gidx = place("gidx", [P, NC, 8], U32, M_AT + 3 * KB + 512)
        etop = place("etop", [P, NC, 8], F32, M_AT + 3 * KB + 768)
        junk = place("junk", [P, D], BF16)
        bsp = place("bsp", [P, NH], F32)
        ident = place("ident", [P, P], F32)
        wr_sb = place("wr_sb", [P, KD, NE], F32)
        hTl = place("hTl", [P, KF, P], F32R, top[0] - 2 * KB)
        rb_row = place("rb_row", [P, NE], F32)
        tri = place("tri", [P, P], BF16)
        triI = place("triI", [NE, NE], BF16)
        ones = place("ones", [P, P], BF16)
        ms = place("ms", [P, 5, NC], F32)
        rs = place("rs", [P, 5, NC], F32)
        bst = place("bst", [P, NC, 6], F32)
        bag = place("bag", [P, NC, 2], F32)
        vr = place("vr", [P, NC], F32)
        gidxf = place("gidxf", [P, NC, TOPG], F32)
        gi = place("gi", [P, NG], F32)
        gm = place("gm", [P, NC, NG], F32)
        gsum = place("gsum", [P, NC], F32)
        grec = place("grec", [P, NC], F32)
        pidx = place("pidx", [P, 1], F32)
        dump = place("dump", [P, 1], F32)
        nch = place("nch", [NE, 1 + MAXCH], F32)
        nchb = place("nchb", [NE, P], BF16)
        cols = place("cols", [P, 12], F32)
        tab = place("tab", [4, TAB], I32)
        ends = place("ends", [1, NE + 5], I32)
        mhalf = place("mhalf", [P, 1], F32)
        halves = place("halves", [P, 1], I32)
        sumf = place("sumf", [P, 8], F32)
        idxf = place("idxf", [P, 1], F32)
        idxg = place("idxg", [P, TURN], I32)
        idxs = place("idxs", [P, TURN], I32)
        assert top[0] <= nc.sbuf_usable_end, (top[0], nc.sbuf_usable_end)
        gf_row = place("gf_row", [P, D], F32, Z_AT)

        ps = [ctx.enter_context(nc.psum_tensor(f"ps{i}", [P, 512], F32)) for i in range(8)]

        def sem(name):
            return ctx.enter_context(nc.semaphore(name))

        s_x = [sem(f"x_in{c}") for c in range(NC)]
        s_g1, s_wi, s_small, s_dft = sem("g1_in"), sem("w_in_in"), sem("small_in"), sem("dft_in")
        s_wo_in, s_sh_in, s_sd_in, s_gf = sem("w_out_in"), sem("shared_in"), sem("shared_down_in"), sem("gf_in")
        s_lr, s_eps = sem("v_rstd"), sem("eps_added")
        s_cst, s_mk, s_info = sem("consts_ready"), sem("const_made"), sem("token_info")
        s_sq, s_r1, s_xs, s_t1, s_t1a, s_t1d = (sem(n) for n in (
            "sq1", "rstd1", "xn_rows", "xn_tr", "xn_evac_act", "xn_evac_dve"))
        s_za, s_ge, s_ln, s_vp, s_zb, s_ze = (sem(n) for n in (
            "za_done", "gelu_done", "ln_step", "v_ready", "zb_done", "zT_ready"))
        s_sg, s_ya, s_sqa, s_ra, s_yn, s_ta, s_tae = (sem(n) for n in (
            "sgu_done", "ya_ready", "sqa", "rstda", "ya_normed", "ya_tr", "ya_evac"))
        s_bf, s_v, s_va, s_vd, s_y, s_sqb, s_rb, s_yb, s_tb, s_tbe = (sem(n) for n in (
            "butterfly", "V_done", "V_evac_act", "V_evac_dve", "Y_done", "sqb", "rstdb", "yb_ready", "yb_tr",
            "yb_evac"))
        s_wo, s_hx, s_sq2, s_r2, s_hn, s_t3, s_t3a, s_t3d, s_rt, s_sc = (sem(n) for n in (
            "w_out_done", "h_ready", "sq2", "rstd2", "hn_rows", "hn_tr", "hn_evac_act", "hn_evac_dve", "router_done",
            "scores_ready"))
        s_hst = [sem(f"hn_stored{i}") for i in range(2)]
        s_q, s_ssi, s_hm, s_sdn, s_y0, s_yst = (sem(n) for n in (
            "shared_gu", "shared_silu", "shared_h", "shared_down", "y0_ready", "y0_stored"))
        s_mask, s_chunks, s_cols = sem("mask_ready"), sem("chunks_ready"), sem("item_cols_ready")
        s_rv, s_pm, s_tab = sem("routing_step"), sem("routing_matmul"), sem("tables_ready")
        s_cp = sem("sums_copied")
        s_oh, s_ix, s_it, s_id, s_ia, s_gt = (sem(n) for n in (
            "onehot_ready", "slots_summed", "idx_tmp", "gather_idx", "idx_kept", "gate_kept"))
        s_ga = [sem(f"rows_gathered{u}") for u in range(TURN)]
        s_tr, s_xa, s_xd, s_gu, s_si, s_h, s_ht, s_he = (sem(n) for n in (
            "x_tr", "xT_act", "xT_dve", "gate_up", "silu", "h_rows", "h_tr", "hT_ready"))
        s_dn, s_oa, s_od, s_is, s_add, s_turn = (sem(n) for n in (
            "down_done", "out_act", "out_dve", "scatter_idx", "rows_added", "pool_turn"))
        s_gu_in = [sem(f"gate_up_in{i}") for i in range(2)]
        s_dn_in = [sem(f"down_in{i}") for i in range(2)]
        s_rg, s_rd, s_turn_sp = sem("gate_up_landed"), sem("down_landed"), sem("sp_turn")
        s_hg, s_lg, s_lp, s_hd, s_ld, s_hl = (sem(n) for n in (
            "gu_high", "gu_rest", "gu_rest_pool", "down_high", "down_rest", "hT_rest"))
        s_yl = [sem(f"y_in{c}") for c in range(NC)]
        s_sqf, s_rf, s_of, s_ost = sem("sqf"), sem("rstdf"), sem("out_rows"), sem("out_stored")

        x_v = x.rearrange("(c p) d -> c p d", p=P)
        out_v = out.rearrange("(c p) d -> c p d", p=P)
        hn_v = hn_d.rearrange("(c p) d -> c p d", p=P)
        yv = y_d.rearrange("(c p) d -> c p d", p=P)
        spread = lambda ap, n: ap.rearrange("(a n) -> a n", a=1).to_broadcast([P, n])

        def load_gu(eng, e, at):
            eng.dma_start(raw_gu[:, at, 0, :, :], wg[e].rearrange("(p k) f -> p k f", k=KD)).then_inc(s_gu_in[at], 16)
            eng.dma_start(raw_gu[:, at, 1, :, :], wu[e].rearrange("(p k) f -> p k f", k=KD)).then_inc(s_gu_in[at], 16)

        def load_dn(eng, e, at):
            eng.dma_start(raw_dn[:, at, :, :], wd[e].rearrange("(k p) d -> p k d", p=P)).then_inc(s_dn_in[at], 16)

        def gu_part(t, at, m):
            v = t[:, bass.ds(at, 1), m // 2, (m % 2) * 4:(m % 2) * 4 + 4, :]
            return v.rearrange("p a k f -> p (a k) f")

        def item_count(eng, less=0):
            return eng.value_load(ends[0:1, NE + less:NE + less + 1], min_val=NE - less, max_val=NITEM + 1 - less)

        def turns(eng):
            return eng.value_load(ends[0:1, NE + 4:NE + 5], min_val=NE // TURN, max_val=(NITEM + 1) // TURN)

        def look(eng, row, i, top_val):
            return eng.value_load(tab[row:row + 1, bass.ds(i, 1)], min_val=0, max_val=top_val)

        block = ctx.enter_context(nc.Block())

        @block.sync
        def _(sp):
            sp.dma_start(xh[:, 0, :], x_v[0]).then_inc(s_x[0], 16)
            sp.dma_start(g1_row[:, :], spread(g1, D)).then_inc(s_g1, 16)
            sp.dma_start(xh[:, 1, :], x_v[1]).then_inc(s_x[1], 16)
            for k in range(KD):
                sp.dma_start(w_in_sb[:, k, :], w_in.rearrange("(p k) e -> k p e", k=KD)[k]).then_inc(s_wi, 16)
            for c in range(2, NC):
                sp.dma_start(xh[:, c, :], x_v[c]).then_inc(s_x[c], 16)
            for dst, src in ((lng_row[:, :], spread(ln_g, DA)), (lnb_row[:, :], spread(ln_b, DA)),
                             (ga_row[:, :], spread(ga, DA)), (gb_row[:, :], spread(gb, DA)),
                             (g2_row[:, :], spread(g2, D)), (rb_row[:, :], spread(rbias, NE)),
                             (wsp[:, :, :], wsT.rearrange("h q p -> q h p")), (bsp[:, :], bsT),
                             (wr_sb[:, :, :], w_router.rearrange("(p k) e -> p k e", k=KD))):
                sp.dma_start(dst, src).then_inc(s_small, 16)
            sp.dma_start(dpos[:, :, :, :], dft_pos).then_inc(s_dft, 16)
            sp.dma_start(dch[:, :, :, :], dft_ch).then_inc(s_dft, 16)
            sp.wait_ge(s_zb, 8)
            sp.dma_start(w_out_sb[:, :, :], w_out.rearrange("(k p) d -> p k d", p=P)).then_inc(s_wo_in, 16)
            sp.wait_ge(s_v, 8)
            sp.dma_start(sgu_w[:, 0, :, :], sg.rearrange("(p k) f -> p k f", k=KD)).then_inc(s_sh_in, 16)
            sp.dma_start(sgu_w[:, 1, :, :], su.rearrange("(p k) f -> p k f", k=KD)).then_inc(s_sh_in, 16)
            sp.wait_ge(s_y, 8)
            sp.dma_start(sd_w[:, :, :], sd.rearrange("(k p) d -> p k d", p=P)).then_inc(s_sd_in, 16)
            sp.wait_ge(s_ta, 8)
            sp.wait_ge(s_tb, 8)
            for e in range(2):
                load_gu(sp, e, 1 - e)
                load_dn(sp, e, 1 - e)
            for c in range(NC):
                sp.wait_ge(s_hn, c + 1)
                sp.dma_start(hn_v[c], rows[:, c % 2, :]).then_inc(s_hst[c % 2], 16)
            for at, landed in ((1, s_gu_in), (1, s_dn_in)):
                sp.wait_ge(landed[at], 32 if landed is s_gu_in else 16)
            sp.sem_inc(s_rg, 1)
            sp.sem_inc(s_rd, 1)
            for c in range(NC):
                sp.wait_ge(s_y0, c + 1)
                sp.dma_start(yv[c], xh[:, c, :]).then_inc(s_yst, 16)
            sp.dma_start(yv[NC], xh[:, 0, :]).then_inc(s_yst, 16)
            def next_expert(e, at, fills):
                sp.wait_ge(s_hg, (e - 1) * GU_PARTS)
                sp.sem_inc(s_turn_sp, 1)
                sp.wait_ge(s_lg, (e - 1) * (GU_PARTS - 1))
                sp.sem_inc(s_turn_sp, 1)
                sp.wait_ge(s_lp, e - 1)
                sp.sem_inc(s_turn_sp, 1)
                load_gu(sp, e, at)
                landed(1 - at, fills)
                sp.wait_ge(s_hd, (e - 1) * 2)
                sp.sem_inc(s_turn_sp, 1)
                sp.wait_ge(s_ld, (e - 1) * 2)
                sp.sem_inc(s_turn_sp, 1)
                load_dn(sp, e, at)

            def landed(at, fills):
                sp.wait_ge(s_gu_in[at], fills * 32)
                sp.sem_inc(s_rg, 1)
                sp.wait_ge(s_dn_in[at], fills * 16)
                sp.sem_inc(s_rd, 1)

            with sp.Fori(1, NE // 2) as t:
                next_expert(t * 2, 1, t)
                next_expert(t * 2 + 1, 0, t + 1)
            landed(0, NE // 2)
            n = item_count(sp)
            sp.wait_ge(s_add, n * 16)
            sp.sem_inc(s_turn_sp, 1)
            sp.dma_start(gf_row[:, :], spread(gf, D)).then_inc(s_gf, 16)
            for c in range(NC):
                sp.dma_start(xh[:, c, :], yv[c]).then_inc(s_yl[c], 16)
            for c in range(NC):
                sp.wait_ge(s_of, c + 1)
                sp.dma_start(out_v[c], xh[:, c, :]).then_inc(s_ost, 16)
            sp.wait_ge(s_ost, 16 * NC)

        @block.tensor
        def _(pe):
            def turn_rows(src, banks, count=KD):
                for k in range(count):
                    last = pe.transpose(ps[banks[k // 4]][:, (k % 4) * P:(k % 4 + 1) * P], src[:, k:D:KD], ident[:, :])
                return last

            def turn_x(c):
                pe.wait_ge(s_xs, c + 1)
                if c >= 2:
                    pe.wait_ge(s_t1a, c - 1)
                    pe.wait_ge(s_t1d, c - 1)
                turn_rows(rows[:, c % 2, :], (0, 1) if c % 2 == 0 else (6, 7)).then_inc(s_t1, 1)

            def z_a(c):
                pe.wait_ge(s_t1a, c + 1)
                pe.wait_ge(s_t1d, c + 1)
                if c == 0:
                    pe.wait_ge(s_wi, 16 * KD)
                for half in range(2):
                    if c >= 2:
                        pe.wait_ge(s_ge, 2 * (c - 2) + half + 1)
                    for k in range(KD):
                        mm = pe.matmul(ps[2 + 2 * (c % 2) + half][:, :], T[:, k, c * P:(c + 1) * P],
                                       w_in_sb[:, k, half * DA:(half + 1) * DA], start=(k == 0), stop=(k == KD - 1))
                    mm.then_inc(s_za, 1)

            def z_b(g):
                th, et = g // 4, g % 4
                if g < 4:
                    pe.wait_ge(s_ge, 2 * (NC - 2) + g + 1)
                else:
                    pe.wait_ge(s_ze, g - 3)
                for k in range(KD):
                    mm = pe.matmul(ps[2 + g % 4][:, :], w_in_sb[:, k, 2 * DA + et * P:2 * DA + (et + 1) * P],
                                   T[:, k, th * 512:(th + 1) * 512], start=(k == 0), stop=(k == KD - 1))
                mm.then_inc(s_zb, 1)

            pe.wait_ge(s_cst, 1)
            turn_x(0)
            for c in range(NC):
                if c + 1 < NC:
                    turn_x(c + 1)
                z_a(c)
            for g in range(4):
                z_b(g)

            free4 = (0, 1, 6, 7)
            pe.wait_ge(s_vp, 2 * NC)
            pe.wait_ge(s_small, 16 * 9)
            for h in range(NH):
                if h >= 4:
                    pe.wait_ge(s_ya, h - 3)
                pe.matmul(ps[free4[h % 4]][:, :], wsp[:, h, :], v_sb[:, :, h * HD:(h + 1) * HD],
                          start=True, stop=True).then_inc(s_sg, 1)
            for g in range(4, 8):
                z_b(g)
            pe.wait_ge(s_ya, NH)
            for c in range(NC):
                pe.wait_ge(s_yn, c + 1)
                if c >= 4:
                    pe.wait_ge(s_tae, c - 3)
                for k in range(4):
                    tr = pe.transpose(ps[free4[c % 4]][:, k * P:(k + 1) * P], u_sb[:, c, k * P:(k + 1) * P], ident[:, :])
                tr.then_inc(s_ta, 1)

            terms = {0: [(0, 0)], 4: [(1, 0)], 1: [(2, 0), (3, 2)], 7: [(2, 0), (3, 1)], 2: [(4, 0), (5, 2)],
                     6: [(4, 0), (5, 1)], 3: [(6, 0), (7, 1)], 5: [(6, 0), (7, 2)]}

            def chan(s0):
                if s0 < 2:
                    pe.wait_ge(s_ze, 8)
                    pe.wait_ge(s_bf, BUTTERFLY)
                    pe.wait_ge(s_dft, 32)
                else:
                    pe.wait_ge(s_va, s0 - 1)
                    pe.wait_ge(s_vd, s0 - 1)
                for pair in range(4):
                    bank = ps[2 + 2 * (s0 % 2) + pair // 2]
                    for n, (a, m) in enumerate(terms[s0]):
                        mm = pe.matmul(bank[:, (pair % 2) * 256:(pair % 2 + 1) * 256], U[:, a, pair, :],
                                       dch[:, m, :, :], start=(n == 0), stop=(n == len(terms[s0]) - 1))
                mm.then_inc(s_v, 1)

            def posn(s0):
                pe.wait_ge(s_va, s0 + 1)
                pe.wait_ge(s_vd, s0 + 1)
                if s0 < 2:
                    pe.wait_ge(s_tae, NC)
                else:
                    pe.wait_ge(s_yb, s0 - 1)
                for ri in range(2):
                    mm = pe.matmul(ps[s0 % 2][:, :], dpos[:, ri, s0, :], V[:, s0 % 2, :, ri, :],
                                   start=(ri == 0), stop=(ri == 1))
                mm.then_inc(s_y, 1)

            def turn_b(s0):
                pe.wait_ge(s_yb, s0 + 1)
                if s0 >= 2:
                    pe.wait_ge(s_tbe, s0 - 1)
                for k in range(4):
                    tr = pe.transpose(ps[6 + s0 % 2][:, k * P:(k + 1) * P], yb[:, s0, k * P:(k + 1) * P], ident[:, :])
                tr.then_inc(s_tb, 1)

            for s0 in range(NC + 2):
                if s0 < NC:
                    chan(s0)
                if 1 <= s0 <= NC:
                    posn(s0 - 1)
                if s0 >= 2:
                    turn_b(s0 - 2)

            def w_o(c):
                if c == 0:
                    pe.wait_ge(s_wo_in, 16)
                    pe.wait_ge(s_tbe, NC)
                    pe.wait_ge(s_yb, NC)
                if c >= 2:
                    pe.wait_ge(s_hx, 2 * (c - 1))
                for half in range(2):
                    for k in range(KD):
                        mm = pe.matmul(ps[2 * (c % 2) + half][:, :], T[:, k, c * P:(c + 1) * P],
                                       w_out_sb[:, k, half * 512:(half + 1) * 512], start=(k == 0), stop=(k == KD - 1))
                mm.then_inc(s_wo, 1)

            def turn_hn(c):
                pe.wait_ge(s_hn, c + 1)
                if c >= 1:
                    pe.wait_ge(s_t3a, c)
                    pe.wait_ge(s_t3d, c)
                turn_rows(rows[:, c % 2, :], (4, 5)).then_inc(s_t3, 1)

            def router(c):
                pe.wait_ge(s_t3a, c + 1)
                pe.wait_ge(s_t3d, c + 1)
                if c >= 2:
                    pe.wait_ge(s_sc, c - 1)
                for k in range(KD):
                    mm = pe.matmul(ps[6 + c % 2][:, 0:NE], T[:, k, c * P:(c + 1) * P], wr_sb[:, k, :],
                                   start=(k == 0), stop=(k == KD - 1))
                mm.then_inc(s_rt, 1)

            for c in range(NC + 2):
                if c < NC:
                    w_o(c)
                if 1 <= c <= NC:
                    turn_hn(c - 1)
                if c >= 2:
                    router(c - 2)

            pe.wait_ge(s_sh_in, 32)
            pe.wait_ge(s_hx, 2 * NC)
            for q in range(4):
                th, ft = q // 2, q % 2
                if q >= 2:
                    pe.wait_ge(s_hm, q - 1)
                for j in range(2):
                    for k in range(KD):
                        mm = pe.matmul(ps[2 * (q % 2) + j][:, :], sgu_w[:, j, k, ft * P:(ft + 1) * P],
                                       T[:, k, th * 512:(th + 1) * 512], start=(k == 0), stop=(k == KD - 1))
                mm.then_inc(s_q, 1)
            pe.wait_ge(s_hm, 4)
            pe.wait_ge(s_mask, 1)
            flat = mask[:, :, :].rearrange("p c e -> p (c e)")
            pe.matmul(ps[0][:, :], tri[:, :], flat, start=True, stop=True)
            for d in range(1, NC):
                mm = pe.matmul(ps[0][:, d * NE:], ones[:, :], flat[:, 0:(NC - d) * NE], start=False, stop=True,
                               skip_group_check=True)
            for c in range(NC):
                mm = pe.matmul(ps[1][0:NE, 0:1], mask[:, c, :], ones[:, 0:1], start=(c == 0), stop=(c == NC - 1))
            mm.then_inc(s_pm, 1)

            def s_down(c):
                if c >= 2:
                    pe.wait_ge(s_y0, c - 1)
                if c == 0:
                    pe.wait_ge(s_sd_in, 16)
                    pe.wait_ge(s_sc, NC)
                    pe.wait_ge(s_t3a, NC)
                    pe.wait_ge(s_t3d, NC)
                for half in range(2):
                    for k in range(KF):
                        mm = pe.matmul(ps[4 + 2 * (c % 2) + half][:, :], hsT[:, k, c * P:(c + 1) * P],
                                       sd_w[:, k, half * 512:(half + 1) * 512], start=(k == 0), stop=(k == KF - 1))
                mm.then_inc(s_sdn, 1)

            for c in range(4):
                s_down(c)
            pe.wait_ge(s_chunks, 1)
            pe.matmul(ps[2][:, 0:NE], nchb[:, :], triI[:, :], start=True, stop=True).then_inc(s_pm, 1)
            for c in range(4, NC):
                s_down(c)
            pe.wait_ge(s_cols, 1)
            pe.matmul(ps[3][0:4, 0:P], cols[:, 0:4], ident[:, :], start=True, stop=True).then_inc(s_pm, 1)

            def slot_sums(i):
                e = look(pe, 0, i, NE - 1)
                pe.wait_ge(s_oh, i + 1)
                after(pe, s_cp, i)
                for c in range(NC):
                    mm = pe.matmul(ps[0][:, 0:5], onehot[:, c, :], info[:, c, bass.ds(e, 1), :],
                                   start=(c == 0), stop=(c == NC - 1))
                mm.then_inc(s_ix, 1)

            def turn_item(u, fills):
                pe.wait_ge(s_ga[u], 16 * fills)
                turn_rows(Xg[:, u, :], (1, 2)).then_inc(s_tr, 1)

            def gate_up(i):
                e = look(pe, 0, i, NE - 1)
                at = look(pe, 2, i, 1)
                pe.wait_ge(s_hg, (e + 1) * GU_PARTS)
                pe.wait_ge(s_lg, (e + 1) * (GU_PARTS - 1))
                pe.wait_ge(s_lp, e + 1)
                pe.wait_ge(s_xd, 2 * i + 2)
                for k in range(KD):
                    for x_, part in ((xTh, 0), (xTh, 1), (xTl, 0)):
                        mm = pe.matmul(ps[3][:, :], x_[:, k, :], w_gu[:, bass.ds(at, 1), part, :, k, :],
                                       start=(k == 0 and part == 0 and x_ is xTh), stop=(k == KD - 1 and x_ is xTl))
                mm.then_inc(s_gu, 1)

            def down(i, first=False):
                e = look(pe, 0, i, NE - 1)
                at = look(pe, 2, i, 1)
                pe.wait_ge(s_hd, (e + 1) * 2)
                pe.wait_ge(s_ld, (e + 1) * 2)
                pe.wait_ge(s_hl, i + 1)
                if not first:
                    pe.wait_ge(s_oa, i)
                for half in range(2):
                    for k in range(KF):
                        for h_, part in ((hTh, 0), (hTh, 1), (hTl, 0)):
                            mm = pe.matmul(ps[6 + half][:, :], h_[:, k, :],
                                           w_dn[:, bass.ds(at, 1), part, k, half * 512:(half + 1) * 512],
                                           start=(k == 0 and part == 0 and h_ is hTh), stop=(k == KF - 1 and h_ is hTl))
                mm.then_inc(s_dn, 1)

            def turn_h(i):
                pe.wait_ge(s_h, i + 1)
                for k in range(KF):
                    tr = pe.transpose(ps[5][:, k * P:(k + 1) * P], hh[:, k * P:(k + 1) * P], ident[:, :])
                tr.then_inc(s_ht, 1)

            def item(i, u, turn, first=0):
                gate_up(i)
                turn_item((u + 1) % TURN, turn + 1 if u + 1 < TURN else turn + 2)
                if first != 1:
                    down(i - 1, first == 2)
                turn_h(i)
                slot_sums(i + TURN)

            pe.wait_ge(s_tab, 1)
            pe.wait_ge(s_y0, NC)
            for i in range(TURN):
                slot_sums(i)
            turn_item(0, 1)
            for i in range(TURN):
                item(i, i, 0, i + 1)
            last = item_count(pe, 1)
            with pe.Fori(1, turns(pe)) as t:
                for u in range(TURN):
                    item(t * TURN + u, u, t)
            down(last)

        @block.scalar
        def _(act):
            def square(src, scale, norm, c, done):
                act.activation(junk[:, 0:src.shape[-1]], src, ACT.Square, scale=scale,
                               accum_out=ms[:, norm, c:c + 1]).then_inc(done, 1)

            def sq1(c):
                act.wait_ge(s_x[c], 16)
                if c:
                    act.wait_ge(s_sq, c)
                square(xh[:, c, :], D ** -0.5, 0, c, s_sq)

            def evac_x(c):
                act.wait_ge(s_t1, c + 1)
                act.activation(T[:, 0:4, c * P:(c + 1) * P], ps[0 if c % 2 == 0 else 6][:, :].rearrange(
                    "p (k t) -> p k t", k=4), ACT.Copy).then_inc(s_t1a, 1)

            def gelu(c):
                for half, dst in enumerate((u_sb, v_sb)):
                    act.wait_ge(s_za, 2 * c + half + 1)
                    act.activation(dst[:, c, :], ps[2 + 2 * (c % 2) + half][:, :], ACT.Gelu).then_inc(s_ge, 1)

            sq1(0)
            sq1(1)
            for c in range(NC):
                evac_x(c)
                if c + 2 < NC:
                    sq1(c + 2)
                if c >= 1:
                    gelu(c - 1)
            gelu(NC - 1)

            def evac_z(g):
                act.wait_ge(s_zb, g + 1)
                act.activation(zT[:, g % 4, (g // 4) * 512:(g // 4 + 1) * 512], ps[2 + g % 4][:, :],
                               ACT.Copy).then_inc(s_ze, 1)

            for g in range(4):
                evac_z(g)
            act.wait_ge(s_sq, NC)
            act.wait_ge(s_ya, NH)
            for c in range(NC):
                if c:
                    act.wait_ge(s_sqa, c)
                square(u_sb[:, c, :], DA ** -0.5, 1, c, s_sqa)
            for g in range(4, 8):
                evac_z(g)
            for c in range(NC):
                act.wait_ge(s_ta, c + 1)
                act.activation(T[:, 0:4, c * P:(c + 1) * P], ps[(0, 1, 6, 7)[c % 4]][:, :].rearrange(
                    "p (k t) -> p k t", k=4), ACT.Copy).then_inc(s_tae, 1)
            for s0 in range(NC + 2):
                if s0 < NC:
                    act.wait_ge(s_v, s0 + 1)
                    if s0 >= 2:
                        act.wait_ge(s_y, s0 - 1)
                    act.activation(V[:, s0 % 2, 0:2, :, :], ps[2 + 2 * (s0 % 2)][:, :].rearrange(
                        "p (r i q) -> p r i q", r=2, i=2), ACT.Copy).then_inc(s_va, 1)
                if 1 <= s0 <= NC:
                    act.wait_ge(s_y, s0)
                    if s0 == 1:
                        act.wait_ge(s_sqa, NC)
                    else:
                        act.wait_ge(s_sqb, s0 - 1)
                    square(ps[(s0 - 1) % 2][:, :], DA ** -0.5, 2, s0 - 1, s_sqb)
                if s0 >= 2:
                    act.wait_ge(s_tb, s0 - 1)
                    act.activation(T[:, 4:8, s0 - 2:S:NC], ps[6 + s0 % 2][:, :].rearrange(
                        "p (k t) -> p k t", k=4), ACT.Copy).then_inc(s_tbe, 1)

            for c in range(NC + 2):
                if c < NC:
                    act.wait_ge(s_hx, 2 * c + 2)
                    if c == 0:
                        act.wait_ge(s_sqb, NC)
                    else:
                        act.wait_ge(s_sq2, c)
                    square(xh[:, c, :], D ** -0.5, 3, c, s_sq2)
                if 1 <= c <= NC:
                    act.wait_ge(s_t3, c)
                    act.activation(T[:, 0:4, (c - 1) * P:c * P], ps[4][:, :].rearrange(
                        "p (k t) -> p k t", k=4), ACT.Copy).then_inc(s_t3a, 1)
                if c >= 2:
                    act.wait_ge(s_rt, c - 1)
                    act.activation(scores[:, c - 2, :], ps[6 + c % 2][:, 0:NE], ACT.Sigmoid).then_inc(s_sc, 1)

            for q in range(4):
                act.wait_ge(s_q, q + 1)
                if q >= 2:
                    act.wait_ge(s_hm, q - 1)
                act.activation(s_tmp[:, q % 2, :], ps[2 * (q % 2)][:, :], ACT.Silu).then_inc(s_ssi, 1)

            def split_gu(at):
                for m in range(GU_PARTS):
                    act.activation(gu_part(w_gu[:, :, 0, :, :, :], at, m), gu_part(raw_gu, at, m), ACT.Copy).then_inc(s_hg, 1)

            def split_dn(at):
                for k in range(KF):
                    act.activation(w_dn[:, bass.ds(at, 1), 0, k, :], raw_dn[:, bass.ds(at, 1), k, :],
                                   ACT.Copy).then_inc(s_hd, 1)

            def silu(i):
                act.wait_ge(s_gu, i + 1)
                after(act, s_h, i)
                act.activation(hs[:, :], ps[3][:, 0:F], ACT.Silu).then_inc(s_si, 1)

            def evac_xT(i):
                act.wait_ge(s_tr, i + 1)
                for half in range(2):
                    act.activation(xTh[:, half * 4:half * 4 + 4, :], ps[1 + half][:, :].rearrange(
                        "p (k t) -> p k t", k=4), ACT.Copy).then_inc(s_xa, 1)

            def evac_out(i, u, before=None):
                act.wait_ge(s_dn, i + 1)
                after(act, s_add, 16 * (i - 2 if before is None else before))
                act.activation(ob[:, u, 0:512], ps[6][:, :], ACT.Copy)
                act.activation(ob[:, u, 512:1024], ps[7][:, :], ACT.Copy).then_inc(s_oa, 1)

            def evac_h(i):
                act.wait_ge(s_ht, i + 1)
                act.activation(hTh[:, :, :], ps[5][:, 0:KF * P].rearrange("p (k t) -> p k t", k=KF),
                               ACT.Copy).then_inc(s_he, 1)

            def item(i, u):
                if isinstance(i, int) and i == 0:
                    split_dn(1)
                else:
                    with act.If(look(act, 3, i, 1) > 0):
                        e = look(act, 0, i, NE - 1)
                        at = look(act, 2, i, 1)
                        act.wait_ge(s_rd, e + 1)
                        split_dn(at)
                with act.If(look(act, 3, i + 1, 1) > 0):
                    e = look(act, 0, i + 1, NE - 1)
                    at = look(act, 2, i + 1, 1)
                    act.wait_ge(s_rg, e + 1)
                    split_gu(at)
                silu(i)
                evac_xT(i + 1)
                evac_h(i)
                evac_out(i - 1, (u - 1) % TURN) if not (isinstance(i, int) and i == 0) else None

            act.wait_ge(s_rg, 1)
            split_gu(1)
            act.wait_ge(s_tab, 1)
            act.wait_ge(s_rd, 1)
            act.wait_ge(s_yst, 16 * (NC + 1))
            evac_xT(0)
            for i in range(TURN):
                item(i, i)
            last, before = item_count(act, 1), item_count(act, 3)
            with act.Fori(1, turns(act)) as t:
                for u in range(TURN):
                    item(t * TURN + u, u)
            evac_out(last, TURN - 1, before)

            for c in range(NC):
                act.wait_ge(s_yl[c], 16)
                act.wait_ge(s_sq2, NC) if c == 0 else act.wait_ge(s_sqf, c)
                square(xh[:, c, :], D ** -0.5, 4, c, s_sqf)

        @block.vector
        def _(dv):
            def norm_x(c):
                dv.wait_ge(s_r1, c + 1)
                if c >= 2:
                    dv.wait_ge(s_t1, c - 1)
                if c == 0:
                    dv.wait_ge(s_g1, 16)
                dv.scalar_tensor_tensor(out=rows[:, c % 2, :], in0=xh[:, c, :], scalar=rs[:, 0, c:c + 1],
                                        in1=g1_row[:, :], op0=ALU.mult, op1=ALU.mult).then_inc(s_xs, 1)

            def evac_x(c):
                dv.wait_ge(s_t1, c + 1)
                dv.tensor_copy(T[:, 4:8, c * P:(c + 1) * P], ps[1 if c % 2 == 0 else 7][:, :].rearrange(
                    "p (k t) -> p k t", k=4)).then_inc(s_t1d, 1)

            def norm_v(c):
                dv.wait_ge(s_ge, 2 * c + 2)
                dv.bn_stats(bst[:, c, :], v_sb[:, c, :]).then_inc(s_ln, 1)
                dv.wait_ge(s_ln, 3 * c + 1)
                dv.bn_aggr(bag[:, c, :], bst[:, c, :]).then_inc(s_ln, 1)
                dv.wait_ge(s_lr, c + 1)
                dv.tensor_scalar(v_sb[:, c, :], v_sb[:, c, :], bag[:, c, 0:1], vr[:, c:c + 1], ALU.subtract,
                                 ALU.mult).then_inc(s_ln, 1)

            norm_x(0)
            norm_x(1)
            for c in range(NC):
                evac_x(c)
                if c + 2 < NC:
                    norm_x(c + 2)
                if c >= 1:
                    norm_v(c - 1)
            norm_v(NC - 1)

            dv.wait_ge(s_small, 16 * 9)
            for h in range(NH):
                dv.wait_ge(s_sg, h + 1)
                heads = u_sb[:, :, h * HD:(h + 1) * HD]
                dv.scalar_tensor_tensor(out=heads, in0=ps[(0, 1, 6, 7)[h % 4]][:, :].rearrange(
                    "p (c d) -> p c d", c=NC), scalar=bsp[:, h:h + 1], in1=heads, op0=ALU.add,
                    op1=ALU.mult).then_inc(s_ya, 1)
            for c in range(NC):
                dv.wait_ge(s_ra, c + 1)
                dv.scalar_tensor_tensor(out=u_sb[:, c, :], in0=u_sb[:, c, :], scalar=rs[:, 1, c:c + 1],
                                        in1=ga_row[:, :], op0=ALU.mult, op1=ALU.mult).then_inc(s_yn, 1)

            dv.wait_ge(s_ze, 8)
            steps = [0]

            def fly(ins):
                steps[0] += 1
                ins.then_inc(s_bf, 1)
                dv.wait_ge(s_bf, steps[0])

            a, b = ab[:, 0, :, :], ab[:, 1, :, :]
            pair4 = lambda t: t.rearrange("p r (a q) -> p a r q", q=P)
            fly(dv.tensor_tensor(a, zT[:, :, 0:512], zT[:, :, 512:1024], ALU.add))
            fly(dv.tensor_tensor(b, zT[:, :, 0:512], zT[:, :, 512:1024], ALU.subtract))
            fly(dv.tensor_tensor(U[:, 4:6, :, :], pair4(a[:, :, 0:256]), pair4(a[:, :, 256:512]), ALU.subtract))
            fly(dv.tensor_tensor(U[:, 6:8, :, :], pair4(a[:, :, 0:256]), pair4(a[:, :, 256:512]), ALU.add))
            fly(dv.tensor_tensor(U[:, 0, :, :], U[:, 6, :, :], U[:, 7, :, :], ALU.add))
            fly(dv.tensor_tensor(U[:, 1, :, :], U[:, 6, :, :], U[:, 7, :, :], ALU.subtract))
            dif, tot = a[:, :, 0:128], a[:, :, 128:256]
            fly(dv.tensor_tensor(dif, b[:, :, 128:256], b[:, :, 384:512], ALU.subtract))
            fly(dv.tensor_tensor(tot, b[:, :, 128:256], b[:, :, 384:512], ALU.add))
            for j, r in ((2, R8), (6, -R8)):
                fly(dv.scalar_tensor_tensor(out=U[:, j, :, :], in0=dif, scalar=r, in1=b[:, :, 0:128], op0=ALU.mult,
                                            op1=ALU.add))
                fly(dv.scalar_tensor_tensor(out=U[:, j + 1, :, :], in0=tot, scalar=r, in1=b[:, :, 256:384],
                                            op0=ALU.mult, op1=ALU.add))
            assert steps[0] == BUTTERFLY

            for s0 in range(NC + 1):
                if s0 < NC:
                    dv.wait_ge(s_v, s0 + 1)
                    if s0 >= 2:
                        dv.wait_ge(s_y, s0 - 1)
                    dv.tensor_copy(V[:, s0 % 2, 2:4, :, :], ps[3 + 2 * (s0 % 2)][:, :].rearrange(
                        "p (r i q) -> p r i q", r=2, i=2)).then_inc(s_vd, 1)
                if s0 >= 1:
                    dv.wait_ge(s_rb, s0)
                    dv.scalar_tensor_tensor(out=yb[:, s0 - 1, :], in0=ps[(s0 - 1) % 2][:, :],
                                            scalar=rs[:, 2, s0 - 1:s0], in1=gb_row[:, :], op0=ALU.mult,
                                            op1=ALU.mult).then_inc(s_yb, 1)

            for c in range(NC + 1):
                if c < NC:
                    dv.wait_ge(s_wo, c + 1)
                    for half in range(2):
                        piece = xh[:, c, half * 512:(half + 1) * 512]
                        dv.tensor_tensor(piece, ps[2 * (c % 2) + half][:, :], piece, ALU.add).then_inc(s_hx, 1)
                if c >= 1:
                    dv.wait_ge(s_t3, c)
                    dv.tensor_copy(T[:, 4:8, (c - 1) * P:c * P], ps[5][:, :].rearrange(
                        "p (k t) -> p k t", k=4)).then_inc(s_t3d, 1)
                if c < NC:
                    dv.wait_ge(s_r2, c + 1)
                    if c >= 2:
                        dv.wait_ge(s_t3, c - 1)
                        dv.wait_ge(s_hst[c % 2], 16 * (c // 2))
                    dv.scalar_tensor_tensor(out=rows[:, c % 2, :], in0=xh[:, c, :], scalar=rs[:, 3, c:c + 1],
                                            in1=g2_row[:, :], op0=ALU.mult, op1=ALU.mult).then_inc(s_hn, 1)

            count = [0]

            def step(ins):
                count[0] += 1
                ins.then_inc(s_rv, 1)
                dv.wait_ge(s_rv, count[0])

            def many(instructions):
                for ins in instructions:
                    count[0] += 1
                    ins.then_inc(s_rv, 1)
                dv.wait_ge(s_rv, count[0])

            def shared_h(q):
                dv.wait_ge(s_ssi, q + 1)
                dv.tensor_tensor(hsT[:, q % 2, (q // 2) * 512:(q // 2 + 1) * 512], s_tmp[:, q % 2, :],
                                 ps[2 * (q % 2) + 1][:, :], ALU.mult).then_inc(s_hm, 1)

            def rest_gu(at, e):
                for m in range(GU_PARTS - 1):
                    dv.wait_ge(s_hg, e * GU_PARTS + m + 1)
                    dv.tensor_tensor(gu_part(w_gu[:, :, 1, :, :, :], at, m), gu_part(raw_gu, at, m),
                                     gu_part(w_gu[:, :, 0, :, :, :], at, m).bitcast(F32), ALU.subtract).then_inc(s_lg, 1)

            def rest_dn(at, e):
                for k in range(KF):
                    dv.wait_ge(s_hd, e * KF + k + 1)
                    dv.tensor_tensor(w_dn[:, bass.ds(at, 1), 1, k, :], raw_dn[:, bass.ds(at, 1), k, :],
                                     w_dn[:, bass.ds(at, 1), 0, k, :].bitcast(F32), ALU.subtract).then_inc(s_ld, 1)

            dv.wait_ge(s_cst, 1)
            dv.wait_ge(s_sc, NC)
            wide = [P, NC, NE]
            step(dv.tensor_tensor(rt_a[:, :, :], scores[:, :, :], rb_row[:, None, :].to_broadcast(wide), ALU.add))
            many(dv.max(m8[:, c, g, :], rt_a[:, c, g * GE:(g + 1) * GE]) for c in range(NC) for g in range(NG))
            step(dv.tensor_tensor(gs[:, :, :], m8[:, :, :, 0], m8[:, :, :, 1], ALU.add))
            many(dv.max(gtop[:, c, :], gs[:, c, :]) for c in range(NC))
            many(dv.max_index(gidx[:, c, :], gtop[:, c, :], gs[:, c, :]) for c in range(NC))
            step(dv.tensor_copy(gidxf[:, :, :], gidx[:, :, 0:TOPG]))
            step(dv.tensor_tensor(geq[:, :, :, :], gidxf[:, :, None, :].to_broadcast([P, NC, NG, TOPG]),
                                  gi[:, None, :, None].to_broadcast([P, NC, NG, TOPG]), ALU.is_equal))
            step(dv.tensor_reduce(gm[:, :, :], geq[:, :, :, :], AX.X, ALU.max))
            step(dv.tensor_scalar(gs[:, :, :], gm[:, :, :], 1.0, BIG, ALU.subtract, ALU.mult))
            by_group = lambda t: t[:, :, :].rearrange("p c (g e) -> p c g e", g=NG)
            step(dv.tensor_tensor(by_group(rt_b), by_group(rt_a), gs[:, :, :, None].to_broadcast([P, NC, NG, GE]),
                                  ALU.add))
            many(dv.max(etop[:, c, :], rt_b[:, c, :]) for c in range(NC))
            many(dv.match_replace(rt_a[:, c, :], etop[:, c, :], rt_b[:, c, :], -3.3e38) for c in range(NC))
            dv.wait_ge(s_hst[0], 16 * 4)
            dv.wait_ge(s_hst[1], 16 * 4)
            dv.wait_ge(s_t3, NC)
            shared_h(0)
            step(dv.tensor_tensor(mask[:, :, :], rt_a[:, :, :], rt_b[:, :, :], ALU.not_equal))
            dv.sem_inc(s_mask, 1)
            step(dv.tensor_tensor(rt_a[:, :, :], scores[:, :, :], mask[:, :, :], ALU.mult))
            step(dv.tensor_reduce(gsum[:, :], rt_a[:, :, :], AX.X, ALU.add))
            step(dv.reciprocal(grec[:, :], gsum[:, :]))
            step(dv.tensor_scalar(grec[:, :], grec[:, :], RSCALE, None, ALU.mult))
            step(dv.tensor_tensor(rt_a[:, :, :], rt_a[:, :, :], grec[:, :, None].to_broadcast(wide), ALU.mult))
            shared_h(1)
            dv.wait_ge(s_info, 3)
            step(dv.tensor_copy(info[:, :, :, 2], rt_a[:, :, :]))
            step(dv.tensor_tensor(rt_b[:, :, :], rt_a[:, :, :], info[:, :, :, 2], ALU.subtract))
            step(dv.tensor_copy(info[:, :, :, 3], rt_b[:, :, :]))
            step(dv.tensor_tensor(rt_a[:, :, :], rt_b[:, :, :], info[:, :, :, 3], ALU.subtract))
            step(dv.tensor_copy(info[:, :, :, 4], rt_a[:, :, :]))
            shared_h(2)
            shared_h(3)
            rest_gu(1, 0)
            dv.wait_ge(s_pm, 1)
            step(dv.scalar_tensor_tensor(out=rt_b[:, :, :], in0=ps[0][:, :].rearrange("p (c e) -> p c e", c=NC),
                                         scalar=1.0, in1=mask[:, :, :], op0=ALU.add, op1=ALU.mult))
            step(dv.tensor_scalar(pos[:, :, :], rt_b[:, :, :], -1.0, None, ALU.add))
            for j in range(1, MAXCH):
                step(dv.scalar_tensor_tensor(out=nch[:, j:j + 1], in0=ps[1][0:NE, 0:1], scalar=float(P * j),
                                             in1=nch[:, j - 1:j], op0=ALU.is_gt, op1=ALU.add))
            step(dv.tensor_copy(nchb[:, :], nch[:, MAXCH - 1:MAXCH].to_broadcast([NE, P])))
            dv.sem_inc(s_chunks, 1)

            def y0(c):
                dv.wait_ge(s_sdn, c + 1)
                for half in range(2):
                    piece = xh[:, c, half * 512:(half + 1) * 512]
                    ins = dv.tensor_tensor(piece, ps[4 + 2 * (c % 2) + half][:, :], piece, ALU.add)
                ins.then_inc(s_y0, 1)

            for c in range(4):
                y0(c)
            dv.wait_ge(s_pm, 2)
            step(dv.tensor_copy(le[:, 2, :], ps[2][:, 0:NE]))
            step(dv.tensor_scalar(le[:, 0, :], le[:, 2, :], pidx[:, 0:1], None, ALU.is_le))
            step(dv.tensor_tensor(le[:, 1, :], le[:, 0, :], le[:, 2, :], ALU.mult))
            step(dv.tensor_reduce(cols[:, 8:9], le[:, 0, :], AX.X, ALU.add))
            step(dv.tensor_reduce(cols[:, 4:5], le[:, 1, :], AX.X, ALU.max))
            step(dv.tensor_scalar(cols[:, 0:1], cols[:, 8:9], float(NE - 1), None, ALU.min))
            step(dv.tensor_scalar(halves[:, :], cols[:, 0:1], 0.5, 0.5, ALU.add, ALU.mult))
            step(dv.tensor_scalar(cols[:, 9:10], halves[:, :], -2.0, 1.0, ALU.mult, ALU.add))
            step(dv.tensor_tensor(cols[:, 2:3], cols[:, 9:10], cols[:, 0:1], ALU.add))
            step(dv.tensor_scalar(cols[:, 5:6], cols[:, 4:5], pidx[:, 0:1], float(P), ALU.subtract, ALU.mult))
            step(dv.tensor_scalar(cols[:, 6:7], cols[:, 8:9], float(NE), -float(S), ALU.is_ge, ALU.mult))
            step(dv.tensor_tensor(cols[:, 7:8], cols[:, 5:6], cols[:, 6:7], ALU.add))
            step(dv.tensor_scalar(cols[:, 1:2], cols[:, 7:8], float(S), 0.0, ALU.add, ALU.max))
            step(dv.tensor_scalar(cols[:, 10:11], cols[:, 4:5], pidx[:, 0:1], None, ALU.is_equal))
            step(dv.tensor_scalar(cols[:, 11:12], cols[:, 8:9], float(NE), None, ALU.is_lt))
            step(dv.tensor_tensor(cols[:, 3:4], cols[:, 10:11], cols[:, 11:12], ALU.mult))
            dv.sem_inc(s_cols, 1)
            for c in range(4, NC):
                y0(c)
            step(dv.tensor_copy(ends[0:1, 0:NE], ps[2][0:1, 0:NE]))
            step(dv.tensor_scalar(ends[0:1, NE + 4:NE + 5], ps[2][0:1, NE - 1:NE], 1.0, 1.0 / TURN, ALU.add, ALU.mult))
            for less in range(TURN + 1):
                step(dv.tensor_scalar(ends[0:1, NE + less:NE + less + 1], ends[0:1, NE + 4:NE + 5], float(TURN),
                                      float(less), ALU.mult, ALU.subtract))
            dv.wait_ge(s_pm, 3)
            dv.tensor_copy(tab[0:4, 0:P], ps[3][0:4, 0:P]).then_inc(s_tab, 1)

            def one_hot(i):
                e = look(dv, 0, i, NE - 1)
                back = look(dv, 1, i, S)
                shape = [P, NC, P]
                after(dv, s_ix, i)
                dv.tensor_tensor(onehot[:, :, :], pos[:, :, bass.ds(e, 1)].to_broadcast(shape),
                                 slots[:, None, bass.ds(S - back, P)].to_broadcast(shape),
                                 ALU.is_equal).then_inc(s_oh, 1)

            def indices(i, u):
                dv.wait_ge(s_ix, i + 1)
                after(dv, s_ia, i)
                after(dv, s_gt, i)
                dv.tensor_copy(sumf[:, 0:5], ps[0][:, 0:5]).then_inc(s_cp, 1)
                dv.wait_ge(s_cp, i + 1)
                dv.scalar_tensor_tensor(out=idxf[:, :], in0=sumf[:, 0:1], scalar=EMPTY, in1=sumf[:, 1:2],
                                        op0=ALU.add, op1=ALU.add).then_inc(s_it, 1)
                dv.scalar_tensor_tensor(out=gate_all[:, bass.ds(i, 1)], in0=sumf[:, 2:3], scalar=sumf[:, 3:4],
                                        in1=sumf[:, 4:5], op0=ALU.add, op1=ALU.add).then_inc(s_gt, 1)
                dv.wait_ge(s_it, i + 1)
                dv.tensor_scalar(idxg[:, u:u + 1], idxf[:, :], dump[:, 0:1], None, ALU.min).then_inc(s_id, 1)
                dv.tensor_scalar(idx_all[:, bass.ds(i, 1)], idxf[:, :], dump[:, 0:1], None, ALU.min).then_inc(s_ia, 1)

            def gated_h(i):
                dv.wait_ge(s_si, i + 1)
                dv.wait_ge(s_gt, i + 1)
                after(dv, s_ht, i)
                dv.scalar_tensor_tensor(out=hh[:, :], in0=hs[:, :], scalar=gate_all[:, bass.ds(i, 1)],
                                        in1=ps[3][:, F:2 * F], op0=ALU.mult, op1=ALU.mult).then_inc(s_h, 1)

            def rest_xT(i):
                for half in range(2):
                    dv.wait_ge(s_xa, 2 * i + half + 1)
                    part = slice(half * 4, half * 4 + 4)
                    dv.tensor_tensor(xTl[:, part, :], ps[1 + half][:, :].rearrange("p (k t) -> p k t", k=4),
                                     xTh[:, part, :].bitcast(F32), ALU.subtract).then_inc(s_xd, 1)

            def rest_h(i):
                dv.wait_ge(s_he, i + 1)
                dv.tensor_tensor(hTl[:, :, :], ps[5][:, 0:KF * P].rearrange("p (k t) -> p k t", k=KF),
                                 hTh[:, :, :].bitcast(F32), ALU.subtract).then_inc(s_hl, 1)

            def scatter_idx(i, u, before=None):
                dv.wait_ge(s_ia, i + 1)
                after(dv, s_add, 16 * (i - 2 if before is None else before))
                dv.tensor_scalar(idxs[:, u:u + 1], idx_all[:, bass.ds(i, 1)], 0.0, None, ALU.add).then_inc(s_is, 1)

            def item(i, u):
                first = isinstance(i, int) and i == 0
                one_hot(i + TURN)
                if first:
                    rest_dn(1, 0)
                else:
                    with dv.If(look(dv, 3, i, 1) > 0):
                        e = look(dv, 0, i, NE - 1)
                        rest_dn(look(dv, 2, i, 1), e)
                with dv.If(look(dv, 3, i + 1, 1) > 0):
                    e = look(dv, 0, i + 1, NE - 1)
                    rest_gu(look(dv, 2, i + 1, 1), e)
                gated_h(i)
                rest_xT(i + 1)
                rest_h(i)
                indices(i + TURN, u)
                if not first:
                    scatter_idx(i - 1, (u - 1) % TURN)

            dv.wait_ge(s_tab, 1)
            for i in range(TURN):
                one_hot(i)
                indices(i, i)
            rest_xT(0)
            for i in range(TURN):
                item(i, i)
            last, before = item_count(dv, 1), item_count(dv, 3)
            with dv.Fori(1, turns(dv)) as t:
                for u in range(TURN):
                    item(t * TURN + u, u)
            scatter_idx(last, TURN - 1, before)

            dv.wait_ge(s_gf, 16)
            for c in range(NC):
                dv.wait_ge(s_rf, c + 1)
                dv.scalar_tensor_tensor(out=xh[:, c, :], in0=xh[:, c, :], scalar=rs[:, 4, c:c + 1],
                                        in1=gf_row[:, :], op0=ALU.mult, op1=ALU.mult).then_inc(s_of, 1)

        @block.gpsimd
        def _(gp):
            made = [0]

            def make(ins):
                made[0] += 1
                ins.then_inc(s_mk, 1)

            make(gp.memset(ident[:, :], 0.0))
            make(gp.memset(tri[:, :], 1.0))
            make(gp.memset(triI[:, :], 1.0))
            make(gp.memset(ones[:, :], 1.0))
            make(gp.memset(nch[:, 0:1], 1.0))
            make(gp.memset(tab[:, :], 0))
            make(gp.memset(mhalf[:, :], -0.5))
            make(gp.iota(gi[:, :], pattern=[[1, NG]], base=0, channel_multiplier=0, allow_small_or_imprecise_dtypes=True))
            make(gp.iota(pidx[:, :], pattern=[[1, 1]], base=0, channel_multiplier=1, allow_small_or_imprecise_dtypes=True))
            make(gp.iota(dump[:, :], pattern=[[1, 1]], base=S, channel_multiplier=1, allow_small_or_imprecise_dtypes=True))
            gp.wait_ge(s_mk, made[0])
            make(gp.affine_select(out=ident[:, :], in_=ident[:, :], compare_op=ALU.not_equal, fill=1.0, base=0,
                                  pattern=[[-1, P]], channel_multiplier=1))
            make(gp.affine_select(out=tri[:, :], in_=tri[:, :], compare_op=ALU.is_gt, fill=0.0, base=0,
                                  pattern=[[1, P]], channel_multiplier=-1))
            make(gp.affine_select(out=triI[:, :], in_=triI[:, :], compare_op=ALU.is_ge, fill=0.0, base=0,
                                  pattern=[[1, NE]], channel_multiplier=-1))
            gp.wait_ge(s_mk, made[0])
            gp.sem_inc(s_cst, 1)

            roots = [0]

            def inverse_root(dst, src, done):
                roots[0] += 1
                gp.tensor_scalar(dst, src, EPS, None, ALU.add).then_inc(s_eps, 1)
                gp.wait_ge(s_eps, roots[0])
                gp.tensor_tensor(dst, dst, mhalf[:, :], ALU.pow).then_inc(done, 1)

            def rstd(norm, c, squares, done):
                gp.wait_ge(squares, c + 1)
                inverse_root(rs[:, norm, c:c + 1], ms[:, norm, c:c + 1], done)

            rstd(0, 0, s_sq, s_r1)
            rstd(0, 1, s_sq, s_r1)
            gp.wait_ge(s_small, 16 * 9)
            for step_ in range(NC + 1):
                if step_ + 2 < NC:
                    rstd(0, step_ + 2, s_sq, s_r1)
                if step_ == 0:
                    continue
                c = step_ - 1
                gp.wait_ge(s_ln, 3 * c + 2)
                inverse_root(vr[:, c:c + 1], bag[:, c, 1:2], s_lr)
                gp.wait_ge(s_ln, 3 * (c + 1))
                gp.tensor_tensor(v_sb[:, c, :], v_sb[:, c, :], lng_row[:, :], ALU.mult).then_inc(s_vp, 1)
                gp.wait_ge(s_vp, 2 * c + 1)
                gp.tensor_tensor(v_sb[:, c, :], v_sb[:, c, :], lnb_row[:, :], ALU.add).then_inc(s_vp, 1)
            for c in range(NC):
                rstd(1, c, s_sqa, s_ra)
            for c in range(NC):
                rstd(2, c, s_sqb, s_rb)

            gp.wait_ge(s_yb, NC)
            gp.iota(info[:, :, :, 0], pattern=[[P, NC], [0, NE]], base=-int(EMPTY), channel_multiplier=0,
                    allow_small_or_imprecise_dtypes=True).then_inc(s_info, 1)
            gp.iota(info[:, :, :, 1], pattern=[[0, NC], [0, NE]], base=0, channel_multiplier=1,
                    allow_small_or_imprecise_dtypes=True).then_inc(s_info, 1)
            gp.iota(slots[:, :], pattern=[[1, S + P]], base=0, channel_multiplier=0,
                    allow_small_or_imprecise_dtypes=True).then_inc(s_info, 1)

            for c in range(NC):
                rstd(3, c, s_sq2, s_r2)

            top_row = gp.to_reg(S - 1)
            top_dump = gp.to_reg(S + P - 1)

            def gather(i, u):
                gp.wait_ge(s_id, i + 1)
                after(gp, s_tr, i - 2)
                gp.sem_inc(s_turn, 1)
                gp.indirect_dma_start(out=Xg[:, u, :], out_offset=None, in_=hn_d[:, :],
                                      in_offset=bass.IndirectOffsetOnAxis(ap=idxg[:, u:u + 1], axis=0),
                                      bounds_check=top_row, oob_is_err=False).then_inc(s_ga[u], 16)

            def add_rows(i, u, before=None):
                gp.wait_ge(s_oa, i + 1)
                gp.wait_ge(s_is, i + 1)
                after(gp, s_add, 16 * i)
                gp.sem_inc(s_turn, 1)
                gp.indirect_dma_start(out=y_d[:, :], out_offset=bass.IndirectOffsetOnAxis(ap=idxs[:, u:u + 1], axis=0),
                                      in_=ob[:, u, :], in_offset=None, compute_op=ALU.add,
                                      bounds_check=top_dump).then_inc(s_add, 16)

            def rest_gu(at, e):
                m = GU_PARTS - 1
                gp.wait_ge(s_hg, (e + 1) * GU_PARTS)
                gp.tensor_tensor(gu_part(w_gu[:, :, 1, :, :, :], at, m), gu_part(raw_gu, at, m),
                                 gu_part(w_gu[:, :, 0, :, :, :], at, m).bitcast(F32), ALU.subtract).then_inc(s_lp, 1)

            def item(i, u):
                with gp.If(look(gp, 3, i + 1, 1) > 0):
                    e = look(gp, 0, i + 1, NE - 1)
                    rest_gu(look(gp, 2, i + 1, 1), e)
                if not (isinstance(i, int) and i == 0):
                    add_rows(i - 1, (u - 1) % TURN)
                gather(i + TURN, u)

            rest_gu(1, 0)
            gp.wait_ge(s_hst[0], 16 * 4)
            gp.wait_ge(s_hst[1], 16 * 4)
            gp.wait_ge(s_yst, 16 * (NC + 1))
            gp.wait_ge(s_tab, 1)
            for i in range(TURN):
                gather(i, i)
            for i in range(TURN):
                item(i, i)
            last = item_count(gp, 1)
            with gp.Fori(1, turns(gp)) as t:
                for u in range(TURN):
                    item(t * TURN + u, u)
            add_rows(last, TURN - 1)
            for c in range(NC):
                rstd(4, c, s_sqf, s_rf)


BUTTERFLY = 12


def after(eng, semaphore, value):
    if not isinstance(value, int) or value > 0:
        eng.wait_ge(semaphore, value)


_INS = ["x", "norm1_g", "w_in", "sgu_ln_g", "sgu_ln_b", "w_spatial", "b_spatial", "out_norm_a_g", "out_norm_b_g",
        "w_out", "norm2_g", "w_router", "router_bias", "w_gate", "w_up", "w_down", "ws_gate", "ws_up", "ws_down"]


def dft_tables():
    import numpy as np
    q = np.arange(P)[:, None, None]
    s = NC * np.arange(P)[None, None, :] + np.arange(NC)[None, :, None]
    th = 2 * np.pi * ((q * s) % S) / S
    pos = np.stack([np.cos(th), np.sin(th)], axis=1) / 256.0
    k = np.arange(64)
    th = 2 * np.pi * (np.outer(k, k) % 64) / 64
    C = np.kron(np.eye(2), np.cos(th))
    Sn = np.kron(np.eye(2), np.sin(th))
    ch = np.stack([np.stack([C, -Sn], 1), np.stack([Sn, C], 1), np.stack([-Sn, -C], 1)], 1)
    return pos.astype(np.float32), ch.astype(np.float32)


def kernel(**inputs):
    import numpy as np
    import concourse.bacc as bacc
    from concourse.bass_utils import run_bass_kernel_spmd as run

    nc = bacc.Bacc("TRN2", target_bir_lowering=False, num_devices=1)
    a = {k: np.asarray(inputs[k])[0] for k in _INS}
    a["final_norm_g"] = np.asarray(inputs["final_norm_g"])
    a["w_spatial"] = np.ascontiguousarray(a["w_spatial"].transpose(0, 2, 1))
    a["b_spatial"] = np.ascontiguousarray(a["b_spatial"].T)
    a["dft_pos"], a["dft_ch"] = dft_tables()
    order = _INS + ["dft_pos", "dft_ch"]
    order.insert(len(_INS), "final_norm_g")
    h = {k: nc.dram_tensor("in_" + k, a[k].shape, F32, kind="ExternalInput").ap() for k in order}
    out = nc.dram_tensor("result", (S, D), F32, kind="ExternalOutput").ap()
    hn_d = nc.dram_tensor("hn_rows_dram", (S, D), F32, kind="Internal").ap()
    y_d = nc.dram_tensor("y_rows_dram", (S + P, D), F32, kind="Internal").ap()
    build(nc, h["x"], h["norm1_g"], h["w_in"], h["sgu_ln_g"], h["sgu_ln_b"], h["w_spatial"], h["b_spatial"],
          h["out_norm_a_g"], h["out_norm_b_g"], h["w_out"], h["norm2_g"], h["w_router"], h["router_bias"],
          h["w_gate"], h["w_up"], h["w_down"], h["ws_gate"], h["ws_up"], h["ws_down"], h["dft_pos"], h["dft_ch"],
          h["final_norm_g"], out, hn_d, y_d)
    r = run(nc, [{"in_" + k: np.ascontiguousarray(a[k]) for k in order}], core_ids=[0])
    return r.results[0]["result"].reshape(1, S, D)
```

```python
from contextlib import ExitStack

import concourse.bass as bass
from concourse import mybir

P = 128
D = 1024
S = 1024
NC = S // P
KD = D // P
DA = 512
NH = 8
HD = DA // NH
NE = 64
TOPK = 8
NG = 8
GE = NE // NG
TOPG = 4
F = 256
KF = F // P
RSCALE = 2.5
EPS = 1e-6
MAXCH = S // P
NITEM = (S * TOPK) // P + NE
TAB = NITEM + 8
EMPTY = 4096.0
BIG = 3.0e38
TURN = 3
GU_PARTS = 4

ALU = mybir.AluOpType
ACT = mybir.ActivationFunctionType
AX = mybir.AxisListType
F32 = mybir.dt.float32
BF16 = mybir.dt.bfloat16
F32R = mybir.dt.float32r
I32 = mybir.dt.int32
U32 = mybir.dt.uint32
R8 = 0.5 ** 0.5


def build(nc, x, g1, w_in, ln_g, ln_b, wsT, bsT, ga, gb, w_out, g2, w_router, rbias, wg, wu, wd,
          sg, su, sd, dft_pos, dft_ch, gf, out, hn_d, y_d):
    ctx = ExitStack()
    with ctx:
        top = [nc.sbuf_base]

        def place(name, shape, dt, at=None):
            size = 2 if dt == BF16 else 4
            n = size
            for s in shape[1:]:
                n *= s
            n = (n + 31) // 32 * 32
            if at is None:
                at = top[0]
                top[0] += n
            return nc.alloc_sbuf_tensor_at(name, shape, dt, offset=at)

        base0 = top[0] = (top[0] + 63) // 64 * 64
        KB = 1024
        X_AT = base0
        T_AT = X_AT + 32 * KB
        W_AT = T_AT + 32 * KB
        U_AT = W_AT + 48 * KB
        V_AT = U_AT + 16 * KB
        Z_AT = V_AT + 16 * KB
        S_AT = Z_AT + 16 * KB
        D_AT = S_AT + 8 * KB
        R_AT = D_AT + 8 * KB
        top[0] = R_AT + 12 * KB

        xh = place("xh", [P, NC, D], F32, X_AT)
        T = place("T", [P, KD, S], F32, T_AT)
        w_in_sb = place("w_in_sb", [P, KD, 3 * DA], F32, W_AT)
        w_in_high = place("w_in_high", [P, KD, 2 * DA], F32R, X_AT)
        w_in_rest = place("w_in_rest", [P, KD, 3 * DA], F32R, W_AT)
        x_ring = place("x_ring", [P, 2, D], F32, Z_AT)
        xt_rest = place("xt_rest", [P, 2, KD, P], F32R, Z_AT + 8 * KB)
        xt_high = place("xt_high", [P, 2, KD, P], F32R, D_AT)
        w_out_sb = place("w_out_sb", [P, KD, D], F32, W_AT)
        w_out_high = [place("w_out_high0", [P, 4, D], F32R, U_AT), place("w_out_high1", [P, 4, D], F32R, Z_AT)]
        w_out_rest = place("w_out_rest", [P, KD, D], F32R, W_AT)
        cat_high = place("cat_high", [P, 2, KD, P], F32R, V_AT)
        cat_rest = place("cat_rest", [P, 2, KD, P], F32R, V_AT + 8 * KB)
        U = place("U", [P, 8, 4, P], F32, W_AT + 32 * KB)
        sgu_w = place("sgu_w", [P, 2, KD, F], F32, W_AT + 32 * KB)
        u_sb = place("u_sb", [P, NC, DA], F32, U_AT)
        v_sb = place("v_sb", [P, NC, DA], F32, V_AT)
        ab = place("ab", [P, 2, 4, 512], F32, V_AT)
        yb = place("yb", [P, NC, DA], F32, V_AT)
        zT = place("zT", [P, 4, S], F32, Z_AT)
        rows = place("rows", [P, 2, D], F32, S_AT)
        dt = place("dt", [P, 2, 4, P], F32, S_AT)
        V = place("V", [P, 2, 4, 2, P], F32, S_AT)
        hsT = place("hsT", [P, KF, S], F32, S_AT)
        dpos = place("dpos", [P, 2, 8, P], F32, D_AT)
        sd_w = place("sd_w", [P, KF, D], F32, D_AT)
        g1_row = place("g1_row", [P, D], F32, R_AT)
        lng_row = place("lng_row", [P, DA], F32, R_AT + 4 * KB)
        lnb_row = place("lnb_row", [P, DA], F32, R_AT + 6 * KB)
        ga_row = place("ga_row", [P, DA], F32, R_AT + 8 * KB)
        gb_row = place("gb_row", [P, DA], F32, R_AT + 10 * KB)
        pos = place("pos", [P, NC, NE], F32, R_AT)
        info = place("info", [P, NC, NE, 5], BF16, R_AT + 2 * KB)
        slots = place("slots", [P, 1024 + P], F32, R_AT + 7 * KB)
        raw_gu = place("raw_gu", [P, 2, 2, KD, F], F32, U_AT)
        raw_dn = place("raw_dn", [P, 2, KF, D], F32, Z_AT)
        w_gu = place("w_gu", [P, 2, 2, 2, KD, F], F32R, X_AT)
        w_dn = place("w_dn", [P, 2, 2, KF, D], F32R, W_AT)
        s_tmp = place("s_tmp", [P, 2, 512], F32, W_AT + 24 * KB)
        rt_a = place("rt_a", [P, NC, NE], F32, W_AT + 28 * KB)
        rt_b = place("rt_b", [P, NC, NE], F32, W_AT + 30 * KB)
        Xg = place("Xg", [P, TURN, D], F32, W_AT + 32 * KB)
        xTh = place("xTh", [P, KD, P], F32R, W_AT + 44 * KB)
        ob = place("ob", [P, TURN, D], F32, S_AT)
        xTl = place("xTl", [P, KD, P], F32R, S_AT + 12 * KB)
        g2_row = place("g2_row", [P, D], F32)
        idx_all = place("idx_all", [P, TAB], I32, top[0] - 4 * KB)
        gate_all = place("gate_all", [P, TAB], F32, top[0] - 3 * KB)
        le = place("le", [P, 3, NE], F32, top[0] - 2 * KB)
        dch = place("dch", [P, 3, 2, P], F32)
        C_AT = top[0] - 3 * KB
        scores = place("scores", [P, NC, NE], F32, C_AT)
        mask = place("mask", [P, NC, NE], BF16, C_AT + 2 * KB)
        info_i = place("info_i", [P, NC, 5], BF16)
        hs = place("hs", [P, F], F32, C_AT)
        hh = place("hh", [P, F], F32, C_AT + KB)
        hTh = place("hTh", [P, KF, P], F32R, C_AT + 2 * KB)
        wsp = place("wsp", [P, NH, P], F32)
        M_AT = top[0] - 4 * KB
        onehot = place("onehot", [P, NC, P], BF16, M_AT)
        m8 = place("m8", [P, NC, NG, 8], F32, M_AT)
        geq = place("geq", [P, NC, NG, TOPG], F32, M_AT + 2 * KB)
        gs = place("gs", [P, NC, NG], F32, M_AT + 3 * KB)
        gtop = place("gtop", [P, NC, 8], F32, M_AT + 3 * KB + 256)
        gidx = place("gidx", [P, NC, 8], U32, M_AT + 3 * KB + 512)
        etop = place("etop", [P, NC, 8], F32, M_AT + 3 * KB + 768)
        junk = place("junk", [P, D], BF16)
        bsp = place("bsp", [P, NH], F32)
        ident = place("ident", [P, P], F32)
        wr_sb = place("wr_sb", [P, KD, NE], F32)
        hTl = place("hTl", [P, KF, P], F32R, top[0] - 2 * KB)
        rb_row = place("rb_row", [P, NE], F32)
        tri = place("tri", [P, P], BF16)
        triI = place("triI", [NE, NE], BF16)
        ones = place("ones", [P, P], BF16)
        ms = place("ms", [P, 5, NC], F32)
        rs = place("rs", [P, 5, NC], F32)
        bst = place("bst", [P, NC, 6], F32)
        bag = place("bag", [P, NC, 2], F32)
        vr = place("vr", [P, NC], F32)
        gidxf = place("gidxf", [P, NC, TOPG], F32)
        gi = place("gi", [P, NG], F32)
        gm = place("gm", [P, NC, NG], F32)
        gsum = place("gsum", [P, NC], F32)
        grec = place("grec", [P, NC], F32)
        pidx = place("pidx", [P, 1], F32)
        dump = place("dump", [P, 1], F32)
        nch = place("nch", [NE, 1 + MAXCH], F32)
        nchb = place("nchb", [NE, P], BF16)
        cols = place("cols", [P, 12], F32)
        tab = place("tab", [4, TAB], I32)
        ends = place("ends", [1, NE + 5], I32)
        mhalf = place("mhalf", [P, 1], F32)
        halves = place("halves", [P, 1], I32)
        sumf = place("sumf", [P, 8], F32)
        idxf = place("idxf", [P, 1], F32)
        idxg = place("idxg", [P, TURN], I32)
        idxs = place("idxs", [P, TURN], I32)
        assert top[0] <= nc.sbuf_usable_end, (top[0], nc.sbuf_usable_end)
        gf_row = place("gf_row", [P, D], F32, Z_AT)

        ps = [ctx.enter_context(nc.psum_tensor(f"ps{i}", [P, 512], F32)) for i in range(8)]

        def sem(name):
            return ctx.enter_context(nc.semaphore(name))

        s_x = [sem(f"x_in{c}") for c in range(NC)]
        s_wi = [sem(f"w_in_uv_in{k}") for k in range(KD)]
        s_g1, s_wib, s_small, s_dft = sem("g1_in"), sem("w_in_b_in"), sem("small_in"), sem("dft_in")
        s_wo_in, s_sh_in, s_sd_in, s_gf = sem("w_out_in"), sem("shared_in"), sem("shared_down_in"), sem("gf_in")
        s_lr, s_eps = sem("v_rstd"), sem("eps_added")
        s_cst, s_mk, s_info = sem("consts_ready"), sem("const_made"), sem("token_info")
        s_sq, s_r1, s_xs, s_t1, s_t1a, s_t1d = (sem(n) for n in (
            "sq1", "rstd1", "xn_rows", "xn_tr", "xn_evac_act", "xn_evac_dve"))
        s_za, s_ge, s_ln, s_vp, s_zb, s_ze = (sem(n) for n in (
            "za_done", "gelu_done", "ln_step", "v_ready", "zb_done", "zT_ready"))
        s_wih, s_wil, s_xth, s_xtl = (sem(n) for n in ("w_in_high", "w_in_rest", "xT_high", "xT_rest"))
        s_sg, s_ya, s_sqa, s_ra, s_yn, s_ta, s_tae = (sem(n) for n in (
            "sgu_done", "ya_ready", "sqa", "rstda", "ya_normed", "ya_tr", "ya_evac"))
        s_bf, s_v, s_va, s_vd, s_y, s_sqb, s_rb, s_yb, s_tb, s_tbe = (sem(n) for n in (
            "butterfly", "V_done", "V_evac_act", "V_evac_dve", "Y_done", "sqb", "rstdb", "yb_ready", "yb_tr",
            "yb_evac"))
        s_wo, s_hx, s_sq2, s_r2, s_hn, s_t3, s_t3a, s_t3d, s_rt, s_sc = (sem(n) for n in (
            "w_out_done", "h_ready", "sq2", "rstd2", "hn_rows", "hn_tr", "hn_evac_act", "hn_evac_dve", "router_done",
            "scores_ready"))
        s_woh, s_wol, s_ch, s_cl = (sem(n) for n in ("w_out_high", "w_out_rest", "cat_high", "cat_rest"))
        s_hst = [sem(f"hn_stored{i}") for i in range(2)]
        s_q, s_ssi, s_hm, s_sdn, s_y0, s_yst = (sem(n) for n in (
            "shared_gu", "shared_silu", "shared_h", "shared_down", "y0_ready", "y0_stored"))
        s_mask, s_chunks, s_cols = sem("mask_ready"), sem("chunks_ready"), sem("item_cols_ready")
        s_rv, s_pm, s_tab = sem("routing_step"), sem("routing_matmul"), sem("tables_ready")
        s_cp, s_pk = sem("sums_copied"), sem("expert_info_picked")
        s_oh, s_ix, s_it, s_id, s_ia, s_gt = (sem(n) for n in (
            "onehot_ready", "slots_summed", "idx_tmp", "gather_idx", "idx_kept", "gate_kept"))
        s_ga = [sem(f"rows_gathered{u}") for u in range(TURN)]
        s_tr, s_xa, s_xd, s_gu, s_si, s_h, s_ht, s_he = (sem(n) for n in (
            "x_tr", "xT_act", "xT_dve", "gate_up", "silu", "h_rows", "h_tr", "hT_ready"))
        s_dn, s_oa, s_od, s_is, s_add, s_turn = (sem(n) for n in (
            "down_done", "out_act", "out_dve", "scatter_idx", "rows_added", "pool_turn"))
        s_gu_in = [sem(f"gate_up_in{i}") for i in range(2)]
        s_dn_in = [sem(f"down_in{i}") for i in range(2)]
        s_rg, s_rd, s_turn_sp = sem("gate_up_landed"), sem("down_landed"), sem("sp_turn")
        s_hg, s_lg, s_hd, s_ld, s_hl = (sem(n) for n in ("gu_high", "gu_rest", "down_high", "down_rest", "hT_rest"))
        s_yl = [sem(f"y_in{c}") for c in range(NC)]
        s_sqf, s_rf, s_of, s_ost = sem("sqf"), sem("rstdf"), sem("out_rows"), sem("out_stored")

        x_v = x.rearrange("(c p) d -> c p d", p=P)
        out_v = out.rearrange("(c p) d -> c p d", p=P)
        hn_v = hn_d.rearrange("(c p) d -> c p d", p=P)
        yv = y_d.rearrange("(c p) d -> c p d", p=P)
        spread = lambda ap, n: ap.rearrange("(a n) -> a n", a=1).to_broadcast([P, n])

        def load_gu(eng, e, at):
            eng.dma_start(raw_gu[:, at, 0, :, :], wg[e].rearrange("(p k) f -> p k f", k=KD)).then_inc(s_gu_in[at], 16)
            eng.dma_start(raw_gu[:, at, 1, :, :], wu[e].rearrange("(p k) f -> p k f", k=KD)).then_inc(s_gu_in[at], 16)

        def load_dn(eng, e, at):
            eng.dma_start(raw_dn[:, at, :, :], wd[e].rearrange("(k p) d -> p k d", p=P)).then_inc(s_dn_in[at], 16)

        def gu_part(t, at, m):
            v = t[:, bass.ds(at, 1), m // 2, (m % 2) * 4:(m % 2) * 4 + 4, :]
            return v.rearrange("p a k f -> p (a k) f")

        def item_count(eng, less=0):
            return eng.value_load(ends[0:1, NE + less:NE + less + 1], min_val=NE - less, max_val=NITEM + 1 - less)

        def turns(eng):
            return eng.value_load(ends[0:1, NE + 4:NE + 5], min_val=NE // TURN, max_val=(NITEM + 1) // TURN)

        def look(eng, row, i, top_val):
            return eng.value_load(tab[row:row + 1, bass.ds(i, 1)], min_val=0, max_val=top_val)

        def place_of(eng, e):
            return eng.snap((e + 1) % 2, min_val=0, max_val=1)

        block = ctx.enter_context(nc.Block())

        @block.sync
        def _(sp):
            sp.dma_start(x_ring[:, 0, :], x_v[0]).then_inc(s_x[0], 16)
            sp.dma_start(g1_row[:, :], spread(g1, D)).then_inc(s_g1, 16)
            sp.dma_start(x_ring[:, 1, :], x_v[1]).then_inc(s_x[1], 16)
            w_in_v = w_in.rearrange("(p k) e -> p k e", k=KD)
            for k in range(KD):
                sp.dma_start(w_in_sb[:, k, 0:2 * DA], w_in_v[:, k, 0:2 * DA]).then_inc(s_wi[k], 16)

            def next_x(c):
                sp.wait_ge(s_xs, c - 1)
                sp.dma_start(x_ring[:, c % 2, :], x_v[c]).then_inc(s_x[c], 16)

            next_x(2)
            for dst, src in ((lng_row[:, :], spread(ln_g, DA)), (lnb_row[:, :], spread(ln_b, DA)),
                             (ga_row[:, :], spread(ga, DA)), (gb_row[:, :], spread(gb, DA)),
                             (g2_row[:, :], spread(g2, D)), (rb_row[:, :], spread(rbias, NE)),
                             (wsp[:, :, :], wsT.rearrange("h q p -> q h p")), (bsp[:, :], bsT),
                             (wr_sb[:, :, :], w_router.rearrange("(p k) e -> p k e", k=KD))):
                sp.dma_start(dst, src).then_inc(s_small, 16)
            sp.dma_start(w_in_sb[:, :, 2 * DA:], w_in_v[:, :, 2 * DA:]).then_inc(s_wib, 16)
            for c in range(3, NC):
                next_x(c)
            sp.wait_ge(s_za, 2 * NC)
            for c in range(NC):
                sp.dma_start(xh[:, c, :], x_v[c]).then_inc(s_x[c], 16)
            sp.dma_start(dpos[:, :, :, :], dft_pos).then_inc(s_dft, 16)
            sp.dma_start(dch[:, :, :, :], dft_ch).then_inc(s_dft, 16)
            sp.wait_ge(s_zb, 8)
            sp.dma_start(w_out_sb[:, :, :], w_out.rearrange("(k p) d -> p k d", p=P)).then_inc(s_wo_in, 16)
            sp.wait_ge(s_v, 8)
            sp.dma_start(sgu_w[:, 0, :, :], sg.rearrange("(p k) f -> p k f", k=KD)).then_inc(s_sh_in, 16)
            sp.dma_start(sgu_w[:, 1, :, :], su.rearrange("(p k) f -> p k f", k=KD)).then_inc(s_sh_in, 16)
            sp.wait_ge(s_y, 8)
            sp.dma_start(sd_w[:, :, :], sd.rearrange("(k p) d -> p k d", p=P)).then_inc(s_sd_in, 16)
            for c in range(NC):
                sp.wait_ge(s_hn, c + 1)
                sp.dma_start(hn_v[c], rows[:, c % 2, :]).then_inc(s_hst[c % 2], 16)
            sp.wait_ge(s_wo, NC)
            for e in range(2):
                load_gu(sp, e, 1 - e)
                load_dn(sp, e, 1 - e)
            sp.wait_ge(s_gu_in[1], 32)
            sp.sem_inc(s_rg, 1)
            for c in range(NC):
                sp.wait_ge(s_y0, c + 1)
                sp.dma_start(yv[c], xh[:, c, :]).then_inc(s_yst, 16)
            sp.dma_start(yv[NC], xh[:, 0, :]).then_inc(s_yst, 16)
            def load_next_gu(e, at):
                sp.wait_ge(s_hg, (e - 1) * GU_PARTS)
                sp.sem_inc(s_turn_sp, 1)
                sp.wait_ge(s_lg, (e - 1) * GU_PARTS)
                sp.sem_inc(s_turn_sp, 1)
                load_gu(sp, e, at)

            def load_next_dn(e, at):
                sp.wait_ge(s_hd, (e - 1) * KF)
                sp.sem_inc(s_turn_sp, 1)
                sp.wait_ge(s_ld, (e - 1) * KF)
                sp.sem_inc(s_turn_sp, 1)
                load_dn(sp, e, at)

            def gu_landed(at, fills):
                sp.wait_ge(s_gu_in[at], fills * 32)
                sp.sem_inc(s_rg, 1)

            def dn_landed(at, fills):
                sp.wait_ge(s_dn_in[at], fills * 16)
                sp.sem_inc(s_rd, 1)

            load_next_gu(2, 1)
            gu_landed(0, 1)
            dn_landed(1, 1)
            with sp.Fori(1, NE // 2 - 1) as t:
                load_next_gu(t * 2 + 1, 0)
                gu_landed(1, t + 1)
                load_next_dn(t * 2, 1)
                dn_landed(0, t)
                load_next_gu(t * 2 + 2, 1)
                gu_landed(0, t + 1)
                load_next_dn(t * 2 + 1, 0)
                dn_landed(1, t + 1)
            load_next_gu(NE - 1, 0)
            gu_landed(1, NE // 2)
            load_next_dn(NE - 2, 1)
            dn_landed(0, NE // 2 - 1)
            gu_landed(0, NE // 2)
            load_next_dn(NE - 1, 0)
            dn_landed(1, NE // 2)
            dn_landed(0, NE // 2)
            n = item_count(sp)
            sp.wait_ge(s_add, n * 16)
            sp.sem_inc(s_turn_sp, 1)
            sp.dma_start(gf_row[:, :], spread(gf, D)).then_inc(s_gf, 16)
            for c in range(NC):
                sp.dma_start(xh[:, c, :], yv[c]).then_inc(s_yl[c], 16)
            for c in range(NC):
                sp.wait_ge(s_of, c + 1)
                sp.dma_start(out_v[c], xh[:, c, :]).then_inc(s_ost, 16)
            sp.wait_ge(s_ost, 16 * NC)

        @block.tensor
        def _(pe):
            def turn_rows(src, banks, count=KD):
                for k in range(count):
                    last = pe.transpose(ps[banks[k // 4]][:, (k % 4) * P:(k % 4 + 1) * P], src[:, k:D:KD], ident[:, :])
                return last

            def turn_x(c):
                pe.wait_ge(s_xs, c + 1)
                if c >= 2:
                    pe.wait_ge(s_t1a, c - 1)
                    pe.wait_ge(s_t1d, c - 1)
                turn_rows(rows[:, c % 2, :], (0, 1) if c % 2 == 0 else (6, 7)).then_inc(s_t1, 1)

            def z_a_products(c, half, k):
                cols_ = slice(half * DA, (half + 1) * DA)
                high, rest = w_in_high[:, k, cols_], w_in_rest[:, k, cols_]
                for n, (x_, w_) in enumerate(((xt_high, high), (xt_high, rest), (xt_rest, high))):
                    mm = pe.matmul(ps[2 + 2 * (c % 2) + half][:, :], x_[:, c % 2, k, :], w_,
                                   start=(k == 0 and n == 0), stop=(k == KD - 1 and n == 2))
                return mm

            def z_a(c):
                pe.wait_ge(s_xth, c + 1)
                pe.wait_ge(s_xtl, c + 1)
                if c == 0:
                    for k in range(KD):
                        pe.wait_ge(s_wih, k + 1)
                        pe.wait_ge(s_wil, k + 1)
                        for half in range(2):
                            mm = z_a_products(c, half, k)
                            if k == KD - 1:
                                mm.then_inc(s_za, 1)
                    return
                for half in range(2):
                    if c >= 2:
                        pe.wait_ge(s_ge, 2 * (c - 2) + half + 1)
                    for k in range(KD):
                        mm = z_a_products(c, half, k)
                    mm.then_inc(s_za, 1)

            def z_b(g):
                th, et = g // 4, g % 4
                if g == 0:
                    pe.wait_ge(s_wib, 16)
                if g < 4:
                    pe.wait_ge(s_ge, 2 * (NC - 2) + g + 1)
                else:
                    pe.wait_ge(s_ze, g - 3)
                for k in range(KD):
                    mm = pe.matmul(ps[2 + g % 4][:, :], w_in_sb[:, k, 2 * DA + et * P:2 * DA + (et + 1) * P],
                                   T[:, k, th * 512:(th + 1) * 512], start=(k == 0), stop=(k == KD - 1))
                mm.then_inc(s_zb, 1)

            pe.wait_ge(s_cst, 1)
            turn_x(0)
            for c in range(NC):
                if c + 1 < NC:
                    turn_x(c + 1)
                z_a(c)
            for g in range(4):
                z_b(g)

            free4 = (0, 1, 6, 7)
            pe.wait_ge(s_vp, 2 * NC)
            pe.wait_ge(s_small, 16 * 9)
            for h in range(NH):
                if h >= 4:
                    pe.wait_ge(s_ya, h - 3)
                pe.matmul(ps[free4[h % 4]][:, :], wsp[:, h, :], v_sb[:, :, h * HD:(h + 1) * HD],
                          start=True, stop=True).then_inc(s_sg, 1)
            for g in range(4, 8):
                z_b(g)
            pe.wait_ge(s_ya, NH)
            for c in range(NC):
                pe.wait_ge(s_yn, c + 1)
                if c >= 4:
                    pe.wait_ge(s_tae, c - 3)
                for k in range(4):
                    tr = pe.transpose(ps[free4[c % 4]][:, k * P:(k + 1) * P], u_sb[:, c, k * P:(k + 1) * P], ident[:, :])
                tr.then_inc(s_ta, 1)

            terms = {0: [(0, 0)], 4: [(1, 0)], 1: [(2, 0), (3, 2)], 7: [(2, 0), (3, 1)], 2: [(4, 0), (5, 2)],
                     6: [(4, 0), (5, 1)], 3: [(6, 0), (7, 1)], 5: [(6, 0), (7, 2)]}

            def chan(s0):
                if s0 < 2:
                    pe.wait_ge(s_ze, 8)
                    pe.wait_ge(s_bf, BUTTERFLY)
                    pe.wait_ge(s_dft, 32)
                else:
                    pe.wait_ge(s_va, s0 - 1)
                    pe.wait_ge(s_vd, s0 - 1)
                for pair in range(4):
                    bank = ps[2 + 2 * (s0 % 2) + pair // 2]
                    for n, (a, m) in enumerate(terms[s0]):
                        mm = pe.matmul(bank[:, (pair % 2) * 256:(pair % 2 + 1) * 256], U[:, a, pair, :],
                                       dch[:, m, :, :], start=(n == 0), stop=(n == len(terms[s0]) - 1))
                mm.then_inc(s_v, 1)

            def posn(s0):
                pe.wait_ge(s_va, s0 + 1)
                pe.wait_ge(s_vd, s0 + 1)
                if s0 < 2:
                    pe.wait_ge(s_tae, NC)
                else:
                    pe.wait_ge(s_yb, s0 - 1)
                for ri in range(2):
                    mm = pe.matmul(ps[s0 % 2][:, :], dpos[:, ri, s0, :], V[:, s0 % 2, :, ri, :],
                                   start=(ri == 0), stop=(ri == 1))
                mm.then_inc(s_y, 1)

            def turn_b(s0):
                pe.wait_ge(s_yb, s0 + 1)
                if s0 >= 2:
                    pe.wait_ge(s_tbe, s0 - 1)
                for k in range(4):
                    tr = pe.transpose(ps[6 + s0 % 2][:, k * P:(k + 1) * P], yb[:, s0, k * P:(k + 1) * P], ident[:, :])
                tr.then_inc(s_tb, 1)

            for s0 in range(NC + 2):
                if s0 < NC:
                    chan(s0)
                if 1 <= s0 <= NC:
                    posn(s0 - 1)
                if s0 >= 2:
                    turn_b(s0 - 2)

            def w_o(c):
                if c == 0:
                    pe.wait_ge(s_woh, KD)
                    pe.wait_ge(s_wol, KD)
                    pe.wait_ge(s_yb, NC)
                pe.wait_ge(s_ch, c + 1)
                pe.wait_ge(s_cl, c + 1)
                if c >= 2:
                    pe.wait_ge(s_hx, 2 * (c - 1))
                for half in range(2):
                    cols_ = slice(half * 512, (half + 1) * 512)
                    for k in range(KD):
                        high, rest = w_out_high[k // 4][:, k % 4, cols_], w_out_rest[:, k, cols_]
                        products = ((cat_high, high), (cat_high, rest), (cat_rest, high))
                        for n, (x_, w_) in enumerate(products):
                            mm = pe.matmul(ps[2 * (c % 2) + half][:, :], x_[:, c % 2, k, :], w_,
                                           start=(k == 0 and n == 0), stop=(k == KD - 1 and n == 2))
                mm.then_inc(s_wo, 1)

            def turn_hn(c):
                pe.wait_ge(s_hn, c + 1)
                if c >= 1:
                    pe.wait_ge(s_t3a, c)
                    pe.wait_ge(s_t3d, c)
                turn_rows(rows[:, c % 2, :], (4, 5)).then_inc(s_t3, 1)

            def router(c):
                pe.wait_ge(s_t3a, c + 1)
                pe.wait_ge(s_t3d, c + 1)
                if c >= 2:
                    pe.wait_ge(s_sc, c - 1)
                for k in range(KD):
                    mm = pe.matmul(ps[6 + c % 2][:, 0:NE], T[:, k, c * P:(c + 1) * P], wr_sb[:, k, :],
                                   start=(k == 0), stop=(k == KD - 1))
                mm.then_inc(s_rt, 1)

            for c in range(NC + 2):
                if c < NC:
                    w_o(c)
                if 1 <= c <= NC:
                    turn_hn(c - 1)
                if c >= 2:
                    router(c - 2)

            def s_gate_up(q):
                th, ft = q // 2, q % 2
                if q >= 2:
                    pe.wait_ge(s_hm, q - 1)
                for j in range(2):
                    for k in range(KD):
                        mm = pe.matmul(ps[2 * (q % 2) + j][:, :], sgu_w[:, j, k, ft * P:(ft + 1) * P],
                                       T[:, k, th * 512:(th + 1) * 512], start=(k == 0), stop=(k == KD - 1))
                mm.then_inc(s_q, 1)

            def s_down(c):
                if c >= 2:
                    pe.wait_ge(s_y0, c - 1)
                for half in range(2):
                    for k in range(KF):
                        mm = pe.matmul(ps[4 + 2 * (c % 2) + half][:, :], hsT[:, k, c * P:(c + 1) * P],
                                       sd_w[:, k, half * 512:(half + 1) * 512], start=(k == 0), stop=(k == KF - 1))
                mm.then_inc(s_sdn, 1)

            pe.wait_ge(s_sh_in, 32)
            pe.wait_ge(s_hx, 2 * NC)
            s_gate_up(0)
            s_gate_up(1)
            pe.wait_ge(s_mask, 1)
            pe.wait_ge(s_sc, NC)
            pe.wait_ge(s_t3a, NC)
            pe.wait_ge(s_t3d, NC)
            flat = mask[:, :, :].rearrange("p c e -> p (c e)")
            pe.matmul(ps[4][:, :], tri[:, :], flat, start=True, stop=True)
            for d in range(1, NC):
                mm = pe.matmul(ps[4][:, d * NE:], ones[:, :], flat[:, 0:(NC - d) * NE], start=False, stop=True,
                               skip_group_check=True)
            for c in range(NC):
                mm = pe.matmul(ps[5][0:NE, 0:1], mask[:, c, :], ones[:, 0:1], start=(c == 0), stop=(c == NC - 1))
            mm.then_inc(s_pm, 1)
            s_gate_up(2)
            pe.wait_ge(s_chunks, 1)
            pe.matmul(ps[6][:, 0:NE], nchb[:, :], triI[:, :], start=True, stop=True).then_inc(s_pm, 1)
            s_gate_up(3)
            pe.wait_ge(s_cols, 1)
            pe.matmul(ps[7][0:4, 0:P], cols[:, 0:4], ident[:, :], start=True, stop=True).then_inc(s_pm, 1)

            def slot_sums(i):
                pe.wait_ge(s_oh, i + 1)
                pe.wait_ge(s_pk, i + 1)
                after(pe, s_cp, i)
                for c in range(NC):
                    mm = pe.matmul(ps[0][:, 0:5], onehot[:, c, :], info_i[:, c, :],
                                   start=(c == 0), stop=(c == NC - 1))
                mm.then_inc(s_ix, 1)

            def turn_item(u, fills):
                pe.wait_ge(s_ga[u], 16 * fills)
                turn_rows(Xg[:, u, :], (1, 2)).then_inc(s_tr, 1)

            def gate_up(i, e, at):
                pe.wait_ge(s_hg, (e + 1) * GU_PARTS)
                pe.wait_ge(s_lg, (e + 1) * GU_PARTS)
                pe.wait_ge(s_xd, 2 * i + 2)
                for k in range(KD):
                    for x_, part in ((xTh, 0), (xTh, 1), (xTl, 0)):
                        mm = pe.matmul(ps[3][:, :], x_[:, k, :], w_gu[:, bass.ds(at, 1), part, :, k, :],
                                       start=(k == 0 and part == 0 and x_ is xTh), stop=(k == KD - 1 and x_ is xTl))
                mm.then_inc(s_gu, 1)

            def down(i, e, at, first=False):
                pe.wait_ge(s_hd, (e + 1) * 2)
                pe.wait_ge(s_ld, (e + 1) * 2)
                pe.wait_ge(s_hl, i + 1)
                if not first:
                    pe.wait_ge(s_oa, i)
                for half in range(2):
                    for k in range(KF):
                        for h_, part in ((hTh, 0), (hTh, 1), (hTl, 0)):
                            mm = pe.matmul(ps[6 + half][:, :], h_[:, k, :],
                                           w_dn[:, bass.ds(at, 1), part, k, half * 512:(half + 1) * 512],
                                           start=(k == 0 and part == 0 and h_ is hTh), stop=(k == KF - 1 and h_ is hTl))
                mm.then_inc(s_dn, 1)

            def turn_h(i):
                pe.wait_ge(s_h, i + 1)
                for k in range(KF):
                    tr = pe.transpose(ps[5][:, k * P:(k + 1) * P], hh[:, k * P:(k + 1) * P], ident[:, :])
                tr.then_inc(s_ht, 1)

            def expert(i):
                e = look(pe, 0, i, NE - 1)
                return e, place_of(pe, e)

            def item(i, u, turn, now, before):
                turn_item((u + 1) % TURN, turn + 1 if u + 1 < TURN else turn + 2)
                if before:
                    down(i - 1, *before, first=isinstance(i, int) and i == 1)
                slot_sums(i + TURN)
                after_this = expert(i + 1)
                turn_h(i)
                gate_up(i + 1, *after_this)
                return after_this

            def turn_of_items(turn, before):
                now = expert(turn * TURN)
                for u in range(TURN):
                    now, before = item(turn * TURN + u, u, turn, now, before), now
                return before

            pe.wait_ge(s_hm, 4)
            pe.wait_ge(s_sd_in, 16)
            pe.wait_ge(s_tab, 1)
            for i in range(TURN):
                s_down(2 * i)
                s_down(2 * i + 1)
                slot_sums(i)
            turn_item(0, 1)
            s_down(2 * TURN)
            s_down(2 * TURN + 1)
            gate_up(0, *expert(0))
            pe.wait_ge(s_y0, NC)
            turn_of_items(0, None)
            last = item_count(pe, 1)
            with pe.Fori(1, turns(pe)) as t:
                turn_of_items(t, expert(t * TURN - 1))
            down(last, *expert(last))

        @block.scalar
        def _(act):
            def square(src, scale, norm, c, done):
                act.activation(junk[:, 0:src.shape[-1]], src, ACT.Square, scale=scale,
                               accum_out=ms[:, norm, c:c + 1]).then_inc(done, 1)

            def sq1(c):
                act.wait_ge(s_x[c], 16)
                if c:
                    act.wait_ge(s_sq, c)
                square(x_ring[:, c % 2, :], D ** -0.5, 0, c, s_sq)

            def evac_x(c):
                act.wait_ge(s_t1, c + 1)
                act.activation(T[:, 0:4, c * P:(c + 1) * P], ps[0 if c % 2 == 0 else 6][:, :].rearrange(
                    "p (k t) -> p k t", k=4), ACT.Copy).then_inc(s_t1a, 1)

            def gelu(c):
                for half, dst in enumerate((u_sb, v_sb)):
                    act.wait_ge(s_za, 2 * c + half + 1)
                    act.activation(dst[:, c, :], ps[2 + 2 * (c % 2) + half][:, :], ACT.Gelu).then_inc(s_ge, 1)

            def split_x(c):
                act.wait_ge(s_t1a, c + 1)
                act.wait_ge(s_t1d, c + 1)
                if c >= 2:
                    act.wait_ge(s_za, 2 * (c - 1))
                act.activation(xt_high[:, c % 2, :, :], T[:, :, c * P:(c + 1) * P], ACT.Copy).then_inc(s_xth, 1)

            sq1(0)
            sq1(1)
            for c in range(NC):
                evac_x(c)
                split_x(c)
                if c == 0:
                    for k in range(KD):
                        act.wait_ge(s_wi[k], 16)
                        act.activation(w_in_high[:, k, :], w_in_sb[:, k, 0:2 * DA], ACT.Copy).then_inc(s_wih, 1)
                if c + 2 < NC:
                    sq1(c + 2)
                if c >= 1:
                    gelu(c - 1)
            gelu(NC - 1)

            def evac_z(g):
                act.wait_ge(s_zb, g + 1)
                act.activation(zT[:, g % 4, (g // 4) * 512:(g // 4 + 1) * 512], ps[2 + g % 4][:, :],
                               ACT.Copy).then_inc(s_ze, 1)

            for g in range(4):
                evac_z(g)
            act.wait_ge(s_sq, NC)
            act.wait_ge(s_ya, NH)
            for c in range(NC):
                if c:
                    act.wait_ge(s_sqa, c)
                square(u_sb[:, c, :], DA ** -0.5, 1, c, s_sqa)
            for g in range(4, 8):
                evac_z(g)
            for c in range(NC):
                act.wait_ge(s_ta, c + 1)
                act.activation(T[:, 0:4, c * P:(c + 1) * P], ps[(0, 1, 6, 7)[c % 4]][:, :].rearrange(
                    "p (k t) -> p k t", k=4), ACT.Copy).then_inc(s_tae, 1)
            for s0 in range(NC + 2):
                if s0 < NC:
                    act.wait_ge(s_v, s0 + 1)
                    if s0 >= 2:
                        act.wait_ge(s_y, s0 - 1)
                    act.activation(V[:, s0 % 2, 0:2, :, :], ps[2 + 2 * (s0 % 2)][:, :].rearrange(
                        "p (r i q) -> p r i q", r=2, i=2), ACT.Copy).then_inc(s_va, 1)
                if 1 <= s0 <= NC:
                    act.wait_ge(s_y, s0)
                    if s0 == 1:
                        act.wait_ge(s_sqa, NC)
                    else:
                        act.wait_ge(s_sqb, s0 - 1)
                    square(ps[(s0 - 1) % 2][:, :], DA ** -0.5, 2, s0 - 1, s_sqb)
                if s0 >= 2:
                    act.wait_ge(s_tb, s0 - 1)
                    act.activation(T[:, 4:8, s0 - 2:S:NC], ps[6 + s0 % 2][:, :].rearrange(
                        "p (k t) -> p k t", k=4), ACT.Copy).then_inc(s_tbe, 1)
                if 1 <= s0 <= KD:
                    k = s0 - 1
                    if k == 0:
                        act.wait_ge(s_wo_in, 16)
                        act.wait_ge(s_ta, NC)
                        act.wait_ge(s_bf, BUTTERFLY)
                    act.activation(w_out_high[k // 4][:, k % 4, :], w_out_sb[:, k, :], ACT.Copy).then_inc(s_woh, 1)

            def split_cat(c):
                if c < 2:
                    act.wait_ge(s_tae, NC)
                    act.wait_ge(s_tbe, NC)
                else:
                    act.wait_ge(s_wo, c - 1)
                act.activation(cat_high[:, c % 2, :, :], T[:, :, c * P:(c + 1) * P], ACT.Copy).then_inc(s_ch, 1)

            split_cat(0)
            split_cat(1)
            for c in range(NC + 2):
                if c < NC:
                    act.wait_ge(s_hx, 2 * c + 2)
                    if c == 0:
                        act.wait_ge(s_sqb, NC)
                    else:
                        act.wait_ge(s_sq2, c)
                    square(xh[:, c, :], D ** -0.5, 3, c, s_sq2)
                    if c + 2 < NC:
                        split_cat(c + 2)
                if 1 <= c <= NC:
                    act.wait_ge(s_t3, c)
                    act.activation(T[:, 0:4, (c - 1) * P:c * P], ps[4][:, :].rearrange(
                        "p (k t) -> p k t", k=4), ACT.Copy).then_inc(s_t3a, 1)
                if c >= 2:
                    act.wait_ge(s_rt, c - 1)
                    act.activation(scores[:, c - 2, :], ps[6 + c % 2][:, 0:NE], ACT.Sigmoid).then_inc(s_sc, 1)

            for q in range(4):
                act.wait_ge(s_q, q + 1)
                if q >= 2:
                    act.wait_ge(s_hm, q - 1)
                act.activation(s_tmp[:, q % 2, :], ps[2 * (q % 2)][:, :], ACT.Silu).then_inc(s_ssi, 1)

            def split_gu(at):
                for m in range(GU_PARTS):
                    act.activation(gu_part(w_gu[:, :, 0, :, :, :], at, m), gu_part(raw_gu, at, m), ACT.Copy).then_inc(s_hg, 1)

            def split_dn(at):
                for k in range(KF):
                    act.activation(w_dn[:, bass.ds(at, 1), 0, k, :], raw_dn[:, bass.ds(at, 1), k, :],
                                   ACT.Copy).then_inc(s_hd, 1)

            def silu(i):
                act.wait_ge(s_gu, i + 1)
                after(act, s_h, i)
                act.activation(hs[:, :], ps[3][:, 0:F], ACT.Silu).then_inc(s_si, 1)

            def evac_xT(i):
                act.wait_ge(s_tr, i + 1)
                for half in range(2):
                    act.activation(xTh[:, half * 4:half * 4 + 4, :], ps[1 + half][:, :].rearrange(
                        "p (k t) -> p k t", k=4), ACT.Copy).then_inc(s_xa, 1)

            def evac_out(i, u, before=None):
                act.wait_ge(s_dn, i + 1)
                after(act, s_add, 16 * (i - 2 if before is None else before))
                act.activation(ob[:, u, 0:512], ps[6][:, :], ACT.Copy)
                act.activation(ob[:, u, 512:1024], ps[7][:, :], ACT.Copy).then_inc(s_oa, 1)

            def evac_h(i):
                act.wait_ge(s_ht, i + 1)
                act.activation(hTh[:, :, :], ps[5][:, 0:KF * P].rearrange("p (k t) -> p k t", k=KF),
                               ACT.Copy).then_inc(s_he, 1)

            def expert(i):
                both = look(act, 3, i, 2 * NE - 1)
                e = act.snap(both // 2, min_val=0, max_val=NE - 1)
                return act.snap(both % 2, min_val=0, max_val=1), e, place_of(act, e)

            def item(i, u, now, coming):
                with act.If(coming[0] > 0):
                    act.wait_ge(s_rg, coming[1] + 1)
                    split_gu(coming[2])
                now = now or expert(i)
                later = expert(i + 2) if u + 1 < TURN else None
                silu(i)
                evac_xT(i + 1)
                with act.If(now[0] > 0):
                    act.wait_ge(s_rd, now[1] + 1)
                    split_dn(now[2])
                evac_h(i)
                if not (isinstance(i, int) and i == 0):
                    evac_out(i - 1, (u - 1) % TURN)
                return later

            def turn_of_items(turn):
                now, coming = None, expert(turn * TURN + 1)
                for u in range(TURN):
                    now, coming = coming, item(turn * TURN + u, u, now, coming)

            act.wait_ge(s_rg, 1)
            split_gu(1)
            act.wait_ge(s_tab, 1)
            evac_xT(0)
            act.wait_ge(s_yst, 16 * (NC + 1))
            turn_of_items(0)
            last, before = item_count(act, 1), item_count(act, 3)
            with act.Fori(1, turns(act)) as t:
                turn_of_items(t)
            evac_out(last, TURN - 1, before)

            for c in range(NC):
                act.wait_ge(s_yl[c], 16)
                act.wait_ge(s_sq2, NC) if c == 0 else act.wait_ge(s_sqf, c)
                square(xh[:, c, :], D ** -0.5, 4, c, s_sqf)

        @block.vector
        def _(dv):
            def norm_x(c):
                dv.wait_ge(s_r1, c + 1)
                if c >= 2:
                    dv.wait_ge(s_t1, c - 1)
                if c == 0:
                    dv.wait_ge(s_g1, 16)
                dv.scalar_tensor_tensor(out=rows[:, c % 2, :], in0=x_ring[:, c % 2, :], scalar=rs[:, 0, c:c + 1],
                                        in1=g1_row[:, :], op0=ALU.mult, op1=ALU.mult).then_inc(s_xs, 1)

            def evac_x(c):
                dv.wait_ge(s_t1, c + 1)
                dv.tensor_copy(T[:, 4:8, c * P:(c + 1) * P], ps[1 if c % 2 == 0 else 7][:, :].rearrange(
                    "p (k t) -> p k t", k=4)).then_inc(s_t1d, 1)

            def norm_v(c):
                dv.wait_ge(s_ge, 2 * c + 2)
                dv.bn_stats(bst[:, c, :], v_sb[:, c, :]).then_inc(s_ln, 1)
                dv.wait_ge(s_ln, 3 * c + 1)
                dv.bn_aggr(bag[:, c, :], bst[:, c, :]).then_inc(s_ln, 1)
                dv.wait_ge(s_lr, c + 1)
                dv.tensor_scalar(v_sb[:, c, :], v_sb[:, c, :], bag[:, c, 0:1], vr[:, c:c + 1], ALU.subtract,
                                 ALU.mult).then_inc(s_ln, 1)

            def rest_x(c):
                dv.wait_ge(s_xth, c + 1)
                if c >= 2:
                    dv.wait_ge(s_za, 2 * (c - 1))
                dv.tensor_tensor(xt_rest[:, c % 2, :, :], T[:, :, c * P:(c + 1) * P],
                                 xt_high[:, c % 2, :, :].bitcast(F32), ALU.subtract).then_inc(s_xtl, 1)

            norm_x(0)
            norm_x(1)
            for c in range(NC):
                evac_x(c)
                rest_x(c)
                if c == 0:
                    for k in range(KD):
                        dv.wait_ge(s_wih, k + 1)
                        dv.tensor_tensor(w_in_rest[:, k, 0:2 * DA], w_in_sb[:, k, 0:2 * DA],
                                         w_in_high[:, k, :].bitcast(F32), ALU.subtract).then_inc(s_wil, 1)
                if c + 2 < NC:
                    norm_x(c + 2)
                if c >= 1:
                    norm_v(c - 1)
            norm_v(NC - 1)

            dv.wait_ge(s_small, 16 * 9)
            for h in range(NH):
                dv.wait_ge(s_sg, h + 1)
                heads = u_sb[:, :, h * HD:(h + 1) * HD]
                dv.scalar_tensor_tensor(out=heads, in0=ps[(0, 1, 6, 7)[h % 4]][:, :].rearrange(
                    "p (c d) -> p c d", c=NC), scalar=bsp[:, h:h + 1], in1=heads, op0=ALU.add,
                    op1=ALU.mult).then_inc(s_ya, 1)
            for c in range(NC):
                dv.wait_ge(s_ra, c + 1)
                dv.scalar_tensor_tensor(out=u_sb[:, c, :], in0=u_sb[:, c, :], scalar=rs[:, 1, c:c + 1],
                                        in1=ga_row[:, :], op0=ALU.mult, op1=ALU.mult).then_inc(s_yn, 1)

            steps = [0]

            def fly(*instructions):
                for ins in instructions:
                    steps[0] += 1
                    ins.then_inc(s_bf, 1)
                dv.wait_ge(s_bf, steps[0])

            a, b = ab[:, 0, :, :], ab[:, 1, :, :]
            dif, tot = dt[:, 0, :, :], dt[:, 1, :, :]
            pair4 = lambda t: t.rearrange("p r (a q) -> p a r q", q=P)
            for et in range(4):
                dv.wait_ge(s_ze, 5 + et)
                near, far = zT[:, et, 0:512], zT[:, et, 512:1024]
                fly(dv.tensor_tensor(a[:, et, :], near, far, ALU.add),
                    dv.tensor_tensor(b[:, et, :], near, far, ALU.subtract))
                fly(dv.tensor_tensor(dif[:, et, :], b[:, et, 128:256], b[:, et, 384:512], ALU.subtract),
                    dv.tensor_tensor(tot[:, et, :], b[:, et, 128:256], b[:, et, 384:512], ALU.add))
            fly(dv.tensor_tensor(U[:, 4:6, :, :], pair4(a[:, :, 0:256]), pair4(a[:, :, 256:512]), ALU.subtract),
                dv.tensor_tensor(U[:, 6:8, :, :], pair4(a[:, :, 0:256]), pair4(a[:, :, 256:512]), ALU.add))
            fly(dv.tensor_tensor(U[:, 0, :, :], U[:, 6, :, :], U[:, 7, :, :], ALU.add),
                dv.tensor_tensor(U[:, 1, :, :], U[:, 6, :, :], U[:, 7, :, :], ALU.subtract))
            fly(*(dv.scalar_tensor_tensor(out=U[:, j + im, :, :], in0=part, scalar=r, in1=b[:, :, 256 * im:256 * im + 128],
                                          op0=ALU.mult, op1=ALU.add)
                  for j, r in ((2, R8), (6, -R8)) for im, part in ((0, dif), (1, tot))))
            assert steps[0] == BUTTERFLY

            for s0 in range(NC + 1):
                if s0 < NC:
                    dv.wait_ge(s_v, s0 + 1)
                    if s0 >= 2:
                        dv.wait_ge(s_y, s0 - 1)
                    dv.tensor_copy(V[:, s0 % 2, 2:4, :, :], ps[3 + 2 * (s0 % 2)][:, :].rearrange(
                        "p (r i q) -> p r i q", r=2, i=2)).then_inc(s_vd, 1)
                if s0 >= 1:
                    dv.wait_ge(s_rb, s0)
                    dv.scalar_tensor_tensor(out=yb[:, s0 - 1, :], in0=ps[(s0 - 1) % 2][:, :],
                                            scalar=rs[:, 2, s0 - 1:s0], in1=gb_row[:, :], op0=ALU.mult,
                                            op1=ALU.mult).then_inc(s_yb, 1)
                    k = s0 - 1
                    dv.wait_ge(s_woh, k + 1)
                    dv.tensor_tensor(w_out_rest[:, k, :], w_out_sb[:, k, :], w_out_high[k // 4][:, k % 4, :].bitcast(F32),
                                     ALU.subtract).then_inc(s_wol, 1)

            def rest_cat(c):
                dv.wait_ge(s_ch, c + 1)
                if c >= 2:
                    dv.wait_ge(s_wo, c - 1)
                dv.tensor_tensor(cat_rest[:, c % 2, :, :], T[:, :, c * P:(c + 1) * P],
                                 cat_high[:, c % 2, :, :].bitcast(F32), ALU.subtract).then_inc(s_cl, 1)

            rest_cat(0)
            rest_cat(1)
            for c in range(NC + 1):
                if c < NC:
                    dv.wait_ge(s_wo, c + 1)
                    dv.wait_ge(s_x[c], 32)
                    for half in range(2):
                        piece = xh[:, c, half * 512:(half + 1) * 512]
                        dv.tensor_tensor(piece, ps[2 * (c % 2) + half][:, :], piece, ALU.add).then_inc(s_hx, 1)
                    if c + 2 < NC:
                        rest_cat(c + 2)
                if c >= 1:
                    dv.wait_ge(s_t3, c)
                    dv.tensor_copy(T[:, 4:8, (c - 1) * P:c * P], ps[5][:, :].rearrange(
                        "p (k t) -> p k t", k=4)).then_inc(s_t3d, 1)
                if c < NC:
                    dv.wait_ge(s_r2, c + 1)
                    if c >= 2:
                        dv.wait_ge(s_t3, c - 1)
                        dv.wait_ge(s_hst[c % 2], 16 * (c // 2))
                    dv.scalar_tensor_tensor(out=rows[:, c % 2, :], in0=xh[:, c, :], scalar=rs[:, 3, c:c + 1],
                                            in1=g2_row[:, :], op0=ALU.mult, op1=ALU.mult).then_inc(s_hn, 1)

            count = [0]

            def step(ins):
                count[0] += 1
                ins.then_inc(s_rv, 1)
                dv.wait_ge(s_rv, count[0])

            def many(instructions):
                for ins in instructions:
                    count[0] += 1
                    ins.then_inc(s_rv, 1)
                dv.wait_ge(s_rv, count[0])

            def shared_h(q):
                dv.wait_ge(s_ssi, q + 1)
                dv.tensor_tensor(hsT[:, q % 2, (q // 2) * 512:(q // 2 + 1) * 512], s_tmp[:, q % 2, :],
                                 ps[2 * (q % 2) + 1][:, :], ALU.mult).then_inc(s_hm, 1)

            def rest_gu(at, e):
                for m in range(GU_PARTS):
                    dv.wait_ge(s_hg, e * GU_PARTS + m + 1)
                    dv.tensor_tensor(gu_part(w_gu[:, :, 1, :, :, :], at, m), gu_part(raw_gu, at, m),
                                     gu_part(w_gu[:, :, 0, :, :, :], at, m).bitcast(F32), ALU.subtract).then_inc(s_lg, 1)

            dv.wait_ge(s_cst, 1)
            dv.wait_ge(s_sc, NC)
            wide = [P, NC, NE]
            step(dv.tensor_tensor(rt_a[:, :, :], scores[:, :, :], rb_row[:, None, :].to_broadcast(wide), ALU.add))
            many(dv.max(m8[:, c, g, :], rt_a[:, c, g * GE:(g + 1) * GE]) for c in range(NC) for g in range(NG))
            step(dv.tensor_tensor(gs[:, :, :], m8[:, :, :, 0], m8[:, :, :, 1], ALU.add))
            many(dv.max(gtop[:, c, :], gs[:, c, :]) for c in range(NC))
            many(dv.max_index(gidx[:, c, :], gtop[:, c, :], gs[:, c, :]) for c in range(NC))
            step(dv.tensor_copy(gidxf[:, :, :], gidx[:, :, 0:TOPG]))
            step(dv.tensor_tensor(geq[:, :, :, :], gidxf[:, :, None, :].to_broadcast([P, NC, NG, TOPG]),
                                  gi[:, None, :, None].to_broadcast([P, NC, NG, TOPG]), ALU.is_equal))
            step(dv.tensor_reduce(gm[:, :, :], geq[:, :, :, :], AX.X, ALU.max))
            step(dv.tensor_scalar(gs[:, :, :], gm[:, :, :], 1.0, BIG, ALU.subtract, ALU.mult))
            by_group = lambda t: t[:, :, :].rearrange("p c (g e) -> p c g e", g=NG)
            step(dv.tensor_tensor(by_group(rt_b), by_group(rt_a), gs[:, :, :, None].to_broadcast([P, NC, NG, GE]),
                                  ALU.add))
            many(dv.max(etop[:, c, :], rt_b[:, c, :]) for c in range(NC))
            many(dv.match_replace(rt_a[:, c, :], etop[:, c, :], rt_b[:, c, :], -3.3e38) for c in range(NC))
            dv.wait_ge(s_hst[0], 16 * 4)
            dv.wait_ge(s_hst[1], 16 * 4)
            dv.wait_ge(s_t3, NC)
            shared_h(0)
            step(dv.tensor_tensor(mask[:, :, :], rt_a[:, :, :], rt_b[:, :, :], ALU.not_equal))
            dv.sem_inc(s_mask, 1)
            step(dv.tensor_tensor(rt_a[:, :, :], scores[:, :, :], mask[:, :, :], ALU.mult))
            step(dv.tensor_reduce(gsum[:, :], rt_a[:, :, :], AX.X, ALU.add))
            step(dv.reciprocal(grec[:, :], gsum[:, :]))
            step(dv.tensor_scalar(grec[:, :], grec[:, :], RSCALE, None, ALU.mult))
            step(dv.tensor_tensor(rt_a[:, :, :], rt_a[:, :, :], grec[:, :, None].to_broadcast(wide), ALU.mult))
            shared_h(1)
            dv.wait_ge(s_pm, 1)
            step(dv.scalar_tensor_tensor(out=rt_b[:, :, :], in0=ps[4][:, :].rearrange("p (c e) -> p c e", c=NC),
                                         scalar=1.0, in1=mask[:, :, :], op0=ALU.add, op1=ALU.mult))
            step(dv.tensor_scalar(pos[:, :, :], rt_b[:, :, :], -1.0, None, ALU.add))
            for j in range(1, MAXCH):
                step(dv.scalar_tensor_tensor(out=nch[:, j:j + 1], in0=ps[5][0:NE, 0:1], scalar=float(P * j),
                                             in1=nch[:, j - 1:j], op0=ALU.is_gt, op1=ALU.add))
            step(dv.tensor_copy(nchb[:, :], nch[:, MAXCH - 1:MAXCH].to_broadcast([NE, P])))
            dv.sem_inc(s_chunks, 1)

            dv.wait_ge(s_info, 3)
            step(dv.tensor_copy(info[:, :, :, 2], rt_a[:, :, :]))
            step(dv.tensor_tensor(rt_b[:, :, :], rt_a[:, :, :], info[:, :, :, 2], ALU.subtract))
            step(dv.tensor_copy(info[:, :, :, 3], rt_b[:, :, :]))
            step(dv.tensor_tensor(rt_a[:, :, :], rt_b[:, :, :], info[:, :, :, 3], ALU.subtract))
            step(dv.tensor_copy(info[:, :, :, 4], rt_a[:, :, :]))
            shared_h(2)
            dv.wait_ge(s_pm, 2)
            step(dv.tensor_copy(le[:, 2, :], ps[6][:, 0:NE]))
            step(dv.tensor_scalar(le[:, 0, :], le[:, 2, :], pidx[:, 0:1], None, ALU.is_le))
            step(dv.tensor_tensor(le[:, 1, :], le[:, 0, :], le[:, 2, :], ALU.mult))
            step(dv.tensor_reduce(cols[:, 8:9], le[:, 0, :], AX.X, ALU.add))
            step(dv.tensor_reduce(cols[:, 4:5], le[:, 1, :], AX.X, ALU.max))
            step(dv.tensor_scalar(cols[:, 0:1], cols[:, 8:9], float(NE - 1), None, ALU.min))
            step(dv.tensor_scalar(halves[:, :], cols[:, 0:1], 0.5, 0.5, ALU.add, ALU.mult))
            step(dv.tensor_scalar(cols[:, 9:10], halves[:, :], -2.0, 1.0, ALU.mult, ALU.add))
            step(dv.tensor_tensor(cols[:, 2:3], cols[:, 9:10], cols[:, 0:1], ALU.add))
            step(dv.tensor_scalar(cols[:, 5:6], cols[:, 4:5], pidx[:, 0:1], float(P), ALU.subtract, ALU.mult))
            step(dv.tensor_scalar(cols[:, 6:7], cols[:, 8:9], float(NE), -float(S), ALU.is_ge, ALU.mult))
            step(dv.tensor_tensor(cols[:, 7:8], cols[:, 5:6], cols[:, 6:7], ALU.add))
            step(dv.tensor_scalar(cols[:, 1:2], cols[:, 7:8], float(S), 0.0, ALU.add, ALU.max))
            step(dv.tensor_scalar(cols[:, 10:11], cols[:, 4:5], pidx[:, 0:1], None, ALU.is_equal))
            step(dv.tensor_scalar(cols[:, 11:12], cols[:, 8:9], float(NE), None, ALU.is_lt))
            step(dv.tensor_tensor(cols[:, 7:8], cols[:, 10:11], cols[:, 11:12], ALU.mult))
            step(dv.tensor_tensor(cols[:, 10:11], cols[:, 0:1], cols[:, 0:1], ALU.add))
            step(dv.tensor_tensor(cols[:, 3:4], cols[:, 10:11], cols[:, 7:8], ALU.add))
            dv.sem_inc(s_cols, 1)
            step(dv.tensor_copy(ends[0:1, 0:NE], ps[6][0:1, 0:NE]))
            step(dv.tensor_scalar(ends[0:1, NE + 4:NE + 5], ps[6][0:1, NE - 1:NE], 1.0, 1.0 / TURN, ALU.add, ALU.mult))
            for less in range(TURN + 1):
                step(dv.tensor_scalar(ends[0:1, NE + less:NE + less + 1], ends[0:1, NE + 4:NE + 5], float(TURN),
                                      float(less), ALU.mult, ALU.subtract))
            shared_h(3)
            dv.wait_ge(s_pm, 3)
            dv.tensor_copy(tab[0:4, 0:P], ps[7][0:4, 0:P]).then_inc(s_tab, 1)

            def one_hot(i, e, back):
                shape = [P, NC, P]
                after(dv, s_ix, i)
                dv.tensor_tensor(onehot[:, :, :], pos[:, :, bass.ds(e, 1)].to_broadcast(shape),
                                 slots[:, None, bass.ds(S - back, P)].to_broadcast(shape),
                                 ALU.is_equal).then_inc(s_oh, 1)

            def indices(i, u):
                dv.wait_ge(s_ix, i + 1)
                after(dv, s_ia, i)
                after(dv, s_gt, i)
                dv.tensor_copy(sumf[:, 0:5], ps[0][:, 0:5]).then_inc(s_cp, 1)
                dv.wait_ge(s_cp, i + 1)
                dv.scalar_tensor_tensor(out=idxf[:, :], in0=sumf[:, 0:1], scalar=EMPTY, in1=sumf[:, 1:2],
                                        op0=ALU.add, op1=ALU.add).then_inc(s_it, 1)
                dv.scalar_tensor_tensor(out=gate_all[:, bass.ds(i, 1)], in0=sumf[:, 2:3], scalar=sumf[:, 3:4],
                                        in1=sumf[:, 4:5], op0=ALU.add, op1=ALU.add).then_inc(s_gt, 1)
                dv.wait_ge(s_it, i + 1)
                dv.tensor_scalar(idxg[:, u:u + 1], idxf[:, :], dump[:, 0:1], None, ALU.min).then_inc(s_id, 1)
                dv.tensor_scalar(idx_all[:, bass.ds(i, 1)], idxf[:, :], dump[:, 0:1], None, ALU.min).then_inc(s_ia, 1)

            def gated_h(i):
                dv.wait_ge(s_si, i + 1)
                dv.wait_ge(s_gt, i + 1)
                after(dv, s_ht, i)
                dv.scalar_tensor_tensor(out=hh[:, :], in0=hs[:, :], scalar=gate_all[:, bass.ds(i, 1)],
                                        in1=ps[3][:, F:2 * F], op0=ALU.mult, op1=ALU.mult).then_inc(s_h, 1)

            def rest_xT(i):
                for half in range(2):
                    dv.wait_ge(s_xa, 2 * i + half + 1)
                    part = slice(half * 4, half * 4 + 4)
                    dv.tensor_tensor(xTl[:, part, :], ps[1 + half][:, :].rearrange("p (k t) -> p k t", k=4),
                                     xTh[:, part, :].bitcast(F32), ALU.subtract).then_inc(s_xd, 1)

            def rest_h(i):
                dv.wait_ge(s_he, i + 1)
                dv.tensor_tensor(hTl[:, :, :], ps[5][:, 0:KF * P].rearrange("p (k t) -> p k t", k=KF),
                                 hTh[:, :, :].bitcast(F32), ALU.subtract).then_inc(s_hl, 1)

            def scatter_idx(i, u, before=None):
                dv.wait_ge(s_ia, i + 1)
                after(dv, s_add, 16 * (i - 2 if before is None else before))
                dv.tensor_scalar(idxs[:, u:u + 1], idx_all[:, bass.ds(i, 1)], 0.0, None, ALU.add).then_inc(s_is, 1)

            def expert(i):
                both = look(dv, 3, i, 2 * NE - 1)
                e = dv.snap(both // 2, min_val=0, max_val=NE - 1)
                return dv.snap(both % 2, min_val=0, max_val=1), e, place_of(dv, e)

            def item(i, u, coming):
                first = isinstance(i, int) and i == 0
                with dv.If(coming[0] > 0):
                    rest_gu(coming[2], coming[1])
                later = expert(i + 2) if u + 1 < TURN else None
                ahead = look(dv, 0, i + TURN + 1, NE - 1), look(dv, 1, i + TURN + 1, S)
                gated_h(i)
                rest_xT(i + 1)
                rest_h(i)
                indices(i + TURN, u)
                if not first:
                    scatter_idx(i - 1, (u - 1) % TURN)
                one_hot(i + TURN + 1, *ahead)
                return later

            def turn_of_items(turn):
                coming = expert(turn * TURN + 1)
                for u in range(TURN):
                    coming = item(turn * TURN + u, u, coming)

            def y0(c):
                dv.wait_ge(s_sdn, c + 1)
                for half in range(2):
                    piece = xh[:, c, half * 512:(half + 1) * 512]
                    ins = dv.tensor_tensor(piece, ps[4 + 2 * (c % 2) + half][:, :], piece, ALU.add)
                ins.then_inc(s_y0, 1)

            dv.wait_ge(s_tab, 1)
            one_hot(0, look(dv, 0, 0, NE - 1), look(dv, 1, 0, S))
            rest_gu(1, 0)
            for i in range(TURN):
                y0(2 * i)
                y0(2 * i + 1)
                indices(i, i)
                one_hot(i + 1, look(dv, 0, i + 1, NE - 1), look(dv, 1, i + 1, S))
            y0(2 * TURN)
            y0(2 * TURN + 1)
            rest_xT(0)
            turn_of_items(0)
            last, before = item_count(dv, 1), item_count(dv, 3)
            with dv.Fori(1, turns(dv)) as t:
                turn_of_items(t)
            scatter_idx(last, TURN - 1, before)

            dv.wait_ge(s_gf, 16)
            for c in range(NC):
                dv.wait_ge(s_rf, c + 1)
                dv.scalar_tensor_tensor(out=xh[:, c, :], in0=xh[:, c, :], scalar=rs[:, 4, c:c + 1],
                                        in1=gf_row[:, :], op0=ALU.mult, op1=ALU.mult).then_inc(s_of, 1)

        @block.gpsimd
        def _(gp):
            made = [0]

            def make(ins):
                made[0] += 1
                ins.then_inc(s_mk, 1)

            make(gp.memset(ident[:, :], 0.0))
            make(gp.memset(tri[:, :], 1.0))
            make(gp.memset(triI[:, :], 1.0))
            make(gp.memset(ones[:, :], 1.0))
            make(gp.memset(nch[:, 0:1], 1.0))
            make(gp.memset(tab[:, :], 0))
            make(gp.memset(mhalf[:, :], -0.5))
            make(gp.iota(gi[:, :], pattern=[[1, NG]], base=0, channel_multiplier=0, allow_small_or_imprecise_dtypes=True))
            make(gp.iota(pidx[:, :], pattern=[[1, 1]], base=0, channel_multiplier=1, allow_small_or_imprecise_dtypes=True))
            make(gp.iota(dump[:, :], pattern=[[1, 1]], base=S, channel_multiplier=1, allow_small_or_imprecise_dtypes=True))
            gp.wait_ge(s_mk, made[0])
            make(gp.affine_select(out=ident[:, :], in_=ident[:, :], compare_op=ALU.not_equal, fill=1.0, base=0,
                                  pattern=[[-1, P]], channel_multiplier=1))
            make(gp.affine_select(out=tri[:, :], in_=tri[:, :], compare_op=ALU.is_gt, fill=0.0, base=0,
                                  pattern=[[1, P]], channel_multiplier=-1))
            make(gp.affine_select(out=triI[:, :], in_=triI[:, :], compare_op=ALU.is_ge, fill=0.0, base=0,
                                  pattern=[[1, NE]], channel_multiplier=-1))
            gp.wait_ge(s_mk, made[0])
            gp.sem_inc(s_cst, 1)

            roots = [0]

            def inverse_root(dst, src, done):
                roots[0] += 1
                gp.tensor_scalar(dst, src, EPS, None, ALU.add).then_inc(s_eps, 1)
                gp.wait_ge(s_eps, roots[0])
                gp.tensor_tensor(dst, dst, mhalf[:, :], ALU.pow).then_inc(done, 1)

            def rstd(norm, c, squares, done):
                gp.wait_ge(squares, c + 1)
                inverse_root(rs[:, norm, c:c + 1], ms[:, norm, c:c + 1], done)

            rstd(0, 0, s_sq, s_r1)
            rstd(0, 1, s_sq, s_r1)
            gp.wait_ge(s_small, 16 * 9)
            for step_ in range(NC + 1):
                if step_ + 2 < NC:
                    rstd(0, step_ + 2, s_sq, s_r1)
                if step_ == 0:
                    continue
                c = step_ - 1
                gp.wait_ge(s_ln, 3 * c + 2)
                inverse_root(vr[:, c:c + 1], bag[:, c, 1:2], s_lr)
                gp.wait_ge(s_ln, 3 * (c + 1))
                gp.tensor_tensor(v_sb[:, c, :], v_sb[:, c, :], lng_row[:, :], ALU.mult).then_inc(s_vp, 1)
                gp.wait_ge(s_vp, 2 * c + 1)
                gp.tensor_tensor(v_sb[:, c, :], v_sb[:, c, :], lnb_row[:, :], ALU.add).then_inc(s_vp, 1)
            for c in range(NC):
                rstd(1, c, s_sqa, s_ra)
            for c in range(NC):
                rstd(2, c, s_sqb, s_rb)

            gp.wait_ge(s_yb, NC)
            gp.iota(info[:, :, :, 0], pattern=[[P, NC], [0, NE]], base=-int(EMPTY), channel_multiplier=0,
                    allow_small_or_imprecise_dtypes=True).then_inc(s_info, 1)
            gp.iota(info[:, :, :, 1], pattern=[[0, NC], [0, NE]], base=0, channel_multiplier=1,
                    allow_small_or_imprecise_dtypes=True).then_inc(s_info, 1)
            gp.iota(slots[:, :], pattern=[[1, S + P]], base=0, channel_multiplier=0,
                    allow_small_or_imprecise_dtypes=True).then_inc(s_info, 1)

            for c in range(NC):
                rstd(3, c, s_sq2, s_r2)

            top_row = gp.to_reg(S - 1)
            top_dump = gp.to_reg(S + P - 1)

            def gather(i, u):
                gp.wait_ge(s_id, i + 1)
                after(gp, s_tr, i - 2)
                gp.sem_inc(s_turn, 1)
                gp.indirect_dma_start(out=Xg[:, u, :], out_offset=None, in_=hn_d[:, :],
                                      in_offset=bass.IndirectOffsetOnAxis(ap=idxg[:, u:u + 1], axis=0),
                                      bounds_check=top_row, oob_is_err=False).then_inc(s_ga[u], 16)

            def add_rows(i, u, before=None):
                gp.wait_ge(s_oa, i + 1)
                gp.wait_ge(s_is, i + 1)
                after(gp, s_add, 16 * i)
                gp.sem_inc(s_turn, 1)
                gp.indirect_dma_start(out=y_d[:, :], out_offset=bass.IndirectOffsetOnAxis(ap=idxs[:, u:u + 1], axis=0),
                                      in_=ob[:, u, :], in_offset=None, compute_op=ALU.add,
                                      bounds_check=top_dump).then_inc(s_add, 16)

            def rest_dn(at, e):
                gp.wait_ge(s_hd, (e + 1) * KF)
                for k in range(KF):
                    gp.tensor_tensor(w_dn[:, bass.ds(at, 1), 1, k, :], raw_dn[:, bass.ds(at, 1), k, :],
                                     w_dn[:, bass.ds(at, 1), 0, k, :].bitcast(F32), ALU.subtract).then_inc(s_ld, 1)

            def pick(i):
                e = look(gp, 0, i, NE - 1)
                after(gp, s_ix, i)
                gp.sem_inc(s_turn, 1)
                gp.tensor_copy(info_i[:, :, :], info[:, :, bass.ds(e, 1), :].rearrange("p c e j -> p c (e j)")).then_inc(s_pk, 1)

            def expert(i):
                both = look(gp, 3, i, 2 * NE - 1)
                e = gp.snap(both // 2, min_val=0, max_val=NE - 1)
                return gp.snap(both % 2, min_val=0, max_val=1), e, place_of(gp, e)

            def item(i, u, now):
                with gp.If(now[0] > 0):
                    rest_dn(now[2], now[1])
                pick(i + TURN + 1)
                later = expert(i + 1) if u + 1 < TURN else None
                if not (isinstance(i, int) and i == 0):
                    add_rows(i - 1, (u - 1) % TURN)
                gather(i + TURN, u)
                return later

            def turn_of_items(turn):
                now = expert(turn * TURN)
                for u in range(TURN):
                    now = item(turn * TURN + u, u, now)

            gp.wait_ge(s_hst[0], 16 * 4)
            gp.wait_ge(s_hst[1], 16 * 4)
            gp.wait_ge(s_tab, 1)
            pick(0)
            for i in range(TURN):
                gather(i, i)
                pick(i + 1)
            gp.wait_ge(s_yst, 16 * (NC + 1))
            turn_of_items(0)
            last = item_count(gp, 1)
            with gp.Fori(1, turns(gp)) as t:
                turn_of_items(t)
            add_rows(last, TURN - 1)
            for c in range(NC):
                rstd(4, c, s_sqf, s_rf)


BUTTERFLY = 24


def after(eng, semaphore, value):
    if not isinstance(value, int) or value > 0:
        eng.wait_ge(semaphore, value)


_INS = ["x", "norm1_g", "w_in", "sgu_ln_g", "sgu_ln_b", "w_spatial", "b_spatial", "out_norm_a_g", "out_norm_b_g",
        "w_out", "norm2_g", "w_router", "router_bias", "w_gate", "w_up", "w_down", "ws_gate", "ws_up", "ws_down"]


def dft_tables():
    import numpy as np
    q = np.arange(P)[:, None, None]
    s = NC * np.arange(P)[None, None, :] + np.arange(NC)[None, :, None]
    th = 2 * np.pi * ((q * s) % S) / S
    pos = np.stack([np.cos(th), np.sin(th)], axis=1) / 256.0
    k = np.arange(64)
    th = 2 * np.pi * (np.outer(k, k) % 64) / 64
    C = np.kron(np.eye(2), np.cos(th))
    Sn = np.kron(np.eye(2), np.sin(th))
    ch = np.stack([np.stack([C, -Sn], 1), np.stack([Sn, C], 1), np.stack([-Sn, -C], 1)], 1)
    return pos.astype(np.float32), ch.astype(np.float32)


def kernel(**inputs):
    import numpy as np
    import concourse.bacc as bacc
    from concourse.bass_utils import run_bass_kernel_spmd as run

    nc = bacc.Bacc("TRN2", target_bir_lowering=False, num_devices=1)
    a = {k: np.asarray(inputs[k])[0] for k in _INS}
    a["final_norm_g"] = np.asarray(inputs["final_norm_g"])
    a["w_spatial"] = np.ascontiguousarray(a["w_spatial"].transpose(0, 2, 1))
    a["b_spatial"] = np.ascontiguousarray(a["b_spatial"].T)
    a["dft_pos"], a["dft_ch"] = dft_tables()
    order = _INS + ["dft_pos", "dft_ch"]
    order.insert(len(_INS), "final_norm_g")
    h = {k: nc.dram_tensor("in_" + k, a[k].shape, F32, kind="ExternalInput").ap() for k in order}
    out = nc.dram_tensor("result", (S, D), F32, kind="ExternalOutput").ap()
    hn_d = nc.dram_tensor("hn_rows_dram", (S, D), F32, kind="Internal").ap()
    y_d = nc.dram_tensor("y_rows_dram", (S + P, D), F32, kind="Internal").ap()
    build(nc, h["x"], h["norm1_g"], h["w_in"], h["sgu_ln_g"], h["sgu_ln_b"], h["w_spatial"], h["b_spatial"],
          h["out_norm_a_g"], h["out_norm_b_g"], h["w_out"], h["norm2_g"], h["w_router"], h["router_bias"],
          h["w_gate"], h["w_up"], h["w_down"], h["ws_gate"], h["ws_up"], h["ws_down"], h["dft_pos"], h["dft_ch"],
          h["final_norm_g"], out, hn_d, y_d)
    r = run(nc, [{"in_" + k: np.ascontiguousarray(a[k]) for k in order}], core_ids=[0])
    return r.results[0]["result"].reshape(1, S, D)
```
